# Optimizing a Trainium2 kernel written in Bass

```python
import math
import jax, jax.numpy as jnp
from jax import lax
import numpy as np

D_MODEL = 1024
BATCH = 1
SEQ = 256
DEPTH = 2

RNN_WIDTH = D_MODEL // 2
RNN_BLOCKS = 8
RNN_BLOCK = RNN_WIDTH // RNN_BLOCKS
CONV_WIDTH = 4
RGLRU_C = 8.0
ATTN_HEADS = 4
ATTN_HEAD_DIM = 64
ATTN_V_DIM = 2 * ATTN_HEAD_DIM
QK_WIDTH = ATTN_HEADS * 2 * ATTN_HEAD_DIM
ATTN_WIDTH = ATTN_HEADS * ATTN_V_DIM
ROPE_THETA = 10000.0
Q_BLOCK = 128
NEG_INF = -1e30
SSM_WIDTH = D_MODEL // 2
SSM_GROUP = 16
SSM_GROUPS = SSM_WIDTH // SSM_GROUP
SSM_STATE = 64
N_BRANCH = 3
IN_SPLITS = (RNN_WIDTH, 2 * RNN_WIDTH, 2 * RNN_WIDTH + QK_WIDTH, 2 * RNN_WIDTH + 2 * QK_WIDTH, 2 * RNN_WIDTH + 2 * QK_WIDTH + ATTN_WIDTH, 2 * RNN_WIDTH + 2 * QK_WIDTH + ATTN_WIDTH + SSM_WIDTH)
IN_COLS = IN_SPLITS[-1] + N_BRANCH * D_MODEL
N_GROUPS = 4
EXPERTS_PER_GROUP = 8
TOP_K_FINE = 2
EXPERT_FF = D_MODEL // 2

kernel_name = 'hybrid_rglru_diffattn_s5_hmoe'

def rmsnorm(x, g, eps=1e-6):
    xf = x.astype(jnp.float32)
    y = xf * lax.rsqrt(jnp.mean(xf * xf, axis=-1, keepdims=True) + eps)
    return (y * g.astype(jnp.float32)).astype(x.dtype)

def rope(x, positions):
    d = x.shape[-1]
    inv_freq = ROPE_THETA ** (-jnp.arange(0, d, 2, dtype=jnp.float32) / d)
    ang = positions.astype(jnp.float32)[..., None] * inv_freq
    ang = jnp.concatenate([ang, ang], axis=-1)[:, :, None, None, :]
    xf = x.astype(jnp.float32)
    rot = jnp.concatenate([-xf[..., d // 2:], xf[..., :d // 2]], axis=-1)
    return (xf * jnp.cos(ang) + rot * jnp.sin(ang)).astype(x.dtype)

def causal_depthwise_conv(x, w, b):
    K = w.shape[0]
    L = x.shape[1]
    xp = jnp.pad(x, ((0, 0), (K - 1, 0), (0, 0)))
    y = b
    for k in range(K):
        y = y + w[k] * xp[:, K - 1 - k:K - 1 - k + L]
    return y

def _real_combine(e1, e2):
    a1, b1 = e1
    a2, b2 = e2
    return (a1 * a2, a2 * b1 + b2)

def _complex_combine(e1, e2):
    a1r, a1i, b1r, b1i = e1
    a2r, a2i, b2r, b2i = e2
    return (a2r * a1r - a2i * a1i, a2r * a1i + a2i * a1r,
            a2r * b1r - a2i * b1i + b2r, a2r * b1i + a2i * b1r + b2i)

def rglru_branch(x_rnn, g_rnn, reset, conv_w, conv_b, rg_wa, rg_ba, rg_wx, rg_bx, rg_lambda):
    B_, L_, _ = x_rnn.shape
    xc = causal_depthwise_conv(x_rnn, conv_w, conv_b).astype(jnp.float32)
    xb = xc.reshape(B_, L_, RNN_BLOCKS, RNN_BLOCK)
    r = jax.nn.sigmoid(jnp.einsum('blhi,hij->blhj', xb, rg_wa.astype(jnp.float32)).reshape(B_, L_, RNN_WIDTH) + rg_ba)
    i = jax.nn.sigmoid(jnp.einsum('blhi,hij->blhj', xb, rg_wx.astype(jnp.float32)).reshape(B_, L_, RNN_WIDTH) + rg_bx)
    log_a = -RGLRU_C * r * jax.nn.softplus(-rg_lambda.astype(jnp.float32))
    a = jnp.exp(log_a)
    mult = jnp.sqrt(-jnp.expm1(2.0 * log_a))
    rs = reset[..., None]
    mult = jnp.where(rs, 1.0, mult)
    a = jnp.where(rs, 0.0, a)
    _, h = lax.associative_scan(_real_combine, (a, mult * i * xc), axis=1)
    return (h * jax.nn.gelu(g_rnn.astype(jnp.float32))).astype(x_rnn.dtype)

def diff_attention(q, k, v, lam, lambda_init, subln_g):
    B_, L_, H, _, d = q.shape
    nb = L_ // Q_BLOCK
    qf = q.astype(jnp.float32).transpose(0, 2, 3, 1, 4)
    kf = k.astype(jnp.float32).transpose(0, 2, 3, 1, 4)
    vf = v.astype(jnp.float32).transpose(0, 2, 1, 3)
    q_blocks = qf.reshape(B_, H, 2, nb, Q_BLOCK, d).transpose(3, 0, 1, 2, 4, 5)
    key_idx = jnp.arange(L_)
    scale = d ** -0.5

    def attend_block(args):
        qb, bi = args
        s = jnp.einsum('bhcqd,bhckd->bhcqk', qb, kf) * scale
        q_idx = bi * Q_BLOCK + jnp.arange(Q_BLOCK)
        causal = key_idx[None, :] <= q_idx[:, None]
        p = jax.nn.softmax(jnp.where(causal, s, NEG_INF), axis=-1)
        w = p[:, :, 0] - lam * p[:, :, 1]
        return jnp.einsum('bhqk,bhkv->bhqv', w, vf)

    o = lax.map(attend_block, (q_blocks, jnp.arange(nb)))
    o = o.transpose(1, 0, 3, 2, 4).reshape(B_, L_, H, 2 * d)
    o = rmsnorm(o, subln_g, eps=1e-5) * (1.0 - lambda_init)
    return o.reshape(B_, L_, H * 2 * d).astype(q.dtype)

def s5_branch(u, lam_re, lam_im, b_re, b_im, c_re, c_im, d_skip, log_dt, glu_w, glu_b):
    B_, L_, _ = u.shape
    uf = u.astype(jnp.float32).reshape(B_, L_, SSM_GROUPS, SSM_GROUP)
    lr = lam_re.astype(jnp.float32)
    li = lam_im.astype(jnp.float32)
    dt = jnp.exp(log_dt.astype(jnp.float32))[:, None]
    mag = jnp.exp(lr * dt)
    ar = mag * jnp.cos(li * dt)
    ai = mag * jnp.sin(li * dt)
    den = lr * lr + li * li
    cr = ((ar - 1.0) * lr + ai * li) / den
    ci = (ai * lr - (ar - 1.0) * li) / den
    br = b_re.astype(jnp.float32)
    bi = b_im.astype(jnp.float32)
    bbar_re = cr[..., None] * br - ci[..., None] * bi
    bbar_im = cr[..., None] * bi + ci[..., None] * br
    bu_re = jnp.einsum('blgi,gni->blgn', uf, bbar_re)
    bu_im = jnp.einsum('blgi,gni->blgn', uf, bbar_im)
    a_re = jnp.broadcast_to(ar, (1, L_) + ar.shape)
    a_im = jnp.broadcast_to(ai, (1, L_) + ai.shape)
    _, _, s_re, s_im = lax.associative_scan(_complex_combine, (a_re, a_im, bu_re, bu_im), axis=1)
    y = (jnp.einsum('blgn,gin->blgi', s_re, c_re.astype(jnp.float32))
         - jnp.einsum('blgn,gin->blgi', s_im, c_im.astype(jnp.float32))
         + d_skip.astype(jnp.float32) * uf)
    z = jax.nn.gelu(y.reshape(B_, L_, SSM_WIDTH))
    out = z * jax.nn.sigmoid(z @ glu_w.astype(jnp.float32) + glu_b.astype(jnp.float32))
    return out.astype(u.dtype)

def token_mixer(xn, positions, layer_idx, w_in, conv_w, conv_b, rg_wa, rg_ba, rg_wx, rg_bx, rg_lambda,
                lam_q1, lam_k1, lam_q2, lam_k2, subln_g,
                ssm_lambda_re, ssm_lambda_im, ssm_b_re, ssm_b_im, ssm_c_re, ssm_c_im, ssm_d, ssm_log_dt,
                ssm_glu_w, ssm_glu_b, proj_rnn, proj_attn, proj_ssm, w_out):
    B_, L_, _ = xn.shape
    h = xn @ w_in
    x_rnn, g_rnn, q, k, v, u, gate_logits = jnp.split(h, IN_SPLITS, axis=-1)
    y_rnn = rglru_branch(x_rnn, g_rnn, positions == 0, conv_w, conv_b, rg_wa, rg_ba, rg_wx, rg_bx, rg_lambda)
    q = rope(q.reshape(B_, L_, ATTN_HEADS, 2, ATTN_HEAD_DIM), positions)
    k = rope(k.reshape(B_, L_, ATTN_HEADS, 2, ATTN_HEAD_DIM), positions)
    lambda_init = 0.8 - 0.6 * math.exp(-0.3 * layer_idx)
    lam = (jnp.exp(jnp.sum(lam_q1.astype(jnp.float32) * lam_k1.astype(jnp.float32)))
           - jnp.exp(jnp.sum(lam_q2.astype(jnp.float32) * lam_k2.astype(jnp.float32))) + lambda_init)
    y_attn = diff_attention(q, k, v.reshape(B_, L_, ATTN_HEADS, ATTN_V_DIM), lam, lambda_init, subln_g)
    y_ssm = s5_branch(u, ssm_lambda_re, ssm_lambda_im, ssm_b_re, ssm_b_im, ssm_c_re, ssm_c_im, ssm_d,
                      ssm_log_dt, ssm_glu_w, ssm_glu_b)
    gates = jax.nn.sigmoid(gate_logits.astype(jnp.float32)).astype(xn.dtype).reshape(B_, L_, N_BRANCH, D_MODEL)
    merged = (gates[:, :, 0] * (y_rnn @ proj_rnn)
              + gates[:, :, 1] * (y_attn @ proj_attn)
              + gates[:, :, 2] * (y_ssm @ proj_ssm))
    return merged @ w_out

def hierarchical_moe(xn, rc_w, rc_b, rf_w, rf_b, w1, w3, w2):
    B_, L_, D = xn.shape
    xt = xn.reshape(B_ * L_, D)
    coarse = (xt @ rc_w + rc_b).astype(jnp.float32)
    p_group = jax.nn.softmax(coarse, axis=-1)
    _, g_idx = lax.top_k(coarse, 1)
    p_sel = jnp.take_along_axis(p_group, g_idx, axis=-1)
    fine = (xt @ rf_w + rf_b).astype(jnp.float32).reshape(-1, N_GROUPS, EXPERTS_PER_GROUP)
    fine_sel = jnp.take_along_axis(fine, g_idx[:, :, None], axis=1)[:, 0]
    top_vals, top_idx = lax.top_k(fine_sel, TOP_K_FINE)
    top_w = jax.nn.softmax(top_vals, axis=-1)
    fine_gate = jnp.einsum('nk,nke->ne', top_w, jax.nn.one_hot(top_idx, EXPERTS_PER_GROUP, dtype=jnp.float32))
    gate = ((p_sel * jax.nn.one_hot(g_idx[:, 0], N_GROUPS, dtype=jnp.float32))[:, :, None]
            * fine_gate[:, None, :]).astype(xn.dtype)
    out = jnp.zeros_like(xt)
    for gi in range(N_GROUPS):
        hid = jax.nn.silu(jnp.einsum('nd,edf->nef', xt, w1[gi])) * jnp.einsum('nd,edf->nef', xt, w3[gi])
        out = out + jnp.einsum('nef,ne,efd->nd', hid, gate[:, gi], w2[gi])
    return out.reshape(B_, L_, D)

def setup_inputs(seed: int = 0) -> dict:
    key = jax.random.key(seed)
    ks = iter(jax.random.split(key, 64))
    f32 = jnp.float32

    def nrm(shape, scale):
        return scale * jax.random.normal(next(ks), shape, f32)

    x = jax.random.normal(next(ks), (BATCH, SEQ, D_MODEL), f32)
    positions = jnp.broadcast_to(jnp.arange(SEQ, dtype=jnp.int32), (BATCH, SEQ))
    a0 = jnp.sqrt(jax.random.uniform(next(ks), (DEPTH, RNN_WIDTH), f32, 0.81, 0.998))
    n_idx = jnp.arange(SSM_STATE, dtype=f32)
    return {
        'x': x,
        'positions': positions,
        'mix_norm_g': 1.0 + nrm((DEPTH, D_MODEL), 0.02),
        'w_in': nrm((DEPTH, D_MODEL, IN_COLS), D_MODEL ** -0.5),
        'conv_w': nrm((DEPTH, CONV_WIDTH, RNN_WIDTH), CONV_WIDTH ** -0.5),
        'conv_b': nrm((DEPTH, RNN_WIDTH), 0.01),
        'rg_wa': nrm((DEPTH, RNN_BLOCKS, RNN_BLOCK, RNN_BLOCK), RNN_BLOCK ** -0.5),
        'rg_ba': nrm((DEPTH, RNN_WIDTH), 0.01),
        'rg_wx': nrm((DEPTH, RNN_BLOCKS, RNN_BLOCK, RNN_BLOCK), RNN_BLOCK ** -0.5),
        'rg_bx': nrm((DEPTH, RNN_WIDTH), 0.01),
        'rg_lambda': jnp.log(a0) - jnp.log1p(-a0),
        'lam_q1': nrm((DEPTH, ATTN_HEAD_DIM), 0.1),
        'lam_k1': nrm((DEPTH, ATTN_HEAD_DIM), 0.1),
        'lam_q2': nrm((DEPTH, ATTN_HEAD_DIM), 0.1),
        'lam_k2': nrm((DEPTH, ATTN_HEAD_DIM), 0.1),
        'subln_g': 1.0 + nrm((DEPTH, ATTN_V_DIM), 0.02),
        'ssm_lambda_re': -0.5 + nrm((DEPTH, SSM_GROUPS, SSM_STATE), 0.01),
        'ssm_lambda_im': math.pi * n_idx + nrm((DEPTH, SSM_GROUPS, SSM_STATE), 0.01),
        'ssm_b_re': nrm((DEPTH, SSM_GROUPS, SSM_STATE, SSM_GROUP), (2 * SSM_GROUP) ** -0.5),
        'ssm_b_im': nrm((DEPTH, SSM_GROUPS, SSM_STATE, SSM_GROUP), (2 * SSM_GROUP) ** -0.5),
        'ssm_c_re': nrm((DEPTH, SSM_GROUPS, SSM_GROUP, SSM_STATE), SSM_STATE ** -0.5),
        'ssm_c_im': nrm((DEPTH, SSM_GROUPS, SSM_GROUP, SSM_STATE), SSM_STATE ** -0.5),
        'ssm_d': nrm((DEPTH, SSM_GROUPS, SSM_GROUP), 1.0),
        'ssm_log_dt': jax.random.uniform(next(ks), (DEPTH, SSM_GROUPS), f32, math.log(1e-3), math.log(1e-1)),
        'ssm_glu_w': nrm((DEPTH, SSM_WIDTH, SSM_WIDTH), SSM_WIDTH ** -0.5),
        'ssm_glu_b': nrm((DEPTH, SSM_WIDTH), 0.01),
        'proj_rnn': nrm((DEPTH, RNN_WIDTH, D_MODEL), RNN_WIDTH ** -0.5),
        'proj_attn': nrm((DEPTH, ATTN_WIDTH, D_MODEL), ATTN_WIDTH ** -0.5),
        'proj_ssm': nrm((DEPTH, SSM_WIDTH, D_MODEL), SSM_WIDTH ** -0.5),
        'w_out': nrm((DEPTH, D_MODEL, D_MODEL), D_MODEL ** -0.5),
        'ffn_norm_g': 1.0 + nrm((DEPTH, D_MODEL), 0.02),
        'router_coarse_w': nrm((DEPTH, D_MODEL, N_GROUPS), D_MODEL ** -0.5),
        'router_coarse_b': nrm((DEPTH, N_GROUPS), 0.01),
        'router_fine_w': nrm((DEPTH, D_MODEL, N_GROUPS * EXPERTS_PER_GROUP), D_MODEL ** -0.5),
        'router_fine_b': nrm((DEPTH, N_GROUPS * EXPERTS_PER_GROUP), 0.01),
        'expert_w1': nrm((DEPTH, N_GROUPS, EXPERTS_PER_GROUP, D_MODEL, EXPERT_FF), D_MODEL ** -0.5),
        'expert_w3': nrm((DEPTH, N_GROUPS, EXPERTS_PER_GROUP, D_MODEL, EXPERT_FF), D_MODEL ** -0.5),
        'expert_w2': nrm((DEPTH, N_GROUPS, EXPERTS_PER_GROUP, EXPERT_FF, D_MODEL), EXPERT_FF ** -0.5),
        'final_norm_g': 1.0 + nrm((D_MODEL,), 0.02),
    }

def reference(x, positions, mix_norm_g, w_in, conv_w, conv_b, rg_wa, rg_ba, rg_wx, rg_bx, rg_lambda,
              lam_q1, lam_k1, lam_q2, lam_k2, subln_g,
              ssm_lambda_re, ssm_lambda_im, ssm_b_re, ssm_b_im, ssm_c_re, ssm_c_im, ssm_d, ssm_log_dt,
              ssm_glu_w, ssm_glu_b, proj_rnn, proj_attn, proj_ssm, w_out,
              ffn_norm_g, router_coarse_w, router_coarse_b, router_fine_w, router_fine_b,
              expert_w1, expert_w3, expert_w2, final_norm_g):
    for l in range(DEPTH):
        xn = rmsnorm(x, mix_norm_g[l])
        x = x + token_mixer(xn, positions, l, w_in[l], conv_w[l], conv_b[l], rg_wa[l], rg_ba[l],
                            rg_wx[l], rg_bx[l], rg_lambda[l], lam_q1[l], lam_k1[l], lam_q2[l], lam_k2[l],
                            subln_g[l], ssm_lambda_re[l], ssm_lambda_im[l], ssm_b_re[l], ssm_b_im[l],
                            ssm_c_re[l], ssm_c_im[l], ssm_d[l], ssm_log_dt[l], ssm_glu_w[l], ssm_glu_b[l],
                            proj_rnn[l], proj_attn[l], proj_ssm[l], w_out[l])
        xn = rmsnorm(x, ffn_norm_g[l])
        x = x + hierarchical_moe(xn, router_coarse_w[l], router_coarse_b[l], router_fine_w[l],
                                 router_fine_b[l], expert_w1[l], expert_w3[l], expert_w2[l])
    return rmsnorm(x, final_norm_g)


_drawn_inputs = setup_inputs


def setup_inputs(seed=0):
    import zlib

    import numpy as np

    out = dict(_drawn_inputs(seed))
    spreads = {}
    factors = {'rg_ba': 13.142,
     'rg_bx': 11.545,
     'ssm_lambda_re': 38.0,
     'ssm_glu_b': 7.838,
     'final_norm_g': 7.438,
     'ssm_c_re': 2.923,
     'ssm_c_im': 4.529}
    for name, (base, spread) in spreads.items():
        noise = np.random.default_rng([zlib.crc32(name.encode()), seed]).standard_normal(out[name].shape)
        drawn = base * np.exp(spread * noise) if base else spread * noise
        out[name] = __import__('jax').numpy.asarray(drawn.astype(out[name].dtype))
    for name, factor in factors.items():
        out[name] = (out[name] * factor).astype(out[name].dtype)
    return out
```

```python
from contextlib import ExitStack

import concourse.bass as bass
from concourse import mybir

F32 = mybir.dt.float32
I32 = mybir.dt.int32
ALU = mybir.AluOpType
ACT = mybir.ActivationFunctionType
AX = mybir.AxisListType.X
ds = bass.ds

P = 128
DEPTH = 2
D = 1024
KD = D // P
SEQ = 256
TT = SEQ // P
W = 512
KW = W // P
GATE0 = 6 * W
HEADS = 4
HD = 64
HALF = HD // 2
JT = 16
NS = 64
GI = 16
NEXP = 32
PAIRS = NEXP // 2
SLOTS = 64
FF = 512
MAX_PASSES = SEQ // SLOTS

UNITS = 6
UNIT = 2048
MIX_UNITS = 36
MIX_FILLS = MIX_UNITS // UNITS
PAIR_FILLS = 2

C_ID, C_TRI, C_MASK, C_I64, C_I32, C_FREQ, C_LINIT, C_ONEM = 0, 128, 256, 384, 448, 480, 512, 514
C_COLS = 516

R_DT, R_RE, R_IM, R_MIXG, R_FFNG, R_CW, R_CB, R_BA, R_BX, R_LAM, R_D, R_GLUB, R_SUB = (
    0, 16, 32, 48, 56, 64, 80, 84, 88, 92, 96, 100, 104)
R_ROWS = 105
N_PARAMS = 45

MAGIC = 12582912.0
INV_2PI = 0.15915494309189535
PI = 3.141592502593994
PI_2A, PI_2B, PI_2C = 6.28125, 0.0019350051879882812, 3.0199159819567e-07


def mixer_units():
    units = []
    for c in (5, 0, 1, 2, 3, 4):
        units += [("in", c * W, kh) for kh in range(2)]
    for c in range(6):
        units += [("in", GATE0 + c * W, kh) for kh in range(2)]
    for b in range(2):
        units += [("proj", b, h) for h in range(2)]
    units += [("glu", 0, 0), ("glu", 1, 0)]
    units += [("proj", 2, h) for h in range(2)]
    units += [("out", h, kh) for h in range(2) for kh in range(2)]
    assert len(units) == MIX_UNITS
    return units


def hybrid_kernel(nc, a, consts, out):
    ctx = ExitStack()
    with ctx:
        def sb(name, shape, dt=F32):
            return ctx.enter_context(nc.sbuf_tensor(name, shape, dt))

        def sem(name):
            return ctx.enter_context(nc.semaphore(name))

        ring = sb("ring", [P, UNITS, UNIT])
        cst = sb("cst", [P, C_COLS])
        x = sb("x", [P, TT, D])
        xT = sb("xT", [P, KD, SEQ])
        stage = sb("stage", [P, TT, D])
        qkv = sb("qkv", [P, TT, 3 * W])
        gates = sb("gates", [P, TT, 3 * D])
        xrT = sb("xrT", [P, KW, SEQ + 3])
        grT = sb("grT", [P, KW, SEQ])
        uT = sb("uT", [P, KW, SEQ])
        zT = sb("zT", [P, KW, SEQ])
        qT = sb("qT", [P, HEADS, SEQ])
        kT = sb("kT", [P, HEADS, SEQ])
        work = sb("work", [P, 4, 4 * SEQ])
        tcos = sb("tcos", [P, 4, SEQ])
        tsin = sb("tsin", [P, 4, SEQ])
        bcos = sb("bcos", [P, JT, 32])
        bsin = sb("bsin", [P, JT, 32])
        attn_e = sb("attn_e", [P, 2, SEQ])
        attn_w = sb("attn_w", [P, SEQ])
        attn_wT = sb("attn_wT", [P, 2, P])
        attn_o = sb("attn_o", [P, TT, W])
        raw = sb("raw", [P, P])
        ldt = sb("ldt", [16, 2])
        col = sb("col", [P, P])
        lamv = sb("lamv", [P, 4, HD])
        rbias = sb("rbias", [P, 36])
        rw = sb("rw", [P, KD, 36])
        wa = sb("wa", [P, KW, P])
        wx = sb("wx", [P, KW, P])
        bnat = sb("bnat", [P, 2, JT, 2 * GI])
        bmat = sb("bmat", [P, 2, KW, P])
        cdup = sb("cdup", [P, 2, KW, P])
        ccoef = sb("ccoef", [P, 3, JT, 2 * GI])
        s5 = sb("s5", [P, 24, JT])
        pre = sb("pre", [P, JT, 8, 2])
        rc = sb("rc", [P, TT, HALF])
        rsn = sb("rsn", [P, TT, HALF])
        notreset = sb("notreset", [P, SEQ])
        small = sb("small", [P, 160])
        lg = sb("lg", [P, TT, 36])
        ro = sb("ro", [P, 6, TT, NEXP])
        rank = sb("rank", [P, TT, NEXP + 2])
        gate = sb("gate", [P, TT, NEXP + 2])
        passes = sb("passes", [P, 1], I32)
        passes_f = sb("passes_f", [P, 1])
        ones = sb("ones", [P, P])
        pos_i = sb("pos_i", [P, TT], I32)
        isreset = sb("isreset", [P, SEQ])
        ps = ctx.enter_context(nc.psum_tensor("ps", [P, 8, 512], F32))

        ident = cst[:, C_ID:C_ID + P]
        xe = work[:, 0, :].rearrange("p (k s) -> p k s", k=KD)
        ye = work[:, 1, :]
        hid = work[:, 2, 0:FF]
        sil = work[:, 2, FF:2 * FF]
        hT = work[:, 3, 0:FF].rearrange("p (f s) -> p f s", f=4)
        pgT = work[:, 3, FF:FF + SEQ]
        onehot = attn_o[:, :, 0:P]
        weighted = attn_o[:, :, P:2 * P]

        ring_ready = [sem(f"ring_ready{i}") for i in range(UNITS)]
        unit_used = [sem(f"unit_used{i}") for i in range(UNITS)]
        params_ready = sem("params_ready")
        fill_paced = sem("fill_paced")
        start_ready = sem("start_ready")
        zeroed = sem("zeroed")
        out_ready = sem("out_ready")
        stored = sem("stored")
        layer_sems = []

        def lsem(name):
            s = sem(name)
            layer_sems.append(s)
            return s

        arrive = sem("arrive")
        release_pe, release_act = sem("release_pe"), sem("release_act")
        dve_step, act_step = lsem("dve_step"), lsem("act_step")
        dve_moe_step, act_moe_step = sem("dve_moe_step"), sem("act_moe_step")
        param_cols, col_copied = lsem("param_cols"), lsem("col_copied")
        raw_dt = lsem("raw_dt")
        b_turned, b_copied = lsem("b_turned"), lsem("b_copied")
        c_turned, c_copied = lsem("c_turned"), lsem("c_copied")
        ss_ready, var_ready, root_ready = lsem("ss_ready"), lsem("var_ready"), lsem("root_ready")
        xn_ready, xn_turned, xT_ready = lsem("xn_ready"), lsem("xn_turned"), lsem("xT_ready")
        chunk_out = lsem("chunk_out")
        turned, turn_copied = lsem("turned"), lsem("turn_copied")
        fn_asked, fn_served = lsem("fn_asked"), lsem("fn_served")
        sp_ready = lsem("sp_ready")
        conv_ready, rgate_done, rgate_out = lsem("conv_ready"), lsem("rgate_done"), lsem("rgate_out")
        rg_root, gelu_g, yrnn_ready = lsem("rg_root"), lsem("gelu_g"), lsem("yrnn_ready")
        rope_ready = lsem("rope_ready")
        score_done, scores_read, w_ready = lsem("score_done"), lsem("scores_read"), lsem("w_ready")
        prob_in, prob_ready = lsem("prob_in"), lsem("prob_ready")
        wT_done, wT_out, o_done, o_out = lsem("wT_done"), lsem("wT_out"), lsem("o_done"), lsem("o_out")
        o_normed, oT_done, oT_out = lsem("o_normed"), lsem("oT_done"), lsem("oT_out")
        bu_done, bu_read = lsem("bu_done"), lsem("bu_read")
        s_ready, y_done, y_read = lsem("s_ready"), lsem("y_done"), lsem("y_read")
        z_in, z_out, glu_out, yssm_ready = lsem("z_in"), lsem("z_out"), lsem("glu_out"), lsem("yssm_ready")
        proj_read = lsem("proj_read")
        m_turned, m_copied = lsem("m_turned"), lsem("m_copied")
        res_read = lsem("res_read")
        logit_done, sel_ready, cum_done = lsem("logit_done"), lsem("sel_ready"), lsem("cum_done")
        blank_pair = lsem("blank_pair")
        passes_pe, passes_act, passes_sp = sem("passes_pe"), sem("passes_act"), sem("passes_sp")
        silu_out, hid_ready = sem("silu_out"), sem("hid_ready")
        hT_done, hT_out = sem("hT_done"), sem("hT_out")
        pgT_done, pgT_out = sem("pgT_done"), sem("pgT_out")
        gather_done, xe_out, onehot_ready, weighted_ready = (
            sem("gather_done"), sem("xe_out"), sem("onehot_ready"), sem("weighted_ready"))
        ye_out = sem("ye_out")
        scat_done, scat_read = sem("scat_done"), sem("scat_read")
        rank_moved, layer_out, final_g_ready = sem("rank_moved"), sem("layer_out"), sem("final_g_ready")
        angle_ready, sine_ready = sem("angle_ready"), sem("sine_ready")
        final_in, final_out = sem("final_in"), sem("final_out")

        units = mixer_units()

        def used_in_mixer(eng, i, l, p0):
            eng.wait_ge(unit_used[i % UNITS], l * MIX_FILLS + p0 * (PAIRS * PAIR_FILLS) + (i // UNITS + 2))

        def used_in_pair(eng, u, l, g):
            eng.wait_ge(unit_used[u % UNITS], (l + 1) * MIX_FILLS + g * PAIR_FILLS + (u // UNITS + 2))
        block = ctx.enter_context(nc.Block())

        @block.sync
        def _(sp):
            w_in = a["w_in"].rearrange("l (kh k p) n -> l kh p k n", kh=2, p=P)
            w_out = a["w_out"].rearrange("l (kh k p) n -> l kh p k n", kh=2, p=P)
            proj = [a[n].rearrange("l (k p) n -> l p k n", p=P) for n in ("proj_rnn", "proj_attn", "proj_ssm")]
            glu = a["ssm_glu_w"].rearrange("l (h k p) n -> l h p k n", h=2, p=P)
            w1 = a["expert_w1"].rearrange("l g e (kh k p) f -> (l g e) kh p k f", kh=2, p=P)
            w3 = a["expert_w3"].rearrange("l g e (kh k p) f -> (l g e) kh p k f", kh=2, p=P)
            w2 = a["expert_w2"].rearrange("l g e (k p) n -> (l g e) p k n", p=P)

            def one(ap, l):
                v = ap[ds(l, 1)]
                names = " ".join("bcdef"[:len(v.shape) - 1])
                return v.rearrange(f"a {names} -> (a {names.split()[0]}) {' '.join(names.split()[1:])}")

            sp.dma_start(cst[:, :], consts).then_inc(start_ready, 16)
            sp.dma_start(x[:, :, :], a["x"].rearrange("b (t p) d -> (b p) t d", p=P)).then_inc(start_ready, 16)
            with nc.allow_non_contiguous_dma(reason="one position per partition"):
                sp.dma_start(pos_i[:, :], a["positions"].rearrange("b (t p) -> (b p) t", p=P)).then_inc(start_ready, 16)
            sp.dma_start(notreset[:, :].bitcast(I32), a["positions"].to_broadcast([P, SEQ])).then_inc(start_ready, 16)
            sp.wait_ge(zeroed, 1)

            with sp.Fori(0, DEPTH) as l:
                p0 = sp.value_load(passes[0:1, 0:1], min_val=0, max_val=MAX_PASSES * DEPTH)

                loads = [0]

                def load(dst, src):
                    loads[0] += 1
                    sp.dma_start(dst, src).then_inc(params_ready, 16)

                def rows(r, name, n):
                    v = a[name][ds(l, 1)]
                    names = "b c d"[:2 * len(v.shape) - 3]
                    load(raw[r:r + n, :], v.rearrange(f"a {names} -> (a {names})").rearrange("(n p) -> n p", p=P))

                with nc.allow_non_contiguous_dma(reason="small parameters"):
                    load(ldt[:, :], a["ssm_log_dt"][ds(l, 1)].rearrange("a (j h) -> (a j) h", h=2))
                    rows(R_RE, "ssm_lambda_re", 16)
                    rows(R_IM, "ssm_lambda_im", 16)
                    rows(R_MIXG, "mix_norm_g", 8)
                    rows(R_FFNG, "ffn_norm_g", 8)
                    rows(R_CW, "conv_w", 16)
                    rows(R_CB, "conv_b", 4)
                    rows(R_BA, "rg_ba", 4)
                    rows(R_BX, "rg_bx", 4)
                    rows(R_LAM, "rg_lambda", 4)
                    rows(R_D, "ssm_d", 4)
                    rows(R_GLUB, "ssm_glu_b", 4)
                    rows(R_SUB, "subln_g", 1)
                    for n, name in enumerate(("ssm_b_re", "ssm_b_im")):
                        b = a[name][ds(l, 1)].rearrange("a (j h) n i -> (a h) n j i", h=2)
                        for h in range(2):
                            load(bnat[NS * h:NS * h + NS, n, :, GI * h:GI * h + GI], b[h])
                    for n, name in enumerate(("ssm_c_re", "ssm_c_im")):
                        c = a[name][ds(l, 1)].rearrange("a (k j h) i n -> (a j) h i k n", k=KW, h=2)
                        for j in range(4):
                            for h in range(2):
                                r = 32 * j + GI * h
                                load(cdup[r:r + GI, n, :, NS * h:NS * h + NS], c[j, h])
                    for t, name in ((wa, "rg_wa"), (wx, "rg_wx")):
                        g = a[name][ds(l, 1)].rearrange("a (k h) i j -> (a h) i k j", h=2)
                        for h in range(2):
                            load(t[64 * h:64 * h + 64, :, 64 * h:64 * h + 64], g[h])
                    for n, name in enumerate(("lam_q1", "lam_k1", "lam_q2", "lam_k2")):
                        load(lamv[:, n, :], a[name][ds(l, 1)].to_broadcast([P, HD]))
                    load(rbias[:, 0:4], a["router_coarse_b"][ds(l, 1)].to_broadcast([P, 4]))
                    load(rbias[:, 4:36], a["router_fine_b"][ds(l, 1)].to_broadcast([P, NEXP]))
                    load(rw[:, :, 0:4], a["router_coarse_w"][ds(l, 1)].rearrange("a (k p) n -> (a p) k n", p=P))
                    load(rw[:, :, 4:36], a["router_fine_w"][ds(l, 1)].rearrange("a (k p) n -> (a p) k n", p=P))
                assert loads[0] == N_PARAMS, loads[0]

                def fill(u, before, src, paced=False):
                    sp.wait_ge(unit_used[u], before + 1)
                    if paced:
                        sp.sem_inc(fill_paced, 1)
                    n = src.shape[-1]
                    sp.dma_start(ring[:, u, :].rearrange("p (k n) -> p k n", n=n), src).then_inc(ring_ready[u], 16)

                for i, (name, b, c) in enumerate(units):
                    before = l * MIX_FILLS + p0 * (PAIRS * PAIR_FILLS) + i // UNITS
                    if name == "in":
                        src = w_in[ds(l, 1), c, :, :, b:b + W]
                    elif name == "proj":
                        src = proj[b][ds(l, 1), :, :, c * W:(c + 1) * W]
                    elif name == "glu":
                        src = glu[ds(l, 1), b]
                    else:
                        src = w_out[ds(l, 1), c, :, :, b * W:(b + 1) * W]
                    src = src.rearrange("a p k n -> (a p) k n")
                    if name == "glu":
                        sp.wait_ge(unit_used[i % UNITS], before + 1)
                        sp.dma_start(ring[:, i % UNITS, 0:2 * W].rearrange("p (k n) -> p k n", n=W),
                                     src).then_inc(ring_ready[i % UNITS], 16)
                    else:
                        fill(i % UNITS, before, src, paced=(i == 2))

                sp.wait_ge(passes_sp, 1)
                sp.sem_clear(passes_sp)
                p1 = sp.value_load(passes[0:1, 0:1], min_val=0, max_val=MAX_PASSES * DEPTH)
                with sp.Fori(p0, p1) as p:
                    with sp.Fori(0, PAIRS) as i:
                        before = (l + 1) * MIX_FILLS + (p * PAIRS + i) * PAIR_FILLS
                        u = 0
                        for w in (w1, w3):
                            for kh in range(2):
                                for e in range(2):
                                    src = w[ds(l * NEXP + i * 2 + e, 1), kh].rearrange("a p k n -> (a p) k n")
                                    fill(u % UNITS, before + u // UNITS, src)
                                    u += 1
                        for h in range(2):
                            for e in range(2):
                                src = w2[ds(l * NEXP + i * 2 + e, 1), :, :, h * W:(h + 1) * W]
                                fill(u % UNITS, before + u // UNITS, src.rearrange("a p k n -> (a p) k n"))
                                u += 1

            sp.wait_ge(layer_out, DEPTH)
            sp.dma_start(gates[:, 0, 0:D], a["final_norm_g"].to_broadcast([P, D])).then_inc(final_g_ready, 16)
            sp.wait_ge(out_ready, 1)
            sp.dma_start(out.rearrange("b (t p) d -> (b p) t d", p=P), stage[:, :, :]).then_inc(stored, 16)
            sp.wait_ge(stored, 16)

        @block.tensor
        def _(pe):
            for u in range(UNITS):
                pe.nop().then_inc(unit_used[u], 1)
            pe.wait_ge(start_ready, 64)
            pe.wait_ge(zeroed, 1)

            with pe.Fori(0, DEPTH) as l:
                p0 = pe.value_load(passes[0:1, 0:1], min_val=0, max_val=MAX_PASSES * DEPTH)
                pe.nop().then_inc(arrive, 1)
                pe.wait_ge(release_pe, 1)
                pe.sem_clear(release_pe)

                pe.wait_ge(params_ready, (l + 1) * (16 * N_PARAMS))
                pe.wait_ge(raw_dt, 1)
                pe.transpose(ps[:, 6, 0:R_ROWS], raw[0:R_ROWS, :], ident[0:R_ROWS, 0:R_ROWS]).then_inc(param_cols, 1)
                for n in range(2):
                    for k in range(KW):
                        v = bnat[:, n, 4 * k:4 * k + 4, :].rearrange("p j c -> p (j c)")
                        mm = pe.transpose(ps[:, 4 + n, k * P:(k + 1) * P], v, ident)
                mm.then_inc(b_turned, 1)
                pe.wait_ge(col_copied, 1)
                for n in range(2):
                    for k in range(KW):
                        mm = pe.transpose(ps[:, 6 + n, k * P:(k + 1) * P], cdup[:, n, k, :], ident)
                mm.then_inc(c_turned, 1)

                def turn_x():
                    for k in range(KD):
                        for t in range(TT):
                            mm = pe.transpose(ps[:, k // 2, (k % 2) * SEQ + t * P:(k % 2) * SEQ + (t + 1) * P],
                                              stage[:, t, k * P:(k + 1) * P], ident)
                    return mm

                pe.wait_ge(xn_ready, 1)
                turn_x().then_inc(xn_turned, 1)

                def unit_ready(i):
                    pe.wait_ge(ring_ready[i % UNITS], (l * MIX_FILLS + p0 * (PAIRS * PAIR_FILLS) + (i // UNITS + 1)) * 16)

                def in_half(c, kh):
                    i = 2 * c + kh
                    if kh == 0 and c >= 2:
                        pe.wait_ge(chunk_out, c - 1)
                    unit_ready(i)
                    wt = ring[:, i % UNITS, :].rearrange("p (k n) -> p k n", n=W)
                    for t in range(TT):
                        for k in range(4):
                            kk = 4 * kh + k
                            mm = pe.matmul(ps[:, 2 * (c % 2) + t, :], xT[:, kk, t * P:(t + 1) * P], wt[:, k, :],
                                           start=(kk == 0), stop=(kk == KD - 1))
                    mm.then_inc(unit_used[i % UNITS], 1)

                def turn_chunk(n, src, wait_chunk):
                    pe.wait_ge(wait_chunk[0], wait_chunk[1])
                    if n >= 1:
                        pe.wait_ge(turn_copied, n)
                    for k in range(KW):
                        for t in range(TT):
                            mm = pe.transpose(ps[:, 6 + k // 2, (k % 2) * SEQ + t * P:(k % 2) * SEQ + (t + 1) * P],
                                              src(t, k), ident)
                    mm.then_inc(turned, 1)

                def staged(c):
                    return lambda t, k: stage[:, t, (c % 2) * W + k * P:(c % 2) * W + (k + 1) * P]

                pe.wait_ge(xT_ready, 1)
                pe.wait_ge(c_copied, 1)
                for c in range(6):
                    in_half(c, 0)
                    in_half(c, 1)
                    if 1 <= c <= 3:
                        turn_chunk(c - 1, staged(c - 1), (chunk_out, c))

                def rgate(n, wt):
                    if n == 0:
                        pe.wait_ge(conv_ready, 1)
                        pe.wait_ge(turn_copied, 3)
                    else:
                        pe.wait_ge(rgate_out, 1)
                    for k in range(KW):
                        mm = pe.matmul(ps[:, 6 + k // 2, (k % 2) * SEQ:(k % 2 + 1) * SEQ], wt[:, k, :],
                                       work[:, 0, k * SEQ:(k + 1) * SEQ], start=True, stop=True)
                    mm.then_inc(rgate_done, 1)

                rgate(0, wa)
                in_half(6, 0)
                rgate(1, wx)
                in_half(6, 1)
                pe.wait_ge(rgate_out, 2)
                turn_chunk(3, lambda t, k: qkv[:, t, k * P:(k + 1) * P], (rope_ready, 1))
                in_half(7, 0)
                turn_chunk(4, lambda t, k: qkv[:, t, W + k * P:W + (k + 1) * P], (rope_ready, 1))
                in_half(7, 1)

                def scores(n):
                    h, t = divmod(n, TT)
                    if n == 0:
                        pe.wait_ge(turn_copied, 5)
                        pe.wait_ge(b_copied, 1)
                    else:
                        pe.wait_ge(scores_read, n)
                    for c in range(2):
                        mm = pe.matmul(ps[:, 5 + c, 0:(t + 1) * P], qT[64 * c:64 * c + 64, h, t * P:(t + 1) * P],
                                       kT[64 * c:64 * c + 64, h, 0:(t + 1) * P], start=True, stop=True)
                    mm.then_inc(score_done, 1)

                def turn_w(n):
                    h, t = divmod(n, TT)
                    pe.wait_ge(w_ready, n + 1)
                    if n >= 1:
                        pe.wait_ge(o_out, n)
                    for k in range(t + 1):
                        mm = pe.transpose(ps[:, 7, k * P:(k + 1) * P], attn_w[:, k * P:(k + 1) * P], ident)
                    mm.then_inc(wT_done, 1)

                def attend(n):
                    h, t = divmod(n, TT)
                    pe.wait_ge(wT_out, n + 1)
                    for k in range(t + 1):
                        mm = pe.matmul(ps[:, 7, 2 * P:3 * P], attn_wT[:, k, :], qkv[:, k, 2 * W + h * P:2 * W + (h + 1) * P],
                                       start=(k == 0), stop=(k == t))
                    mm.then_inc(o_done, 1)

                def bu(m):
                    if m >= 1:
                        pe.wait_ge(bu_read, m)
                    for j in (2 * m, 2 * m + 1):
                        k, q = divmod(j, 4)
                        for n in range(2):
                            mm = pe.matmul(ps[:, 4 + j % 2, n * SEQ:(n + 1) * SEQ], bmat[32 * q:32 * q + 32, n, k, :],
                                           uT[32 * q:32 * q + 32, k, :], start=True, stop=True)
                    mm.then_inc(bu_done, 1)

                fillers = [(c, kh) for c in range(8, 12) for kh in range(2)]
                scores(0)
                for n in range(2 * HEADS):
                    in_half(*fillers[n])
                    turn_w(n)
                    if n + 1 < 2 * HEADS:
                        scores(n + 1)
                    attend(n)

                def cy(k):
                    pe.wait_ge(s_ready, k + 1)
                    if k >= 1:
                        pe.wait_ge(y_read, k)
                    for q in range(4):
                        j = 4 * k + q
                        for n, (cm, w) in enumerate(((0, 0), (1, 1), (2, 2), (2, 3))):
                            mm = pe.matmul(ps[32 * q:32 * q + 32, 6, 0:SEQ], ccoef[:, cm, j, :],
                                           work[:, w, q * SEQ:(q + 1) * SEQ], start=(n == 0), stop=(n == 3))
                    mm.then_inc(y_done, 1)

                def project(b, yT, halves):
                    for h in halves:
                        i = (24, 26, 30)[b] + h
                        n = 2 * b + h
                        if n == 0:
                            pe.wait_ge(chunk_out, 12)
                        if n >= 2:
                            pe.wait_ge(proj_read, n - 1)
                        unit_ready(i)
                        wt = ring[:, i % UNITS, :].rearrange("p (k n) -> p k n", n=W)
                        for t in range(TT):
                            for k in range(KW):
                                mm = pe.matmul(ps[:, 2 * (n % 2) + t, :], yT[:, k, t * P:(t + 1) * P], wt[:, k, :],
                                               start=(k == 0), stop=(k == KW - 1))
                        mm.then_inc(unit_used[i % UNITS], 1)

                bu(0)
                pe.wait_ge(yrnn_ready, 1)
                project(0, grT, (0, 1))
                bu(1)
                pe.wait_ge(o_normed, 1)
                for h in range(HEADS):
                    for t in range(TT):
                        mm = pe.transpose(ps[:, 6 + h // 2, (h % 2) * SEQ + t * P:(h % 2) * SEQ + (t + 1) * P],
                                          attn_o[:, t, h * P:(h + 1) * P], ident)
                mm.then_inc(oT_done, 1)
                pe.wait_ge(oT_out, 1)
                project(1, qT, (0,))
                bu(2)
                project(1, qT, (1,))
                cy(0)
                bu(3)
                bu(4)
                cy(1)
                bu(5)
                bu(6)
                cy(2)
                bu(7)
                cy(3)
                pe.wait_ge(z_out, 1)
                unit_ready(28)
                unit_ready(29)
                for m in range(KW):
                    for k in range(KW):
                        wt = ring[:, (28 + k // 2) % UNITS, 0:2 * W].rearrange("p (k n) -> p k n", n=W)
                        mm = pe.matmul(ps[:, 4 + m // 2, (m % 2) * SEQ:(m % 2 + 1) * SEQ], wt[:, k % 2, m * P:(m + 1) * P],
                                       zT[:, k, :], start=(k == 0), stop=(k == KW - 1))
                        if m == KW - 1 and k % 2 == 1:
                            mm.then_inc(unit_used[(28 + k // 2) % UNITS], 1)
                pe.wait_ge(yssm_ready, 1)
                project(2, uT, (0, 1))
                pe.wait_ge(proj_read, 6)
                turn_x().then_inc(m_turned, 1)
                pe.wait_ge(m_copied, 1)
                for h in range(2):
                    for kh in range(2):
                        i = 32 + 2 * h + kh
                        unit_ready(i)
                        wt = ring[:, i % UNITS, :].rearrange("p (k n) -> p k n", n=W)
                        for t in range(TT):
                            for k in range(4):
                                kk = 4 * kh + k
                                mm = pe.matmul(ps[:, 2 * h + t, :], xT[:, kk, t * P:(t + 1) * P], wt[:, k, :],
                                               start=(kk == 0), stop=(kk == KD - 1))
                        mm.then_inc(unit_used[i % UNITS], 1)

                pe.wait_ge(xn_ready, 2)
                turn_x().then_inc(xn_turned, 1)
                pe.wait_ge(xT_ready, 2)
                for t in range(TT):
                    for k in range(KD):
                        mm = pe.matmul(ps[:, 6, t * 64:t * 64 + 36], xT[:, k, t * P:(t + 1) * P], rw[:, k, :],
                                       start=(k == 0), stop=(k == KD - 1))
                mm.then_inc(logit_done, 1)
                pe.wait_ge(sel_ready, 1)
                sel = ro[:, 0, :, :]
                tri = cst[:, C_TRI:C_TRI + P]
                pe.matmul(ps[:, 7, 0:32], tri, sel[:, 0, :], start=True, stop=True)
                pe.matmul(ps[:, 7, 32:64], ones[:, :], sel[:, 0, :], start=True, stop=False)
                pe.matmul(ps[:, 7, 32:64], tri, sel[:, 1, :], start=False, stop=True)
                pe.matmul(ps[:, 7, 64:96], ones[:, :], sel[:, 0, :], start=True, stop=False)
                pe.matmul(ps[:, 7, 64:96], ones[:, :], sel[:, 1, :], start=False, stop=True).then_inc(cum_done, 1)

                pe.wait_ge(passes_pe, 1)
                pe.sem_clear(passes_pe)
                p1 = pe.value_load(passes[0:1, 0:1], min_val=0, max_val=MAX_PASSES * DEPTH)

                def gather(ready):
                    pe.wait_ge(onehot_ready, ready)
                    pe.wait_ge(xe_out, ready)
                    for k in range(KD):
                        for t in range(TT):
                            mm = pe.matmul(ps[:, 4 + k // 4, (k % 4) * P:(k % 4 + 1) * P], stage[:, t, k * P:(k + 1) * P],
                                           onehot[:, t, :], start=(t == 0), stop=(t == TT - 1))
                    mm.then_inc(gather_done, 1)

                def scatter(g):
                    for n in range(2 * TT):
                        h, t = divmod(n, TT)
                        pe.wait_ge(scat_read, g * (2 * TT) + n + 1)
                        pe.matmul(ps[:, 7 - n % 2, :], pgT[:, t * P:(t + 1) * P], ye[:, h * W:(h + 1) * W],
                                  start=True, stop=True).then_inc(scat_done, 1)

                pe.wait_ge(blank_pair, 1)
                gather((l + 1) + p0 * PAIRS)
                with pe.Fori(p0, p1) as p:
                    with pe.Fori(0, PAIRS) as i:
                        g = p * PAIRS + i
                        fills = (l + 1) * MIX_FILLS + g * PAIR_FILLS
                        pe.wait_ge(xe_out, g + (l + 2))
                        u = 0
                        for n in range(2):
                            for kh in range(2):
                                for e in range(2):
                                    pe.wait_ge(ring_ready[(u + e) % UNITS], (fills + ((u + e) // UNITS + 1)) * 16)
                                for k in range(4):
                                    kk = 4 * kh + k
                                    for e in range(2):
                                        wt = ring[:, (u + e) % UNITS, :].rearrange("p (k n) -> p k n", n=W)
                                        mm = pe.matmul(ps[64 * e:64 * e + 64, n, :], xe[:, kk, 64 * e:64 * e + 64], wt[:, k, :],
                                                       start=(kk == 0), stop=(kk == KD - 1))
                                        if k == 3:
                                            mm.then_inc(unit_used[(u + e) % UNITS], 1)
                                u += 2
                        pe.wait_ge(ye_out, g + 1)
                        pe.wait_ge(pgT_out, g + 1)
                        scatter(g + l)
                        pe.wait_ge(hid_ready, g + 1)
                        pe.wait_ge(scat_read, (g + l + 1) * (2 * TT) + 2)
                        for f in range(4):
                            mm = pe.transpose(ps[:, 6, f * P:(f + 1) * P], hid[:, f * P:(f + 1) * P], ident)
                        mm.then_inc(hT_done, 1)
                        pe.wait_ge(weighted_ready, g + (l + 1))
                        for t in range(TT):
                            mm = pe.transpose(ps[:, 7, t * P:(t + 1) * P], weighted[:, t, :], ident)
                        mm.then_inc(pgT_done, 1)
                        gather(g + (l + 2))
                        pe.wait_ge(hT_out, g + 1)
                        for h in range(2):
                            for e in range(2):
                                pe.wait_ge(ring_ready[(u + e) % UNITS], (fills + ((u + e) // UNITS + 1)) * 16)
                            for k in range(4):
                                for e in range(2):
                                    wt = ring[:, (u + e) % UNITS, :].rearrange("p (k n) -> p k n", n=W)
                                    mm = pe.matmul(ps[64 * e:64 * e + 64, 2 + h, :], hT[:, k, 64 * e:64 * e + 64], wt[:, k, :],
                                                   start=(k == 0), stop=(k == 3))
                                    if k == 3:
                                        mm.then_inc(unit_used[(u + e) % UNITS], 1)
                            u += 2
                pe.wait_ge(ye_out, p1 * PAIRS + 1)
                pe.wait_ge(pgT_out, p1 * PAIRS + 1)
                scatter(p1 * PAIRS + l)

        @block.scalar
        def _(act):
            act.wait_ge(start_ready, 64)
            act.wait_ge(zeroed, 1)

            act.nop().then_inc(xe_out, 1)
            act.nop().then_inc(ye_out, 1)
            act.nop().then_inc(pgT_out, 1)
            act.wait_ge(angle_ready, 1)
            act.activation(rsn[:, :, :], rsn[:, :, :], ACT.Sin).then_inc(sine_ready, 1)
            act.activation(rc[:, :, :], rc[:, :, :], ACT.Sin).then_inc(sine_ready, 1)

            with act.Fori(0, DEPTH) as l:
                p0 = act.value_load(passes[0:1, 0:1], min_val=0, max_val=MAX_PASSES * DEPTH)
                act.nop().then_inc(arrive, 1)
                act.wait_ge(release_act, 1)
                act.sem_clear(release_act)
                steps = [0]

                def after(ins):
                    steps[0] += 1
                    ins.then_inc(act_step, 1)
                    act.wait_ge(act_step, steps[0])

                def squares():
                    for t in range(TT):
                        after(act.activation(work[:, 3, :], x[:, t, :], ACT.Square, accum_out=small[:, t:t + 1]))
                    act.nop().then_inc(ss_ready, 1)

                def root(n, v, m):
                    act.wait_ge(var_ready, m)
                    act.activation(v, v, ACT.Sqrt).then_inc(root_ready, 1)

                def turn_out(n, g0):
                    act.wait_ge(xn_turned, n)
                    for k in range(KD):
                        ins = act.activation(xT[:, k, :], ps[:, k // 2, (k % 2) * SEQ:(k % 2 + 1) * SEQ], ACT.Copy,
                                             scale=col[:, g0 + k:g0 + k + 1])
                        after(ins)
                    act.nop().then_inc(xT_ready, 1)

                squares()
                root(0, small[:, 2:4], 1)
                act.wait_ge(param_cols, 1)
                after(act.activation(col[:, 0:R_ROWS], ps[:, 6, 0:R_ROWS], ACT.Copy))
                act.nop().then_inc(col_copied, 1)
                act.nop().then_inc(col_copied, 1)
                act.wait_ge(b_turned, 1)
                for n in range(2):
                    after(act.activation(bmat[:, n, :, :].rearrange("p k c -> p (k c)"), ps[:, 4 + n, :], ACT.Copy))
                act.nop().then_inc(b_copied, 1)
                act.wait_ge(c_turned, 1)
                after(act.activation(work[:, 0, :], ps[:, 6:8, :].rearrange("p b n -> p (b n)"), ACT.Copy))
                act.nop().then_inc(c_copied, 1)
                act.nop().then_inc(c_copied, 1)
                turn_out(1, R_MIXG)

                for m, (v, f) in enumerate(((small[:, 20:40], ACT.Tanh), (s5[:, 0, :], ACT.Tanh),
                                            (small[:, 86:88], ACT.Exp), (s5[:, 3:5, :], ACT.Sin))):
                    act.wait_ge(fn_asked, m + 1)
                    act.activation(v, v, f).then_inc(fn_served, 1)

                def chunk(c):
                    used_in_mixer(act, 2 * c + 1, l, p0)
                    if c < 3:
                        if c >= 2:
                            act.wait_ge(turned, c - 1)
                        dst = stage[:, :, (c % 2) * W:(c % 2 + 1) * W]
                    elif c < 6:
                        dst = qkv[:, :, (c - 3) * W:(c - 2) * W]
                    else:
                        dst = gates[:, :, (c - 6) * W:(c - 5) * W]
                    act.activation(dst, ps[:, 2 * (c % 2):2 * (c % 2) + 2, :], ACT.Copy if c < 6 else ACT.Sigmoid)\
                       .then_inc(chunk_out, 1)

                def turn_copy(n, dst):
                    act.wait_ge(turned, n + 1)
                    act.activation(dst, ps[:, 6:8, :].rearrange("p b (k s) -> p (b k) s", s=SEQ), ACT.Copy)\
                       .then_inc(turn_copied, 1)

                chunk(0)
                chunk(1)
                turn_copy(0, uT[:, :, :])
                chunk(2)
                turn_copy(1, xrT[:, :, 3:])
                chunk(3)
                turn_copy(2, grT[:, :, :])
                chunk(4)
                chunk(5)
                for n, dst in enumerate((1, 2)):
                    act.wait_ge(rgate_done, n + 1)
                    for k in range(KW):
                        b = (R_BA, R_BX)[n] + k
                        after(act.activation(work[:, dst, k * SEQ:(k + 1) * SEQ],
                                             ps[:, 6 + k // 2, (k % 2) * SEQ:(k % 2 + 1) * SEQ], ACT.Sigmoid,
                                             bias=col[:, b:b + 1]))
                    act.nop().then_inc(rgate_out, 1)
                act.wait_ge(sp_ready, 1)
                for k in range(KW):
                    after(act.activation(work[:, 1, k * SEQ:(k + 1) * SEQ], work[:, 1, k * SEQ:(k + 1) * SEQ], ACT.Tanh,
                                         scale=small[:, 44 + k:45 + k]))
                after(act.activation(work[:, 3, :], work[:, 1, :], ACT.Sqrt))
                act.nop().then_inc(rg_root, 1)
                after(act.activation(grT[:, :, :], grT[:, :, :], ACT.Gelu_apprx_tanh))
                act.nop().then_inc(gelu_g, 1)
                chunk(6)
                turn_copy(3, qT[:, :, :])
                turn_copy(4, kT[:, :, :])
                chunk(7)

                for n in range(2 * HEADS):
                    h, t = divmod(n, TT)
                    act.wait_ge(prob_in, n + 1)
                    for c in range(2):
                        after(act.activation(attn_e[:, c, 0:(t + 1) * P], attn_e[:, c, 0:(t + 1) * P], ACT.Exp,
                                             bias=small[:, 52 + c:53 + c], scale=HD ** -0.5, accum_out=small[:, 54 + c:55 + c]))
                    act.nop().then_inc(prob_ready, 1)
                    act.wait_ge(wT_done, n + 1)
                    act.activation(attn_wT[:, 0:t + 1, :], ps[:, 7, 0:(t + 1) * P].rearrange("p (k s) -> p k s", s=P), ACT.Copy)\
                       .then_inc(wT_out, 1)
                    act.wait_ge(o_done, n + 1)
                    act.activation(attn_o[:, t, h * P:(h + 1) * P], ps[:, 7, 2 * P:3 * P], ACT.Copy).then_inc(o_out, 1)
                    if n % 2 == 1:
                        chunk(8 + n // 2)
                root(1, small[:, 64:72], 2)
                act.wait_ge(oT_done, 1)
                after(act.activation(qT[:, :, :], ps[:, 6:8, :].rearrange("p b (k s) -> p (b k) s", s=SEQ), ACT.Copy,
                                     scale=small[:, 84:85]))
                act.nop().then_inc(oT_out, 1)
                act.wait_ge(z_in, 1)
                after(act.activation(zT[:, :, :], zT[:, :, :], ACT.Gelu_apprx_tanh))
                act.nop().then_inc(z_out, 1)
                used_in_mixer(act, 29, l, p0)
                for m in range(KW):
                    after(act.activation(work[:, 0, m * SEQ:(m + 1) * SEQ], ps[:, 4 + m // 2, (m % 2) * SEQ:(m % 2 + 1) * SEQ],
                                         ACT.Sigmoid, bias=col[:, R_GLUB + m:R_GLUB + m + 1]))
                act.nop().then_inc(glu_out, 1)
                act.wait_ge(m_turned, 1)
                for b in range(4):
                    after(act.activation(xT[:, 2 * b:2 * b + 2, :].rearrange("p k s -> p (k s)"), ps[:, b, :], ACT.Copy))
                act.nop().then_inc(m_copied, 1)

                act.wait_ge(res_read, 1)
                squares()
                root(2, small[:, 2:4], 3)
                turn_out(2, R_FFNG)
                act.wait_ge(fn_asked, 5)
                act.activation(ro[:, 1, :, 0:4], ro[:, 1, :, 0:4], ACT.Exp).then_inc(fn_served, 1)
                act.wait_ge(fn_asked, 6)
                act.activation(small[:, 80:82], small[:, 80:82], ACT.Exp).then_inc(fn_served, 1)

                act.wait_ge(passes_act, 1)
                act.sem_clear(passes_act)
                p1 = act.value_load(passes[0:1, 0:1], min_val=0, max_val=MAX_PASSES * DEPTH)

                def gathered(n):
                    act.wait_ge(gather_done, n)
                    for k in range(KD):
                        ins = act.activation(xe[:, k, :], ps[:, 4 + k // 4, (k % 4) * P:(k % 4 + 1) * P], ACT.Copy,
                                             scale=col[:, R_FFNG + k:R_FFNG + k + 1])
                    ins.then_inc(xe_out, 1)

                gathered((l + 1) + p0 * PAIRS)
                with act.Fori(p0, p1) as p:
                    with act.Fori(0, PAIRS) as i:
                        g = p * PAIRS + i
                        used_in_pair(act, 3, l, g)
                        act.activation(sil, ps[:, 0, :], ACT.Silu).then_inc(silu_out, 1)
                        act.wait_ge(hT_done, g + 1)
                        act.activation(hT[:, :, :], ps[:, 6, :].rearrange("p (f s) -> p f s", f=4), ACT.Copy).then_inc(hT_out, 1)
                        act.wait_ge(pgT_done, g + 1)
                        act.activation(pgT, ps[:, 7, 0:SEQ], ACT.Copy).then_inc(pgT_out, 1)
                        gathered(g + (l + 2))
                        used_in_pair(act, 11, l, g)
                        act.activation(ye.rearrange("p (h n) -> p h n", h=2), ps[:, 2:4, :], ACT.Copy).then_inc(ye_out, 1)
            act.wait_ge(final_in, 1)
            for t in range(TT):
                act.activation(work[:, 3, :], x[:, t, :], ACT.Square, accum_out=small[:, t:t + 1]).then_inc(final_out, 1)
                act.wait_ge(final_out, t + 1)
            act.wait_ge(final_in, 2)
            act.activation(small[:, 2:4], small[:, 2:4], ACT.Sqrt).then_inc(final_out, 1)

        @block.vector
        def _(dve):
            steps = [0]

            def after(ins):
                steps[0] += 1
                ins.then_inc(dve_step, 1)
                dve.wait_ge(dve_step, steps[0])

            def tt(o, i0, i1, op):
                after(dve.tensor_tensor(o, i0, i1, op))

            def tsc(o, i0, s1, s2, op0, op1=None):
                after(dve.tensor_scalar(o, i0, s1, s2, op0, op1) if op1 is not None
                      else dve.tensor_scalar(o, i0, s1, None, op0))

            def stt(o, i0, s, i1, op0, op1):
                after(dve.scalar_tensor_tensor(o, i0, s, i1, op0, op1))

            MUL, ADD, SUB, MAX, MIN, EQ = ALU.mult, ALU.add, ALU.subtract, ALU.max, ALU.min, ALU.is_equal

            def reduce_angle(th, kk, c):
                tsc(kk, th, INV_2PI, MAGIC, MUL, ADD)
                tsc(kk, kk, MAGIC, None, SUB)
                for part in (PI_2A, PI_2B, PI_2C):
                    stt(th, kk, -part, th, MUL, ADD)
                tsc(th, th, -PI, PI, MAX, MIN)
                stt(c, th, -1.0, th, MUL, MAX)
                tsc(c, c, -1.0, PI / 2, MUL, ADD)

            for v in (bnat, cdup, wa, wx):
                after(dve.memset(v[:], 0.0))
            after(dve.memset(xrT[:, :, 0:3], 0.0))
            after(dve.memset(ones[:, :], 1.0))
            after(dve.memset(passes_f[:, :], 0.0))
            after(dve.tensor_copy(passes[:, :], passes_f[:, :]))
            dve.nop().then_inc(zeroed, 1)
            dve.nop().then_inc(scat_read, 1)
            dve.nop().then_inc(scat_read, 1)
            dve.wait_ge(start_ready, 64)
            after(dve.tensor_copy(isreset[:, :], notreset[:, :].bitcast(I32)))
            tsc(isreset[:, :], isreset[:, :], 0.0, None, EQ)
            tsc(notreset[:, :], isreset[:, :], -1.0, None, ADD)
            after(dve.tensor_copy(small[:, 0:TT], pos_i[:, :]))
            for t in range(TT):
                tsc(rsn[:, t, :], cst[:, C_FREQ:C_FREQ + HALF], small[:, t:t + 1], None, MUL)
            kk = attn_w[:, 0:TT * HALF].rearrange("p (t e) -> p t e", t=TT)
            reduce_angle(rsn[:, :, :], kk, rc[:, :, :])
            dve.nop().then_inc(angle_ready, 1)
            dve.wait_ge(sine_ready, 2)

            with dve.Fori(0, DEPTH) as l:
                dve.wait_ge(arrive, 2)
                dve.sem_clear(arrive)
                for s in layer_sems:
                    dve.sem_clear(s)
                steps[0] = 0
                dve.nop().then_inc(release_pe, 1)
                dve.nop().then_inc(release_act, 1)

                p0 = dve.value_load(passes[0:1, 0:1], min_val=0, max_val=MAX_PASSES * DEPTH)

                dve.wait_ge(params_ready, (l + 1) * (16 * N_PARAMS))
                after(dve.tensor_copy(raw[0:16, :].rearrange("j (h n) -> j h n", h=2),
                                      ldt[:, :].unsqueeze(2).to_broadcast([16, 2, NS])))
                dve.nop().then_inc(raw_dt, 1)

                def normed(n):
                    dve.wait_ge(ss_ready, n)
                    tsc(small[:, 2:4], small[:, 0:2], 1.0 / D, 1e-6, MUL, ADD)
                    dve.nop().then_inc(var_ready, 1)
                    return small[:, 2:4]

                def scaled(m):
                    dve.wait_ge(root_ready, m)
                    after(dve.reciprocal(small[:, 4:6], small[:, 2:4]))
                    for t in range(TT):
                        tsc(stage[:, t, :], x[:, t, :], small[:, 4 + t:5 + t], None, MUL)
                    dve.nop().then_inc(xn_ready, 1)

                normed(1)
                scaled(1)

                dve.wait_ge(col_copied, 1)
                e = small[:, 20:40]
                tsc(small[:, 20:36], col[:, R_DT:R_DT + JT], 1 / 32, None, MUL)
                tsc(small[:, 40:44], col[:, R_LAM:R_LAM + KW], -1.0, None, MUL)
                tt(small[:, 36:40], small[:, 40:44], col[:, R_LAM:R_LAM + KW], MIN)
                tsc(small[:, 36:40], small[:, 36:40], 1 / 32, None, MUL)
                dve.nop().then_inc(fn_asked, 1)
                dve.wait_ge(fn_served, 1)
                den = small[:, 100:120]
                tsc(den, e, -1.0, 1.0, MUL, ADD)
                tsc(e, e, 1.0, None, ADD)
                after(dve.reciprocal(den, den))
                tt(e, e, den, MUL)
                for _ in range(4):
                    tt(e, e, e, MUL)
                dt = small[:, 20:36]
                lr, li = col[:, R_RE:R_RE + JT], col[:, R_IM:R_IM + JT]
                Q, MAG, SN, CS, AR, AI, CR, CI, T0, T1, T2 = (s5[:, n, :] for n in (0, 1, 3, 4, 5, 6, 7, 8, 9, 10, 11))
                stt(Q, lr, -0.5, dt, MUL, MUL)
                dve.nop().then_inc(fn_asked, 1)
                for n in range(2):
                    tt(lamv[:, 2 * n, :], lamv[:, 2 * n, :], lamv[:, 2 * n + 1, :], MUL)
                    after(dve.tensor_reduce(small[:, 86 + n:87 + n], lamv[:, 2 * n, :], AX, ADD))
                dve.nop().then_inc(fn_asked, 1)
                tt(SN, li, dt, MUL)
                reduce_angle(SN, T0, CS)
                dve.nop().then_inc(fn_asked, 1)
                y4, z4, zz, po = small[:, 36:40], small[:, 120:124], small[:, 124:128], small[:, 128:132]
                tsc(zz, y4, 2.0, None, ADD)
                after(dve.reciprocal(zz, zz))
                tt(z4, y4, zz, MUL)
                tt(zz, z4, z4, MUL)
                tsc(po, zz, 1 / 19, 1 / 17, MUL, ADD)
                for n in (15, 13, 11, 9, 7, 5, 3, 1):
                    tt(po, po, zz, MUL)
                    tsc(po, po, 1 / n, None, ADD)
                stt(po, z4, 2.0, po, MUL, MUL)
                stt(po, small[:, 40:44], 0.0, po, MAX, ADD)
                tsc(small[:, 44:48], po, 4.0, None, MUL)
                dve.nop().then_inc(sp_ready, 1)
                tt(small[:, 84:85], col[:, R_SUB:R_SUB + 1], cst[:, ds(l + C_ONEM, 1)], MUL)
                dve.wait_ge(fn_served, 2)
                tsc(T0, Q, 1.0, None, ADD)
                after(dve.reciprocal(T0, T0))
                tsc(MAG, Q, -1.0, 1.0, MUL, ADD)
                tt(MAG, MAG, T0, MUL)
                dve.wait_ge(fn_served, 3)
                tt(small[:, 88:89], small[:, 87:88], small[:, 86:87], SUB)
                tt(small[:, 88:89], small[:, 88:89], cst[:, ds(l + C_LINIT, 1)], SUB)
                dve.wait_ge(fn_served, 4)
                tt(AR, MAG, CS, MUL)
                tt(AI, MAG, SN, MUL)
                tt(T0, lr, lr, MUL)
                tt(T1, li, li, MUL)
                tt(T0, T0, T1, ADD)
                after(dve.reciprocal(T0, T0))
                tsc(T2, AR, -1.0, None, ADD)
                tt(CR, T2, lr, MUL)
                tt(T1, AI, li, MUL)
                tt(CR, CR, T1, ADD)
                tt(CR, CR, T0, MUL)
                tt(CI, AI, lr, MUL)
                tt(T1, T2, li, MUL)
                tt(CI, CI, T1, SUB)
                tt(CI, CI, T0, MUL)
                dve.wait_ge(c_copied, 1)
                cre = work[:, 0, 0:512].rearrange("p (j c) -> p j c", j=JT)
                cim = work[:, 0, 512:1024].rearrange("p (j c) -> p j c", j=JT)
                crb, cib = (v.unsqueeze(2).to_broadcast([P, JT, 32]) for v in (CR, CI))
                c0, c1, c2 = (ccoef[:, n, :, :] for n in range(3))
                tt(c0, cre, crb, MUL)
                tt(c1, cim, cib, MUL)
                tt(c0, c0, c1, SUB)
                tt(c2, cre, cib, MUL)
                tt(c1, cim, crb, MUL)
                stt(c2, c2, -1.0, c1, MUL, SUB)
                tsc(c1, c0, -1.0, None, MUL)
                after(dve.tensor_copy(pre[:, :, 0, 0], CS))
                after(dve.tensor_copy(pre[:, :, 0, 1], SN))
                for n in range(7):
                    re, im = pre[:, :, n, 0], pre[:, :, n, 1]
                    tt(T0, re, re, MUL)
                    tt(T1, im, im, MUL)
                    tt(pre[:, :, n + 1, 0], T0, T1, SUB)
                    stt(pre[:, :, n + 1, 1], re, 2.0, im, MUL, MUL)

                def double(tc, tsn, n, power, t0, t1, j0, nj):
                    er = pre[:, j0:j0 + nj, power, 0].unsqueeze(2).to_broadcast([P, nj, n])
                    ei = pre[:, j0:j0 + nj, power, 1].unsqueeze(2).to_broadcast([P, nj, n])
                    c, s = tc[:, :, 0:n], tsn[:, :, 0:n]
                    tt(t0, c, er, MUL)
                    tt(t1, s, ei, MUL)
                    tt(tc[:, :, n:2 * n], t0, t1, SUB)
                    tt(t0, c, ei, MUL)
                    tt(t1, s, er, MUL)
                    tt(tsn[:, :, n:2 * n], t0, t1, ADD)

                after(dve.memset(bcos[:, :, 0:1], 1.0))
                after(dve.memset(bsin[:, :, 0:1], 0.0))
                flat = [w.rearrange("p a b -> p (a b)") for w in (tcos[:, :, :], tsin[:, :, :])]
                for n in range(5):
                    t0, t1 = (w[:, 0:JT << n].rearrange("p (j n) -> p j n", j=JT) for w in flat)
                    double(bcos[:, :, :], bsin[:, :, :], 1 << n, n, t0, t1, 0, JT)

                dve.wait_ge(turn_copied, 2)
                for k in range(KW):
                    xc = work[:, 0, k * SEQ:(k + 1) * SEQ]
                    tsc(xc, xrT[:, k, 3:3 + SEQ], col[:, R_CW + k:R_CW + k + 1], col[:, R_CB + k:R_CB + k + 1], MUL, ADD)
                    for j in range(1, 4):
                        c = R_CW + 4 * j + k
                        stt(xc, xrT[:, k, 3 - j:3 - j + SEQ], col[:, c:c + 1], xc, MUL, ADD)
                dve.nop().then_inc(conv_ready, 1)

                dve.wait_ge(chunk_out, 5)
                for t in range(TT):
                    xx = qkv[:, t, 0:2 * W].rearrange("p (h c e) -> p h c e", c=2, e=HALF)
                    t0, t1 = (w.rearrange("p (h c e) -> p h c e", c=2, e=HALF) for w in flat)
                    cb, sbc = (v[:, t, :].unsqueeze(1).unsqueeze(1).to_broadcast([P, 4 * HEADS, 2, HALF]) for v in (rc, rsn))
                    tt(t0, xx, cb, MUL)
                    tt(t1, xx, sbc, MUL)
                    tt(xx[:, :, 0, :], t0[:, :, 0, :], t1[:, :, 1, :], SUB)
                    tt(xx[:, :, 1, :], t0[:, :, 1, :], t1[:, :, 0, :], ADD)
                dve.nop().then_inc(rope_ready, 1)

                dve.wait_ge(rg_root, 1)
                z = zT[:, :, :].rearrange("p k s -> p (k s)")
                def kws(v):
                    return v.rearrange("p (k s) -> p k s", k=KW)
                nrb = notreset[:, :].unsqueeze(1).to_broadcast([P, KW, SEQ])
                rsb = isreset[:, :].unsqueeze(1).to_broadcast([P, KW, SEQ])
                tsc(z, work[:, 1, :], 1.0, None, ADD)
                after(dve.reciprocal(z, z))
                stt(work[:, 1, :], work[:, 1, :], -1.0, z, ADD, MUL)
                tt(kws(work[:, 1, :]), kws(work[:, 1, :]), nrb, MUL)
                stt(work[:, 3, :], work[:, 3, :], -2.0, z, MUL, MUL)
                tt(kws(work[:, 3, :]), kws(work[:, 3, :]), nrb, MUL)
                tt(kws(work[:, 3, :]), kws(work[:, 3, :]), rsb, ADD)
                tt(work[:, 2, :], work[:, 2, :], work[:, 0, :], MUL)
                tt(work[:, 3, :], work[:, 3, :], work[:, 2, :], MUL)
                for k in range(KW):
                    r = slice(k * SEQ, (k + 1) * SEQ)
                    after(dve.tensor_tensor_scan(work[:, 0, r], work[:, 1, r], work[:, 3, r], 0.0, MUL, ADD))
                dve.wait_ge(gelu_g, 1)
                g = grT[:, :, :].rearrange("p k s -> p (k s)")
                tt(g, g, work[:, 0, :], MUL)
                dve.nop().then_inc(yrnn_ready, 1)

                mask = cst[:, C_MASK:C_MASK + P]
                for n in range(2 * HEADS):
                    t = n % TT
                    dve.wait_ge(score_done, n + 1)
                    sc = ps[:, 5:7, 0:SEQ]
                    if t == 1:
                        after(dve.tensor_copy(attn_e[:, :, 0:P], sc[:, :, 0:P]))
                    tt(attn_e[:, :, t * P:(t + 1) * P], sc[:, :, t * P:(t + 1) * P],
                       mask.unsqueeze(1).to_broadcast([P, 2, P]), ADD)
                    dve.nop().then_inc(scores_read, 1)
                    after(dve.tensor_reduce(small[:, 52:54], attn_e[:, :, 0:(t + 1) * P], AX, MAX))
                    tsc(small[:, 52:54], small[:, 52:54], -HD ** -0.5, None, MUL)
                    dve.nop().then_inc(prob_in, 1)
                    dve.wait_ge(prob_ready, n + 1)
                    after(dve.reciprocal(small[:, 56:58], small[:, 54:56]))
                    tt(small[:, 57:58], small[:, 57:58], small[:, 88:89], MUL)
                    if n >= 1:
                        dve.wait_ge(wT_done, n)
                    w = attn_w[:, 0:(t + 1) * P]
                    tsc(w, attn_e[:, 0, 0:(t + 1) * P], small[:, 56:57], None, MUL)
                    stt(w, attn_e[:, 1, 0:(t + 1) * P], small[:, 57:58], w, MUL, ADD)
                    dve.nop().then_inc(w_ready, 1)
                dve.wait_ge(o_out, 2 * HEADS)
                o8 = attn_o[:, :, :].rearrange("p t (h v) -> p (t h) v", v=P)
                sq = work[:, 1, :].rearrange("p (g v) -> p g v", v=P)
                tt(sq, o8, o8, MUL)
                after(dve.tensor_reduce(small[:, 64:72], sq, AX, ADD))
                tsc(small[:, 64:72], small[:, 64:72], 1.0 / P, 1e-5, MUL, ADD)
                dve.nop().then_inc(var_ready, 1)
                dve.wait_ge(root_ready, 2)
                after(dve.reciprocal(small[:, 72:80], small[:, 64:72]))
                tt(o8, o8, small[:, 72:80].unsqueeze(2).to_broadcast([P, TT * HEADS, P]), MUL)
                dve.nop().then_inc(o_normed, 1)

                def tables(k):
                    after(dve.tensor_copy(tcos[:, :, 0:32], bcos[:, 4 * k:4 * k + 4, :]))
                    after(dve.tensor_copy(tsin[:, :, 0:32], bsin[:, 4 * k:4 * k + 4, :]))
                    for n in (5, 6, 7):
                        t0, t1 = (kT[:, 2 * r:2 * r + 2, :].rearrange("p a s -> p (a s)")[:, 0:4 << n].rearrange("p (j n) -> p j n", j=4) for r in range(2))
                        double(tcos[:, :, :], tsin[:, :, :], 1 << n, n, t0, t1, 4 * k, 4)

                def turn_in(m):
                    q = 2 * (m % 2)
                    dve.wait_ge(bu_done, m + 1)
                    pr, pi = ps[:, 4:6, 0:SEQ], ps[:, 4:6, SEQ:2 * SEQ]
                    c, s = tcos[:, q:q + 2, :], tsin[:, q:q + 2, :]
                    w = [work[:, n, q * SEQ:(q + 2) * SEQ].rearrange("p (j s) -> p j s", j=2) for n in range(4)]
                    tt(w[0], pr, c, MUL)
                    tt(w[1], pi, s, MUL)
                    tt(w[2], pi, c, MUL)
                    tt(w[3], pr, s, MUL)
                    dve.nop().then_inc(bu_read, 1)

                def recur(k):
                    tt(work[:, 0, :], work[:, 0, :], work[:, 1, :], ADD)
                    tt(work[:, 2, :], work[:, 2, :], work[:, 3, :], SUB)
                    for n in (0, 2):
                        for q in range(4):
                            r = slice(q * SEQ, (q + 1) * SEQ)
                            m = MAG[:, 4 * k + q:4 * k + q + 1].to_broadcast([P, SEQ])
                            after(dve.tensor_tensor_scan(work[:, n + 1, r], m, work[:, n, r], 0.0, MUL, ADD))
                    c, s = (v[:, :, :].rearrange("p j s -> p (j s)") for v in (tcos, tsin))
                    tt(work[:, 0, :], work[:, 1, :], c, MUL)
                    tt(work[:, 2, :], work[:, 1, :], s, MUL)
                    tt(work[:, 1, :], work[:, 3, :], s, MUL)
                    tt(work[:, 3, :], work[:, 3, :], c, MUL)
                    dve.nop().then_inc(s_ready, 1)

                def y_out(k):
                    dve.wait_ge(y_done, k + 1)
                    stt(zT[:, k, :], uT[:, k, :], col[:, R_D + k:R_D + k + 1], ps[:, 6, 0:SEQ], MUL, ADD)
                    dve.nop().then_inc(y_read, 1)

                def gated(n):
                    b, h = divmod(n, 2)
                    used_in_mixer(dve, (24, 26, 30)[b] + h, l, p0)
                    bank = 2 * (n % 2)
                    gt = gates[:, :, b * D + h * W:b * D + (h + 1) * W]
                    mg = stage[:, :, h * W:(h + 1) * W]
                    tt(mg if b == 0 else gt, ps[:, bank:bank + 2, :], gt, MUL)
                    if b:
                        tt(mg, mg, gt, ADD)
                    dve.nop().then_inc(proj_read, 1)

                dve.wait_ge(turn_copied, 3)
                tables(0)
                turn_in(0)
                gated(0)
                gated(1)
                turn_in(1)
                recur(0)
                gated(2)
                for k in range(1, 4):
                    tables(k)
                    y_out(k - 1)
                    turn_in(2 * k)
                    turn_in(2 * k + 1)
                    recur(k)
                    if k == 1:
                        gated(3)
                y_out(3)
                dve.nop().then_inc(z_in, 1)
                dve.wait_ge(glu_out, 1)
                tt(uT[:, :, :], zT[:, :, :], kws(work[:, 0, :]), MUL)
                dve.nop().then_inc(yssm_ready, 1)
                gated(4)
                gated(5)
                for h in range(2):
                    used_in_mixer(dve, 33 + 2 * h, l, p0)
                    tt(x[:, :, h * W:(h + 1) * W], ps[:, 2 * h:2 * h + 2, :], x[:, :, h * W:(h + 1) * W], ADD)
                dve.nop().then_inc(res_read, 1)

                normed(2)
                scaled(3)
                after(dve.memset(ye, 0.0))
                after(dve.memset(pgT, 0.0))
                dve.nop().then_inc(blank_pair, 1)
                dve.wait_ge(logit_done, 1)
                tt(lg[:, :, :], ps[:, 6, 0:2 * 64].rearrange("p (t n) -> p t n", t=TT)[:, :, 0:36],
                   rbias[:, :].unsqueeze(1).to_broadcast([P, TT, 36]), ADD)
                coarse, fine = lg[:, :, 0:4], lg[:, :, 4:36]
                m2, m3 = small[:, 90:92], small[:, 92:94]

                def first_of_max(oh, v, n, io):
                    after(dve.tensor_reduce(m2, v, AX, MAX))
                    tt(oh, v, m2.unsqueeze(2).to_broadcast([P, TT, n]), EQ)
                    stt(oh, oh, -64.0, io, MUL, ADD)
                    after(dve.tensor_reduce(m3, oh, AX, MIN))
                    tsc(m3, m3, 64.0, None, ADD)
                    tt(oh, io, m3.unsqueeze(2).to_broadcast([P, TT, n]), EQ)

                io32 = cst[:, C_I32:C_I32 + NEXP].unsqueeze(1).to_broadcast([P, TT, NEXP])
                io4 = cst[:, C_I32:C_I32 + 4].unsqueeze(1).to_broadcast([P, TT, 4])
                goh = ro[:, 2, :, 0:4]
                first_of_max(goh, coarse, 4, io4)
                tt(ro[:, 1, :, 0:4], coarse, m2.unsqueeze(2).to_broadcast([P, TT, 4]), SUB)
                dve.nop().then_inc(fn_asked, 1)
                pen = ro[:, 3, :, 0:4]
                tsc(pen, goh, 1e30, -1e30, MUL, ADD)
                fm = ro[:, 4, :, :]
                fm4, fine4 = (v.rearrange("p t (g e) -> p t g e", g=4) for v in (fm, fine))
                for t in range(TT):
                    tt(fm4[:, t], fine4[:, t], goh[:, t].unsqueeze(2).to_broadcast([P, 4, 8]), MUL)
                    tt(fm4[:, t], fm4[:, t], pen[:, t].unsqueeze(2).to_broadcast([P, 4, 8]), ADD)
                dve.wait_ge(fn_served, 5)
                psel = small[:, 94:96]
                after(dve.tensor_reduce(psel, ro[:, 1, :, 0:4], AX, ADD))
                after(dve.reciprocal(psel, psel))
                oh1, oh2 = ro[:, 5, :, :], ro[:, 1, :, :]
                first_of_max(oh1, fm, NEXP, io32)
                after(dve.tensor_copy(small[:, 82:84], m2))
                stt(fm, oh1, -2e30, fm, MUL, ADD)
                first_of_max(oh2, fm, NEXP, io32)
                sel = ro[:, 0, :, :]
                tt(sel, oh1, oh2, ADD)
                dve.nop().then_inc(sel_ready, 1)
                e2 = small[:, 80:82]
                tt(e2, m2, small[:, 82:84], SUB)
                dve.nop().then_inc(fn_asked, 1)
                dve.wait_ge(fn_served, 6)
                w1s, w2s = small[:, 96:98], small[:, 98:100]
                tsc(w1s, e2, 1.0, None, ADD)
                after(dve.reciprocal(w1s, w1s))
                tt(w1s, w1s, psel, MUL)
                tt(w2s, w1s, e2, MUL)
                gt = gate[:, :, 0:NEXP]
                tt(gt, oh1, w1s.unsqueeze(2).to_broadcast([P, TT, NEXP]), MUL)
                tt(oh2, oh2, w2s.unsqueeze(2).to_broadcast([P, TT, NEXP]), MUL)
                tt(gt, gt, oh2, ADD)
                after(dve.tensor_copy(gate[:, :, NEXP:], gate[:, :, 0:2]))
                dve.wait_ge(cum_done, 1)
                rk = rank[:, :, 0:NEXP]
                stt(rk, ps[:, 7, 0:64].rearrange("p (t n) -> p t n", t=TT), 1.0, sel, ADD, MUL)
                tsc(rk, rk, -1.0, None, ADD)
                tsc(rank[:, :, NEXP:], rank[:, :, 0:2], -float(SLOTS), None, ADD)
                top = small[:, 132:133]
                after(dve.tensor_reduce(top, ps[:, 7, 64:96], AX, MAX))
                for n in range(1, MAX_PASSES):
                    tsc(small[:, 133:134], top, float(n * SLOTS), None, ALU.is_gt)
                    tt(passes_f[:, :], passes_f[:, :], small[:, 133:134], ADD)
                tsc(passes_f[:, :], passes_f[:, :], 1.0, None, ADD)
                after(dve.tensor_copy(passes[:, :], passes_f[:, :]))
                for s in (passes_pe, passes_act, passes_sp):
                    dve.nop().then_inc(s, 1)
                p1 = dve.value_load(passes[0:1, 0:1], min_val=0, max_val=MAX_PASSES * DEPTH)

                io64 = cst[:, C_I64:C_I64 + SLOTS]

                def one_hots(e0):
                    for e in range(2):
                        for t in range(TT):
                            ins = dve.tensor_scalar(onehot[:, t, e * SLOTS:(e + 1) * SLOTS], io64,
                                                    rank[:, t, ds(e0 + e, 1)], None, EQ)
                    return ins

                def weigh(e0):
                    for e in range(2):
                        for t in range(TT):
                            ins = dve.tensor_scalar(weighted[:, t, e * SLOTS:(e + 1) * SLOTS], io64,
                                                    rank[:, t, ds(e0 + e, 1)], gate[:, t, ds(e0 + e, 1)], EQ, MUL)
                    return ins

                one_hots(0).then_inc(onehot_ready, 1)
                weigh(0).then_inc(weighted_ready, 1)
                with dve.Fori(p0, p1) as p:
                    with dve.Fori(0, PAIRS) as i:
                        g = p * PAIRS + i
                        dve.wait_ge(gather_done, g + (l + 1))
                        one_hots(i * 2 + 2).then_inc(onehot_ready, 1)
                        dve.wait_ge(silu_out, g + 1)
                        used_in_pair(dve, 7, l, g)
                        dve.tensor_tensor(hid, ps[:, 1, :], sil, MUL).then_inc(hid_ready, 1)
                        for n in range(2 * TT):
                            h, t = divmod(n, TT)
                            dve.wait_ge(scat_done, (g + l) * (2 * TT) + n + 1)
                            xh = x[:, t, h * W:(h + 1) * W]
                            dve.tensor_tensor(xh, ps[:, 7 - n % 2, :], xh, ADD).then_inc(scat_read, 1)
                        dve.wait_ge(pgT_done, g + 1)
                        weigh(i * 2 + 2).then_inc(weighted_ready, 1)
                        dve.wait_ge(weighted_ready, g + (l + 2))
                        dve.wait_ge(onehot_ready, g + (l + 2))
                        rn = rank[:, :, ds(i * 2 + 2, 2)]
                        dve.tensor_scalar(rn, rn, -float(SLOTS), None, ADD).then_inc(rank_moved, 1)
                        dve.wait_ge(rank_moved, g + 1)
                for n in range(2 * TT):
                    h, t = divmod(n, TT)
                    dve.wait_ge(scat_done, (p1 * PAIRS + l) * (2 * TT) + n + 1)
                    xh = x[:, t, h * W:(h + 1) * W]
                    dve.tensor_tensor(xh, ps[:, 7 - n % 2, :], xh, ADD).then_inc(scat_read, 1)
                dve.wait_ge(scat_read, (p1 * PAIRS + l + 1) * (2 * TT) + 2)
                dve.nop().then_inc(layer_out, 1)

            done = steps[0]
            after(dve.tensor_copy(small[:, 90:91], ones[:, 0:1]))
            dve.nop().then_inc(final_in, 1)
            dve.wait_ge(final_out, 2)
            tsc(small[:, 2:4], small[:, 0:2], 1.0 / D, 1e-6, MUL, ADD)
            dve.nop().then_inc(final_in, 1)
            dve.wait_ge(final_out, 3)
            after(dve.reciprocal(small[:, 4:6], small[:, 2:4]))
            dve.wait_ge(final_g_ready, 16)
            for t in range(TT):
                stt(stage[:, t, :], x[:, t, :], small[:, 4 + t:5 + t], gates[:, 0, 0:D], MUL, MUL)
            dve.nop().then_inc(out_ready, 1)


def constants():
    import math

    import numpy as np
    c = np.zeros((P, C_COLS), np.float32)
    r = np.arange(P)
    c[:, C_ID:C_ID + P] = np.eye(P)
    c[:, C_TRI:C_TRI + P] = r[:, None] < r[None, :]
    c[:, C_MASK:C_MASK + P] = np.where(r[None, :] <= r[:, None], 0.0, -1e30 * HD ** 0.5)
    c[:, C_I64:C_I64 + SLOTS] = np.arange(SLOTS)
    c[:, C_I32:C_I32 + NEXP] = np.arange(NEXP)
    c[:, C_FREQ:C_FREQ + HALF] = np.float32(10000.0) ** (-np.arange(0, HD, 2, dtype=np.float32) / np.float32(HD))
    for n in range(DEPTH):
        init = 0.8 - 0.6 * math.exp(-0.3 * n)
        c[:, C_LINIT + n] = init
        c[:, C_ONEM + n] = 1.0 - init
    return c


def kernel(**inputs):
    import numpy as _np
    import concourse.bacc as _bacc
    from concourse import mybir as _mybir
    from concourse.bass_utils import run_bass_kernel_spmd as _run

    nc = _bacc.Bacc("TRN2", target_bir_lowering=False, num_devices=1)
    arrays, aps = {}, {}
    for name, v in inputs.items():
        v = _np.ascontiguousarray(v)
        if v.ndim == 1:
            v = v.reshape(1, -1)
        arrays["in_" + name] = v
        aps[name] = nc.dram_tensor("in_" + name, v.shape, _mybir.dt.from_np(v.dtype), kind="ExternalInput").ap()
    arrays["consts"] = constants()
    consts = nc.dram_tensor("consts", (P, C_COLS), F32, kind="ExternalInput").ap()
    out = nc.dram_tensor("result", (1, SEQ, D), F32, kind="ExternalOutput").ap()
    hybrid_kernel(nc, aps, consts, out)
    return _run(nc, [arrays], core_ids=[0]).results[0]["result"]
```

```python
from contextlib import ExitStack

import concourse.bass as bass
from concourse import mybir

F32 = mybir.dt.float32
I32 = mybir.dt.int32
ALU = mybir.AluOpType
ACT = mybir.ActivationFunctionType
AX = mybir.AxisListType.X
ds = bass.ds

P = 128
DEPTH = 2
D = 1024
KD = D // P
SEQ = 256
TT = SEQ // P
W = 512
KW = W // P
GATE0 = 6 * W
HEADS = 4
HD = 64
HALF = HD // 2
JT = 16
NS = 64
GI = 16
NEXP = 32
PAIRS = NEXP // 2
SLOTS = 64
FF = 512
MAX_PASSES = SEQ // SLOTS

UNITS = 6
PAIR_UNITS = 12
UNIT = 2048
MIX_UNITS = 36
MIX_FILLS = MIX_UNITS // UNITS

C_ID, C_TRI, C_MASK, C_I64, C_I32, C_FREQ, C_LINIT, C_ONEM = 0, 128, 256, 384, 448, 480, 512, 514
C_COLS = 516

R_DT, R_RE, R_IM, R_MIXG, R_FFNG, R_CW, R_CB, R_BA, R_BX, R_LAM, R_D, R_GLUB, R_SUB = (
    0, 16, 32, 48, 56, 64, 80, 84, 88, 92, 96, 100, 104)
R_ROWS = 105
LATE = 8
PROJ_UNIT, GLU_UNIT, OUT_UNIT = (24, 28, 30), 26, 32

PARAM_ROWS = (
    (R_MIXG, "mix_norm_g", 8), (R_RE, "ssm_lambda_re", 16), (R_IM, "ssm_lambda_im", 16), (R_FFNG, "ffn_norm_g", 8),
    (R_CW, "conv_w", 16), (R_CB, "conv_b", 4), (R_BA, "rg_ba", 4), (R_BX, "rg_bx", 4), (R_LAM, "rg_lambda", 4),
    (R_D, "ssm_d", 4), (R_GLUB, "ssm_glu_b", 4), (R_SUB, "subln_g", 1))
N_ROWS = 1 + len(PARAM_ROWS)
N_PARAMS = 32

A_SMALL = 52, 136

MAGIC = 12582912.0
INV_2PI = 0.15915494309189535
PI = 3.141592502593994
PI_2A, PI_2B, PI_2C = 6.28125, 0.0019350051879882812, 3.0199159819567e-07


def mixer_units():
    units = []
    for c in (0, 5, 1, 2, 3, 4):
        units += [("in", c * W, kh) for kh in range(2)]
    for c in range(6):
        units += [("in", GATE0 + c * W, kh) for kh in range(2)]
    units += [("proj", 0, h) for h in range(2)]
    units += [("glu", 0, 0), ("glu", 1, 0)]
    units += [("proj", b, h) for b in (1, 2) for h in range(2)]
    units += [("out", h, kh) for h in range(2) for kh in range(2)]
    assert len(units) == MIX_UNITS
    return units


def hybrid_kernel(nc, a, consts, out):
    ctx = ExitStack()
    with ctx:
        def sb(name, shape, dt=F32):
            return ctx.enter_context(nc.sbuf_tensor(name, shape, dt))

        def sem(name):
            return ctx.enter_context(nc.semaphore(name))

        ring = sb("ring", [P, UNITS, UNIT])
        cst = sb("cst", [P, C_COLS])
        x = sb("x", [P, TT, D])
        xT = sb("xT", [P, KD, SEQ])
        stage = sb("stage", [P, TT, D])
        arena = sb("arena", [P, PAIR_UNITS - UNITS, UNIT])
        flat_arena = arena[:, :, :].rearrange("p u n -> p (u n)")
        gates = flat_arena[:, 0:3 * D * TT].rearrange("p (t n) -> p t n", t=TT)
        qkv = flat_arena[:, 6144:6144 + 3 * W * TT].rearrange("p (t n) -> p t n", t=TT)
        xrT = sb("xrT", [P, KW, SEQ + 3])
        grT = flat_arena[:, 9216:9216 + KW * SEQ].rearrange("p (k s) -> p k s", k=KW)
        uT = flat_arena[:, 10240:10240 + KW * SEQ].rearrange("p (k s) -> p k s", k=KW)
        zT = flat_arena[:, 11264:11264 + KW * SEQ].rearrange("p (k s) -> p k s", k=KW)
        qT = sb("qT", [P, HEADS, SEQ])
        kT = sb("kT", [P, HEADS, SEQ])
        work = sb("work", [P, 4, 4 * SEQ])
        tcos = sb("tcos", [P, 4, SEQ])
        tsin = sb("tsin", [P, 4, SEQ])
        bcos = sb("bcos", [P, JT, 32])
        bsin = sb("bsin", [P, JT, 32])
        attn_e = sb("attn_e", [P, 2, 2, SEQ])
        attn_w = sb("attn_w", [P, SEQ])
        attn_wT = sb("attn_wT", [P, 2, P])
        attn_o = sb("attn_o", [P, TT, W])
        raw = sb("raw", [P, P])
        ldt = sb("ldt", [16, 2])
        col = sb("col", [P, P])
        lamv = sb("lamv", [P, 4, HD])
        rbias = sb("rbias", [P, 36])
        rw = sb("rw", [P, KD, 36])
        wa = sb("wa", [P, KW, P])
        wx = sb("wx", [P, KW, P])
        bnat = sb("bnat", [P, 2, JT, 2 * GI])
        bmat = sb("bmat", [P, 2, KW, P])
        cdup = sb("cdup", [P, 2, KW, P])
        ccoef = sb("ccoef", [P, 3, JT, 2 * GI])
        s5 = sb("s5", [P, 24, JT])
        pre = sb("pre", [P, JT, 8, 2])
        rc = sb("rc", [P, TT, HALF])
        rsn = sb("rsn", [P, TT, HALF])
        notreset = sb("notreset", [P, SEQ])
        small = sb("small", [P, 160])
        lg = sb("lg", [P, TT, 36])
        ro = sb("ro", [P, 6, TT, NEXP])
        rank = sb("rank", [P, TT, NEXP + 2])
        gate = sb("gate", [P, TT, NEXP + 2])
        passes = sb("passes", [P, 1], I32)
        passes_f = sb("passes_f", [P, 1])
        ones = sb("ones", [P, P])
        pos_i = sb("pos_i", [P, TT], I32)
        isreset = sb("isreset", [P, SEQ])
        ps = ctx.enter_context(nc.psum_tensor("ps", [P, 8, 512], F32))

        ident = cst[:, C_ID:C_ID + P]
        xe = work[:, 0, :].rearrange("p (k s) -> p k s", k=KD)
        ye = work[:, 1, :]
        hid = work[:, 2, 0:FF]
        sil = work[:, 2, FF:2 * FF]
        hT = work[:, 3, 0:FF].rearrange("p (f s) -> p f s", f=4)
        pgT = work[:, 3, FF:FF + SEQ]
        onehot = attn_o[:, :, 0:P]
        weighted = attn_o[:, :, P:2 * P]

        ring_ready = [sem(f"ring_ready{i}") for i in range(PAIR_UNITS)]
        unit_used = [sem(f"unit_used{i}") for i in range(PAIR_UNITS)]
        rows_ready, params_ready = sem("rows_ready"), sem("params_ready")
        arena_free = sem("arena_free")
        fill_paced = sem("fill_paced")
        start_ready = sem("start_ready")
        zeroed = sem("zeroed")
        out_ready = sem("out_ready")
        stored = sem("stored")
        layer_sems = []

        def lsem(name):
            s = sem(name)
            layer_sems.append(s)
            return s

        arrive = sem("arrive")
        release_pe, release_act = sem("release_pe"), sem("release_act")
        dve_step, act_step = lsem("dve_step"), lsem("act_step")
        dve_moe_step, act_moe_step = sem("dve_moe_step"), sem("act_moe_step")
        param_cols, col_copied = lsem("param_cols"), lsem("col_copied")
        raw_dt = lsem("raw_dt")
        b_turned, b_copied = lsem("b_turned"), lsem("b_copied")
        c_turned, c_copied = lsem("c_turned"), lsem("c_copied")
        ss_ready, var_ready, root_ready = lsem("ss_ready"), lsem("var_ready"), lsem("root_ready")
        xn_ready, xn_turned, xT_ready = lsem("xn_ready"), lsem("xn_turned"), lsem("xT_ready")
        chunk_out = lsem("chunk_out")
        late_done, late_out = lsem("late_done"), lsem("late_out")
        turned, turn_copied = lsem("turned"), lsem("turn_copied")
        fn_asked, fn_served = lsem("fn_asked"), lsem("fn_served")
        sp_ready = lsem("sp_ready")
        conv_ready, rgate_done, rgate_out = lsem("conv_ready"), lsem("rgate_done"), lsem("rgate_out")
        rg_root, gelu_g, yrnn_ready = lsem("rg_root"), lsem("gelu_g"), lsem("yrnn_ready")
        rope_ready = lsem("rope_ready")
        score_done, w_ready = lsem("score_done"), lsem("w_ready")
        prob_in, prob_ready = lsem("prob_in"), lsem("prob_ready")
        wT_done, wT_out, o_done, o_out = lsem("wT_done"), lsem("wT_out"), lsem("o_done"), lsem("o_out")
        o_normed, oT_done, oT_out = lsem("o_normed"), lsem("oT_done"), lsem("oT_out")
        bu_done, bu_read = lsem("bu_done"), lsem("bu_read")
        s_ready, y_done, y_read = lsem("s_ready"), lsem("y_done"), lsem("y_read")
        z_in, z_out, glu_out, yssm_ready = lsem("z_in"), lsem("z_out"), lsem("glu_out"), lsem("yssm_ready")
        proj_read = lsem("proj_read")
        m_turned, m_copied = lsem("m_turned"), lsem("m_copied")
        res_read = lsem("res_read")
        logit_done, sel_ready, cum_done = lsem("logit_done"), lsem("sel_ready"), lsem("cum_done")
        blank_pair = lsem("blank_pair")
        passes_pe, passes_act, passes_sp = sem("passes_pe"), sem("passes_act"), sem("passes_sp")
        silu_out, hid_ready = sem("silu_out"), sem("hid_ready")
        hT_done, hT_out = sem("hT_done"), sem("hT_out")
        pgT_done, pgT_out = sem("pgT_done"), sem("pgT_out")
        gather_done, xe_out, onehot_ready, weighted_ready = (
            sem("gather_done"), sem("xe_out"), sem("onehot_ready"), sem("weighted_ready"))
        ye_out = sem("ye_out")
        scat_done, scat_read = sem("scat_done"), sem("scat_read")
        rank_moved, layer_out, final_g_ready = sem("rank_moved"), sem("layer_out"), sem("final_g_ready")
        angle_ready, sine_ready = sem("angle_ready"), sem("sine_ready")
        final_in, final_out = sem("final_in"), sem("final_out")

        units = mixer_units()

        def unit(u):
            v = ring[:, u, :] if u < UNITS else arena[:, u - UNITS, :]
            return v.rearrange("p (k n) -> p k n", n=W)

        def mixer_fill(i, l, p0):
            return l * MIX_FILLS + p0 * PAIRS + i // UNITS

        def pair_fill(u, l, g):
            return (l + 1) * MIX_FILLS + g if u < UNITS else g

        def used_in_mixer(eng, i, l, p0):
            eng.wait_ge(unit_used[i % UNITS], mixer_fill(i, l, p0) + 2)

        def used_in_pair(eng, u, l, g):
            eng.wait_ge(unit_used[u], pair_fill(u, l, g) + 2)

        block = ctx.enter_context(nc.Block())

        @block.sync
        def _(sp):
            w_in = a["w_in"].rearrange("l (kh k p) n -> l kh p k n", kh=2, p=P)
            w_out = a["w_out"].rearrange("l (kh k p) n -> l kh p k n", kh=2, p=P)
            proj = [a[n].rearrange("l (k p) n -> l p k n", p=P) for n in ("proj_rnn", "proj_attn", "proj_ssm")]
            glu = a["ssm_glu_w"].rearrange("l (h k p) n -> l h p k n", h=2, p=P)
            w1 = a["expert_w1"].rearrange("l g e (kh k p) f -> (l g e) kh p k f", kh=2, p=P)
            w3 = a["expert_w3"].rearrange("l g e (kh k p) f -> (l g e) kh p k f", kh=2, p=P)
            w2 = a["expert_w2"].rearrange("l g e (k p) n -> (l g e) p k n", p=P)

            def one(ap, l):
                v = ap[ds(l, 1)]
                names = " ".join("bcdef"[:len(v.shape) - 1])
                return v.rearrange(f"a {names} -> (a {names.split()[0]}) {' '.join(names.split()[1:])}")

            sp.dma_start(cst[:, :], consts).then_inc(start_ready, 16)
            sp.dma_start(x[:, :, :], a["x"].rearrange("b (t p) d -> (b p) t d", p=P)).then_inc(start_ready, 16)
            with nc.allow_non_contiguous_dma(reason="one position per partition"):
                sp.dma_start(pos_i[:, :], a["positions"].rearrange("b (t p) -> (b p) t", p=P)).then_inc(start_ready, 16)
            sp.dma_start(notreset[:, :].bitcast(I32), a["positions"].to_broadcast([P, SEQ])).then_inc(start_ready, 16)
            sp.wait_ge(zeroed, 1)

            with sp.Fori(0, DEPTH) as l:
                p0 = sp.value_load(passes[0:1, 0:1], min_val=0, max_val=MAX_PASSES * DEPTH)

                loads = [0]

                def load(dst, src):
                    loads[0] += 1
                    sp.dma_start(dst, src).then_inc(params_ready, 16)

                def rows(r, name, n):
                    v = a[name][ds(l, 1)]
                    names = "b c d"[:2 * len(v.shape) - 3]
                    sp.dma_start(raw[r:r + n, :], v.rearrange(f"a {names} -> (a {names})").rearrange("(n p) -> n p", p=P))\
                      .then_inc(rows_ready, 16)

                def fill(u, before, src, paced=False):
                    sp.wait_ge(unit_used[u], before + 1)
                    if paced:
                        sp.sem_inc(fill_paced, 1)
                    src = src.rearrange("a p k n -> (a p) k n")
                    sp.dma_start(unit(u)[:, 0:src.shape[1], :], src).then_inc(ring_ready[u], 16)

                def mixer_units_from(first, end):
                    for i in range(first, end):
                        name, b, c = units[i]
                        if name == "in":
                            src = w_in[ds(l, 1), c, :, :, b:b + W]
                        elif name == "proj":
                            src = proj[b][ds(l, 1), :, :, c * W:(c + 1) * W]
                        elif name == "glu":
                            src = glu[ds(l, 1), b]
                        else:
                            src = w_out[ds(l, 1), c, :, :, b * W:(b + 1) * W]
                        fill(i % UNITS, mixer_fill(i, l, p0), src, paced=(i == 0))

                with nc.allow_non_contiguous_dma(reason="small parameters"):
                    sp.dma_start(ldt[:, :], a["ssm_log_dt"][ds(l, 1)].rearrange("a (j h) -> (a j) h", h=2)).then_inc(rows_ready, 16)
                    for row in PARAM_ROWS:
                        rows(*row)
                mixer_units_from(0, UNITS)
                with nc.allow_non_contiguous_dma(reason="small parameters"):
                    for n, name in enumerate(("ssm_b_re", "ssm_b_im")):
                        b = a[name][ds(l, 1)].rearrange("a (j h) n i -> (a h) n j i", h=2)
                        for h in range(2):
                            load(bnat[NS * h:NS * h + NS, n, :, GI * h:GI * h + GI], b[h])
                    for n, name in enumerate(("ssm_c_re", "ssm_c_im")):
                        c = a[name][ds(l, 1)].rearrange("a (k j h) i n -> (a j) h i k n", k=KW, h=2)
                        for j in range(4):
                            for h in range(2):
                                r = 32 * j + GI * h
                                load(cdup[r:r + GI, n, :, NS * h:NS * h + NS], c[j, h])
                    for t, name in ((wa, "rg_wa"), (wx, "rg_wx")):
                        g = a[name][ds(l, 1)].rearrange("a (k h) i j -> (a h) i k j", h=2)
                        for h in range(2):
                            load(t[64 * h:64 * h + 64, :, 64 * h:64 * h + 64], g[h])
                    for n, name in enumerate(("lam_q1", "lam_k1", "lam_q2", "lam_k2")):
                        load(lamv[:, n, :], a[name][ds(l, 1)].to_broadcast([P, HD]))
                    load(rbias[:, 0:4], a["router_coarse_b"][ds(l, 1)].to_broadcast([P, 4]))
                    load(rbias[:, 4:36], a["router_fine_b"][ds(l, 1)].to_broadcast([P, NEXP]))
                    load(rw[:, :, 0:4], a["router_coarse_w"][ds(l, 1)].rearrange("a (k p) n -> (a p) k n", p=P))
                    load(rw[:, :, 4:36], a["router_fine_w"][ds(l, 1)].rearrange("a (k p) n -> (a p) k n", p=P))
                assert loads[0] == N_PARAMS, loads[0]

                mixer_units_from(UNITS, MIX_UNITS)

                def fill_pair(p, i):
                    g = p * PAIRS + i
                    u = 0
                    for w in (w1, w3):
                        for kh in range(2):
                            for e in range(2):
                                if u == UNITS:
                                    sp.wait_ge(arena_free, l + 1)
                                    sp.sem_inc(fill_paced, 1)
                                fill(u, pair_fill(u, l, g), w[ds(l * NEXP + i * 2 + e, 1), kh])
                                u += 1
                    for h in range(2):
                        for e in range(2):
                            fill(u, pair_fill(u, l, g), w2[ds(l * NEXP + i * 2 + e, 1), :, :, h * W:(h + 1) * W])
                            u += 1

                with sp.Fori(0, PAIRS) as i:
                    fill_pair(p0, i)
                sp.wait_ge(passes_sp, 1)
                sp.sem_clear(passes_sp)
                p1 = sp.value_load(passes[0:1, 0:1], min_val=0, max_val=MAX_PASSES * DEPTH)
                with sp.If(p0 + 1 < p1):
                    with sp.Fori(p0 + 1, p1) as p:
                        with sp.Fori(0, PAIRS) as i:
                            fill_pair(p, i)

            sp.wait_ge(layer_out, DEPTH)
            sp.dma_start(gates[:, 0, 0:D], a["final_norm_g"].to_broadcast([P, D])).then_inc(final_g_ready, 16)
            sp.wait_ge(out_ready, 1)
            sp.dma_start(out.rearrange("b (t p) d -> (b p) t d", p=P), stage[:, :, :]).then_inc(stored, 16)
            sp.wait_ge(stored, 16)

        @block.tensor
        def _(pe):
            for u in range(PAIR_UNITS):
                pe.nop().then_inc(unit_used[u], 1)
            pe.wait_ge(start_ready, 64)
            pe.wait_ge(zeroed, 1)

            with pe.Fori(0, DEPTH) as l:
                p0 = pe.value_load(passes[0:1, 0:1], min_val=0, max_val=MAX_PASSES * DEPTH)
                pe.nop().then_inc(arrive, 1)
                pe.wait_ge(release_pe, 1)
                pe.sem_clear(release_pe)

                pe.wait_ge(raw_dt, 1)
                pe.transpose(ps[:, 6, 0:R_ROWS], raw[0:R_ROWS, :], ident[0:R_ROWS, 0:R_ROWS]).then_inc(param_cols, 1)

                def turn_x():
                    for k in range(KD):
                        for t in range(TT):
                            mm = pe.transpose(ps[:, k // 2, (k % 2) * SEQ + t * P:(k % 2) * SEQ + (t + 1) * P],
                                              stage[:, t, k * P:(k + 1) * P], ident)
                    return mm

                pe.wait_ge(xn_ready, 1)
                turn_x().then_inc(xn_turned, 1)

                def turn_bc():
                    pe.wait_ge(params_ready, (l + 1) * (16 * N_PARAMS))
                    for n in range(2):
                        for k in range(KW):
                            v = bnat[:, n, 4 * k:4 * k + 4, :].rearrange("p j c -> p (j c)")
                            mm = pe.transpose(ps[:, 4 + n, k * P:(k + 1) * P], v, ident)
                    mm.then_inc(b_turned, 1)
                    pe.wait_ge(col_copied, 1)
                    for n in range(2):
                        for k in range(KW):
                            mm = pe.transpose(ps[:, 6 + n, k * P:(k + 1) * P], cdup[:, n, k, :], ident)
                    mm.then_inc(c_turned, 1)

                def unit_ready(i):
                    pe.wait_ge(ring_ready[i % UNITS], (mixer_fill(i, l, p0) + 1) * 16)

                def in_part(c, kh, t):
                    i = 2 * c + kh
                    if t == 0:
                        if kh == 0 and c >= 2:
                            pe.wait_ge(chunk_out, c - 1)
                        unit_ready(i)
                    for k in range(4):
                        kk = 4 * kh + k
                        mm = pe.matmul(ps[:, 2 * (c % 2) + t, :], xT[:, kk, t * P:(t + 1) * P], unit(i % UNITS)[:, k, :],
                                       start=(kk == 0), stop=(kk == KD - 1))
                    if t == TT - 1:
                        mm.then_inc(unit_used[i % UNITS], 1)

                def in_half(c, kh):
                    for t in range(TT):
                        in_part(c, kh, t)

                def late_part(q):
                    j, kh = divmod(q, 2)
                    c, t = LATE + j // TT, j % TT
                    i = 2 * c + kh
                    if kh == 0:
                        if j < 2:
                            pe.wait_ge(chunk_out, LATE - 1)
                        else:
                            pe.wait_ge(late_out, j - 1)
                    unit_ready(i)
                    for k in range(4):
                        kk = 4 * kh + k
                        mm = pe.matmul(ps[:, j % 2, :], xT[:, kk, t * P:(t + 1) * P], unit(i % UNITS)[:, k, :],
                                       start=(kk == 0), stop=(kk == KD - 1))
                    if t == TT - 1:
                        mm.then_inc(unit_used[i % UNITS], 1)
                    elif kh == 1:
                        mm.then_inc(late_done, 1)

                def turn_chunk(n, src, wait_chunk):
                    pe.wait_ge(wait_chunk[0], wait_chunk[1])
                    if n >= 1:
                        pe.wait_ge(turn_copied, n)
                    for k in range(KW):
                        for t in range(TT):
                            mm = pe.transpose(ps[:, 6 + k // 2, (k % 2) * SEQ + t * P:(k % 2) * SEQ + (t + 1) * P],
                                              src(t, k), ident)
                    mm.then_inc(turned, 1)

                def staged(c):
                    return lambda t, k: stage[:, t, (c % 2) * W + k * P:(c % 2) * W + (k + 1) * P]

                def rgate(n, wt):
                    if n == 0:
                        pe.wait_ge(conv_ready, 1)
                        pe.wait_ge(turn_copied, 2)
                    else:
                        pe.wait_ge(rgate_out, 1)
                    for k in range(KW):
                        mm = pe.matmul(ps[:, 6 + k // 2, (k % 2) * SEQ:(k % 2 + 1) * SEQ], wt[:, k, :],
                                       work[:, 0, k * SEQ:(k + 1) * SEQ], start=True, stop=True)
                    mm.then_inc(rgate_done, 1)

                def scores(n):
                    h, t = divmod(n, TT)
                    if n == 0:
                        pe.wait_ge(turn_copied, 5)
                    else:
                        pe.wait_ge(prob_in, n)
                    for c in range(2):
                        mm = pe.matmul(ps[:, 6 + c, 0:(t + 1) * P], qT[64 * c:64 * c + 64, h, t * P:(t + 1) * P],
                                       kT[64 * c:64 * c + 64, h, 0:(t + 1) * P], start=True, stop=True)
                    mm.then_inc(score_done, 1)

                def turn_w(n):
                    h, t = divmod(n, TT)
                    if n == 0:
                        pe.wait_ge(chunk_out, LATE)
                    pe.wait_ge(w_ready, n + 1)
                    for k in range(t + 1):
                        mm = pe.transpose(ps[:, 2, k * P:(k + 1) * P], attn_w[:, k * P:(k + 1) * P], ident)
                    mm.then_inc(wT_done, 1)

                def attend(n):
                    h, t = divmod(n, TT)
                    pe.wait_ge(wT_out, n + 1)
                    if n >= 1:
                        pe.wait_ge(o_out, n)
                    for k in range(t + 1):
                        mm = pe.matmul(ps[:, 3, 0:P], attn_wT[:, k, :], qkv[:, k, 2 * W + h * P:2 * W + (h + 1) * P],
                                       start=(k == 0), stop=(k == t))
                    mm.then_inc(o_done, 1)

                def bu(m):
                    if m == 0:
                        pe.wait_ge(b_copied, 1)
                        pe.wait_ge(turn_copied, 2)
                    else:
                        pe.wait_ge(bu_read, m)
                    if m >= 2:
                        pe.wait_ge(y_read, m // 2)
                    for j in (2 * m, 2 * m + 1):
                        k, q = divmod(j, 4)
                        for n in range(2):
                            mm = pe.matmul(ps[:, 4 + j % 2, n * SEQ:(n + 1) * SEQ], bmat[32 * q:32 * q + 32, n, k, :],
                                           uT[32 * q:32 * q + 32, k, :], start=True, stop=True)
                    mm.then_inc(bu_done, 1)

                def cy(k):
                    pe.wait_ge(s_ready, k + 1)
                    for q in range(4):
                        j = 4 * k + q
                        for n, (cm, w) in enumerate(((0, 0), (1, 1), (2, 2), (2, 3))):
                            mm = pe.matmul(ps[32 * q:32 * q + 32, 4, 0:SEQ], ccoef[:, cm, j, :],
                                           work[:, w, q * SEQ:(q + 1) * SEQ], start=(n == 0), stop=(n == 3))
                    mm.then_inc(y_done, 1)

                def project(b, yT, halves):
                    for h in halves:
                        i = PROJ_UNIT[b] + h
                        n = 2 * b + h
                        if n == 0:
                            pe.wait_ge(late_out, 2 * HEADS)
                        if n == 1:
                            pe.wait_ge(o_out, 2 * HEADS)
                        if n >= 2:
                            pe.wait_ge(proj_read, n - 1)
                        unit_ready(i)
                        wt = unit(i % UNITS)
                        for t in range(TT):
                            for k in range(KW):
                                mm = pe.matmul(ps[:, 2 * (n % 2) + t, :], yT[:, k, t * P:(t + 1) * P], wt[:, k, :],
                                               start=(k == 0), stop=(k == KW - 1))
                        mm.then_inc(unit_used[i % UNITS], 1)

                pe.wait_ge(xT_ready, 1)
                in_half(0, 0)
                in_half(0, 1)
                turn_bc()
                in_half(1, 0)
                in_half(1, 1)
                pe.wait_ge(c_copied, 1)
                turn_chunk(0, staged(0), (chunk_out, 1))
                in_half(2, 0)
                turn_chunk(1, staged(1), (chunk_out, 2))
                in_half(2, 1)
                rgate(0, wa)
                in_half(3, 0)
                rgate(1, wx)
                bu(0)
                in_half(3, 1)
                pe.wait_ge(rgate_out, 2)
                turn_chunk(2, staged(2), (chunk_out, 3))
                in_half(4, 0)
                in_half(4, 1)
                in_half(5, 0)
                bu(1)
                in_half(5, 1)
                in_half(6, 0)
                cy(0)
                in_half(6, 1)
                turn_chunk(3, lambda t, k: qkv[:, t, k * P:(k + 1) * P], (rope_ready, 1))
                in_half(7, 0)
                turn_chunk(4, lambda t, k: qkv[:, t, W + k * P:W + (k + 1) * P], (rope_ready, 1))
                bu(2)
                in_part(7, 1, 0)
                bu(3)
                in_part(7, 1, 1)
                scores(0)
                late_part(0)
                cy(1)
                scores(1)
                between = {0: lambda: bu(4), 1: lambda: bu(5), 3: lambda: cy(2), 4: lambda: bu(6), 5: lambda: bu(7)}
                for n in range(2 * HEADS):
                    late_part(2 * n + 1)
                    turn_w(n)
                    if n + 2 < 2 * HEADS:
                        scores(n + 2)
                    if n in between:
                        between[n]()
                    if n + 1 < 2 * HEADS:
                        late_part(2 * n + 2)
                    attend(n)
                cy(3)
                pe.wait_ge(yrnn_ready, 1)
                project(0, grT, (0, 1))
                pe.wait_ge(z_out, 1)
                unit_ready(GLU_UNIT)
                unit_ready(GLU_UNIT + 1)
                for m in range(KW):
                    for k in range(KW):
                        u = (GLU_UNIT + k // 2) % UNITS
                        mm = pe.matmul(ps[:, 4 + m // 2, (m % 2) * SEQ:(m % 2 + 1) * SEQ],
                                       unit(u)[:, k % 2, m * P:(m + 1) * P], zT[:, k, :], start=(k == 0), stop=(k == KW - 1))
                        if m == KW - 1 and k % 2 == 1:
                            mm.then_inc(unit_used[u], 1)
                pe.wait_ge(o_normed, 1)
                for h in range(HEADS):
                    for t in range(TT):
                        mm = pe.transpose(ps[:, 6 + h // 2, (h % 2) * SEQ + t * P:(h % 2) * SEQ + (t + 1) * P],
                                          attn_o[:, t, h * P:(h + 1) * P], ident)
                mm.then_inc(oT_done, 1)
                pe.wait_ge(oT_out, 1)
                project(1, qT, (0, 1))
                pe.wait_ge(yssm_ready, 1)
                project(2, uT, (0, 1))
                pe.wait_ge(proj_read, 6)
                turn_x().then_inc(m_turned, 1)
                pe.wait_ge(m_copied, 1)
                for h in range(2):
                    for kh in range(2):
                        i = OUT_UNIT + 2 * h + kh
                        unit_ready(i)
                        wt = unit(i % UNITS)
                        for t in range(TT):
                            for k in range(4):
                                kk = 4 * kh + k
                                mm = pe.matmul(ps[:, 2 * h + t, :], xT[:, kk, t * P:(t + 1) * P], wt[:, k, :],
                                               start=(kk == 0), stop=(kk == KD - 1))
                        mm.then_inc(unit_used[i % UNITS], 1)

                pe.wait_ge(xn_ready, 2)
                turn_x().then_inc(xn_turned, 1)
                pe.wait_ge(xT_ready, 2)
                for t in range(TT):
                    for k in range(KD):
                        mm = pe.matmul(ps[:, 6, t * 64:t * 64 + 36], xT[:, k, t * P:(t + 1) * P], rw[:, k, :],
                                       start=(k == 0), stop=(k == KD - 1))
                mm.then_inc(logit_done, 1)
                pe.wait_ge(sel_ready, 1)
                sel = ro[:, 0, :, :]
                tri = cst[:, C_TRI:C_TRI + P]
                pe.matmul(ps[:, 7, 0:32], tri, sel[:, 0, :], start=True, stop=True)
                pe.matmul(ps[:, 7, 32:64], ones[:, :], sel[:, 0, :], start=True, stop=False)
                pe.matmul(ps[:, 7, 32:64], tri, sel[:, 1, :], start=False, stop=True)
                pe.matmul(ps[:, 7, 64:96], ones[:, :], sel[:, 0, :], start=True, stop=False)
                pe.matmul(ps[:, 7, 64:96], ones[:, :], sel[:, 1, :], start=False, stop=True).then_inc(cum_done, 1)

                pe.wait_ge(passes_pe, 1)
                pe.sem_clear(passes_pe)
                p1 = pe.value_load(passes[0:1, 0:1], min_val=0, max_val=MAX_PASSES * DEPTH)

                def gather(ready):
                    pe.wait_ge(onehot_ready, ready)
                    pe.wait_ge(xe_out, ready)
                    for k in range(KD):
                        for t in range(TT):
                            mm = pe.matmul(ps[:, 4 + k // 4, (k % 4) * P:(k % 4 + 1) * P], stage[:, t, k * P:(k + 1) * P],
                                           onehot[:, t, :], start=(t == 0), stop=(t == TT - 1))
                    mm.then_inc(gather_done, 1)

                def scatter(g):
                    for n in range(2 * TT):
                        h, t = divmod(n, TT)
                        pe.wait_ge(scat_read, g * (2 * TT) + n + 1)
                        pe.matmul(ps[:, 7 - n % 2, :], pgT[:, t * P:(t + 1) * P], ye[:, h * W:(h + 1) * W],
                                  start=True, stop=True).then_inc(scat_done, 1)

                pe.wait_ge(blank_pair, 1)
                gather((l + 1) + p0 * PAIRS)
                with pe.Fori(p0, p1) as p:
                    with pe.Fori(0, PAIRS) as i:
                        g = p * PAIRS + i
                        pe.wait_ge(xe_out, g + (l + 2))
                        u = 0
                        for n in range(2):
                            for kh in range(2):
                                for e in range(2):
                                    pe.wait_ge(ring_ready[u + e], (pair_fill(u + e, l, g) + 1) * 16)
                                for k in range(4):
                                    kk = 4 * kh + k
                                    for e in range(2):
                                        wt = unit(u + e)
                                        mm = pe.matmul(ps[64 * e:64 * e + 64, n, :], xe[:, kk, 64 * e:64 * e + 64], wt[:, k, :],
                                                       start=(kk == 0), stop=(kk == KD - 1))
                                        if k == 3:
                                            mm.then_inc(unit_used[u + e], 1)
                                u += 2
                        pe.wait_ge(ye_out, g + 1)
                        pe.wait_ge(pgT_out, g + 1)
                        scatter(g + l)
                        pe.wait_ge(hid_ready, g + 1)
                        pe.wait_ge(scat_read, (g + l + 1) * (2 * TT) + 2)
                        for f in range(4):
                            mm = pe.transpose(ps[:, 6, f * P:(f + 1) * P], hid[:, f * P:(f + 1) * P], ident)
                        mm.then_inc(hT_done, 1)
                        pe.wait_ge(weighted_ready, g + (l + 1))
                        for t in range(TT):
                            mm = pe.transpose(ps[:, 7, t * P:(t + 1) * P], weighted[:, t, :], ident)
                        mm.then_inc(pgT_done, 1)
                        gather(g + (l + 2))
                        pe.wait_ge(hT_out, g + 1)
                        for h in range(2):
                            for e in range(2):
                                pe.wait_ge(ring_ready[u + e], (pair_fill(u + e, l, g) + 1) * 16)
                            for k in range(4):
                                for e in range(2):
                                    wt = unit(u + e)
                                    mm = pe.matmul(ps[64 * e:64 * e + 64, 2 + h, :], hT[:, k, 64 * e:64 * e + 64], wt[:, k, :],
                                                   start=(k == 0), stop=(k == 3))
                                    if k == 3:
                                        mm.then_inc(unit_used[u + e], 1)
                            u += 2
                pe.wait_ge(ye_out, p1 * PAIRS + 1)
                pe.wait_ge(pgT_out, p1 * PAIRS + 1)
                scatter(p1 * PAIRS + l)

        @block.scalar
        def _(act):
            act.wait_ge(start_ready, 64)
            act.wait_ge(zeroed, 1)

            act.nop().then_inc(xe_out, 1)
            act.nop().then_inc(ye_out, 1)
            act.nop().then_inc(pgT_out, 1)
            act.wait_ge(angle_ready, 1)
            act.activation(rsn[:, :, :], rsn[:, :, :], ACT.Sin).then_inc(sine_ready, 1)
            act.activation(rc[:, :, :], rc[:, :, :], ACT.Sin).then_inc(sine_ready, 1)

            with act.Fori(0, DEPTH) as l:
                p0 = act.value_load(passes[0:1, 0:1], min_val=0, max_val=MAX_PASSES * DEPTH)
                act.nop().then_inc(arrive, 1)
                act.wait_ge(release_act, 1)
                act.sem_clear(release_act)
                steps = [0]

                def after(ins):
                    steps[0] += 1
                    ins.then_inc(act_step, 1)
                    act.wait_ge(act_step, steps[0])

                def squares():
                    for t in range(TT):
                        after(act.activation(work[:, 3, :], x[:, t, :], ACT.Square, accum_out=small[:, t:t + 1]))
                    act.nop().then_inc(ss_ready, 1)

                def root(n, v, m):
                    act.wait_ge(var_ready, m)
                    act.activation(v, v, ACT.Sqrt).then_inc(root_ready, 1)

                def turn_out(n, g0):
                    act.wait_ge(xn_turned, n)
                    for k in range(KD):
                        ins = act.activation(xT[:, k, :], ps[:, k // 2, (k % 2) * SEQ:(k % 2 + 1) * SEQ], ACT.Copy,
                                             scale=col[:, g0 + k:g0 + k + 1])
                        after(ins)
                    act.nop().then_inc(xT_ready, 1)

                squares()
                root(0, small[:, 2:4], 1)
                act.wait_ge(param_cols, 1)
                after(act.activation(col[:, 0:R_ROWS], ps[:, 6, 0:R_ROWS], ACT.Copy))
                act.nop().then_inc(col_copied, 1)
                act.nop().then_inc(col_copied, 1)
                turn_out(1, R_MIXG)

                def serve(m, v, f):
                    act.wait_ge(fn_asked, m + 1)
                    act.activation(v, v, f).then_inc(fn_served, 1)

                serve(0, small[:, 20:40], ACT.Tanh)
                serve(1, s5[:, 0, :], ACT.Tanh)
                serve(2, s5[:, 3:5, :], ACT.Sin)

                def chunk(c):
                    used_in_mixer(act, 2 * c + 1, l, p0)
                    if c < 3:
                        if c >= 2:
                            act.wait_ge(turned, c - 1)
                        dst = stage[:, :, (c % 2) * W:(c % 2 + 1) * W]
                    elif c < 6:
                        dst = qkv[:, :, (c - 3) * W:(c - 2) * W]
                    else:
                        dst = gates[:, :, (c - 6) * W:(c - 5) * W]
                    act.activation(dst, ps[:, 2 * (c % 2):2 * (c % 2) + 2, :], ACT.Copy if c < 6 else ACT.Sigmoid)\
                       .then_inc(chunk_out, 1)

                def turn_copy(n, dst):
                    act.wait_ge(turned, n + 1)
                    act.activation(dst, ps[:, 6:8, :].rearrange("p b (k s) -> p (b k) s", s=SEQ), ACT.Copy)\
                       .then_inc(turn_copied, 1)

                chunk(0)
                act.wait_ge(b_turned, 1)
                for n in range(2):
                    after(act.activation(bmat[:, n, :, :].rearrange("p k c -> p (k c)"), ps[:, 4 + n, :], ACT.Copy))
                act.nop().then_inc(b_copied, 1)
                act.wait_ge(c_turned, 1)
                after(act.activation(work[:, 0, :], ps[:, 6:8, :].rearrange("p b n -> p (b n)"), ACT.Copy))
                act.nop().then_inc(c_copied, 1)
                act.nop().then_inc(c_copied, 1)
                chunk(1)
                turn_copy(0, xrT[:, :, 3:])
                turn_copy(1, uT[:, :, :])
                chunk(2)
                serve(3, small[:, 86:88], ACT.Exp)
                for n in range(2):
                    act.wait_ge(rgate_done, n + 1)
                    for k in range(KW):
                        b = (R_BA, R_BX)[n] + k
                        after(act.activation(work[:, 1 + n, k * SEQ:(k + 1) * SEQ],
                                             ps[:, 6 + k // 2, (k % 2) * SEQ:(k % 2 + 1) * SEQ], ACT.Sigmoid,
                                             bias=col[:, b:b + 1]))
                    act.nop().then_inc(rgate_out, 1)
                act.wait_ge(sp_ready, 1)
                for k in range(KW):
                    after(act.activation(work[:, 1, k * SEQ:(k + 1) * SEQ], work[:, 1, k * SEQ:(k + 1) * SEQ], ACT.Tanh,
                                         scale=small[:, 44 + k:45 + k]))
                after(act.activation(work[:, 3, :], work[:, 1, :], ACT.Sqrt))
                act.nop().then_inc(rg_root, 1)
                chunk(3)
                turn_copy(2, grT[:, :, :])
                act.wait_ge(turn_copied, 3)
                act.activation(grT[:, :, :], grT[:, :, :], ACT.Gelu_apprx_tanh).then_inc(gelu_g, 1)
                chunk(4)
                chunk(5)
                chunk(6)
                turn_copy(3, qT[:, :, :])
                turn_copy(4, kT[:, :, :])
                chunk(7)

                def exponentials(n):
                    t = n % TT
                    act.wait_ge(prob_in, n + 1)
                    e, r = attn_e[:, n % 2], A_SMALL[n % 2]
                    for c in range(2):
                        ins = act.activation(e[:, c, 0:(t + 1) * P], e[:, c, 0:(t + 1) * P], ACT.Exp,
                                             bias=small[:, r + c:r + c + 1], scale=HD ** -0.5,
                                             accum_out=small[:, r + 2 + c:r + 3 + c])
                        after(ins)
                    act.nop().then_inc(prob_ready, 1)

                def late_chunk(j):
                    c, t = LATE + j // TT, j % TT
                    if t == 0:
                        act.wait_ge(late_done, j // TT + 1)
                    else:
                        used_in_mixer(act, 2 * c + 1, l, p0)
                    act.activation(gates[:, t, (c - 6) * W:(c - 5) * W], ps[:, j % 2, :], ACT.Sigmoid).then_inc(late_out, 1)

                exponentials(0)
                for n in range(2 * HEADS):
                    h, t = divmod(n, TT)
                    if n + 1 < 2 * HEADS:
                        exponentials(n + 1)
                    act.wait_ge(wT_done, n + 1)
                    act.activation(attn_wT[:, 0:t + 1, :], ps[:, 2, 0:(t + 1) * P].rearrange("p (k s) -> p k s", s=P),
                                   ACT.Copy).then_inc(wT_out, 1)
                    late_chunk(n)
                    act.wait_ge(o_done, n + 1)
                    act.activation(attn_o[:, t, h * P:(h + 1) * P], ps[:, 3, 0:P], ACT.Copy).then_inc(o_out, 1)
                act.wait_ge(z_in, 1)
                act.activation(zT[:, :, :], zT[:, :, :], ACT.Gelu_apprx_tanh).then_inc(z_out, 1)
                root(1, small[:, 64:72], 2)
                used_in_mixer(act, GLU_UNIT + 1, l, p0)
                for m in range(KW):
                    after(act.activation(work[:, 0, m * SEQ:(m + 1) * SEQ], ps[:, 4 + m // 2, (m % 2) * SEQ:(m % 2 + 1) * SEQ],
                                         ACT.Sigmoid, bias=col[:, R_GLUB + m:R_GLUB + m + 1]))
                act.nop().then_inc(glu_out, 1)
                act.wait_ge(oT_done, 1)
                act.activation(qT[:, :, :], ps[:, 6:8, :].rearrange("p b (k s) -> p (b k) s", s=SEQ), ACT.Copy,
                               scale=small[:, 84:85]).then_inc(oT_out, 1)
                act.wait_ge(m_turned, 1)
                for b in range(4):
                    after(act.activation(xT[:, 2 * b:2 * b + 2, :].rearrange("p k s -> p (k s)"), ps[:, b, :], ACT.Copy))
                act.nop().then_inc(m_copied, 1)

                act.wait_ge(res_read, 1)
                squares()
                root(2, small[:, 2:4], 3)
                turn_out(2, R_FFNG)
                act.wait_ge(fn_asked, 5)
                act.activation(ro[:, 1, :, 0:4], ro[:, 1, :, 0:4], ACT.Exp).then_inc(fn_served, 1)
                act.wait_ge(fn_asked, 6)
                act.activation(small[:, 80:82], small[:, 80:82], ACT.Exp).then_inc(fn_served, 1)

                act.wait_ge(passes_act, 1)
                act.sem_clear(passes_act)
                p1 = act.value_load(passes[0:1, 0:1], min_val=0, max_val=MAX_PASSES * DEPTH)

                def gathered(n):
                    act.wait_ge(gather_done, n)
                    for k in range(KD):
                        ins = act.activation(xe[:, k, :], ps[:, 4 + k // 4, (k % 4) * P:(k % 4 + 1) * P], ACT.Copy,
                                             scale=col[:, R_FFNG + k:R_FFNG + k + 1])
                    ins.then_inc(xe_out, 1)

                gathered((l + 1) + p0 * PAIRS)
                with act.Fori(p0, p1) as p:
                    with act.Fori(0, PAIRS) as i:
                        g = p * PAIRS + i
                        used_in_pair(act, 3, l, g)
                        act.activation(sil, ps[:, 0, :], ACT.Silu).then_inc(silu_out, 1)
                        act.wait_ge(hT_done, g + 1)
                        act.activation(hT[:, :, :], ps[:, 6, :].rearrange("p (f s) -> p f s", f=4), ACT.Copy).then_inc(hT_out, 1)
                        act.wait_ge(pgT_done, g + 1)
                        act.activation(pgT, ps[:, 7, 0:SEQ], ACT.Copy).then_inc(pgT_out, 1)
                        gathered(g + (l + 2))
                        used_in_pair(act, 11, l, g)
                        act.activation(ye.rearrange("p (h n) -> p h n", h=2), ps[:, 2:4, :], ACT.Copy).then_inc(ye_out, 1)
            act.wait_ge(final_in, 1)
            for t in range(TT):
                act.activation(work[:, 3, :], x[:, t, :], ACT.Square, accum_out=small[:, t:t + 1]).then_inc(final_out, 1)
                act.wait_ge(final_out, t + 1)
            act.wait_ge(final_in, 2)
            act.activation(small[:, 2:4], small[:, 2:4], ACT.Sqrt).then_inc(final_out, 1)

        @block.vector
        def _(dve):
            steps = [0]

            def after(ins):
                steps[0] += 1
                ins.then_inc(dve_step, 1)
                dve.wait_ge(dve_step, steps[0])

            def tt(o, i0, i1, op):
                after(dve.tensor_tensor(o, i0, i1, op))

            def tsc(o, i0, s1, s2, op0, op1=None):
                after(dve.tensor_scalar(o, i0, s1, s2, op0, op1) if op1 is not None
                      else dve.tensor_scalar(o, i0, s1, None, op0))

            def stt(o, i0, s, i1, op0, op1):
                after(dve.scalar_tensor_tensor(o, i0, s, i1, op0, op1))

            MUL, ADD, SUB, MAX, MIN, EQ = ALU.mult, ALU.add, ALU.subtract, ALU.max, ALU.min, ALU.is_equal

            def reduce_angle(th, kk, c):
                tsc(kk, th, INV_2PI, MAGIC, MUL, ADD)
                tsc(kk, kk, MAGIC, None, SUB)
                for part in (PI_2A, PI_2B, PI_2C):
                    stt(th, kk, -part, th, MUL, ADD)
                tsc(th, th, -PI, PI, MAX, MIN)
                stt(c, th, -1.0, th, MUL, MAX)
                tsc(c, c, -1.0, PI / 2, MUL, ADD)

            for v in (bnat, cdup, wa, wx):
                after(dve.memset(v[:], 0.0))
            after(dve.memset(xrT[:, :, 0:3], 0.0))
            after(dve.memset(ones[:, :], 1.0))
            after(dve.memset(passes_f[:, :], 0.0))
            after(dve.tensor_copy(passes[:, :], passes_f[:, :]))
            dve.nop().then_inc(zeroed, 1)
            dve.nop().then_inc(scat_read, 1)
            dve.nop().then_inc(scat_read, 1)
            dve.wait_ge(start_ready, 64)
            after(dve.tensor_copy(isreset[:, :], notreset[:, :].bitcast(I32)))
            tsc(isreset[:, :], isreset[:, :], 0.0, None, EQ)
            tsc(notreset[:, :], isreset[:, :], -1.0, None, ADD)
            after(dve.tensor_copy(small[:, 0:TT], pos_i[:, :]))
            for t in range(TT):
                tsc(rsn[:, t, :], cst[:, C_FREQ:C_FREQ + HALF], small[:, t:t + 1], None, MUL)
            kk = attn_w[:, 0:TT * HALF].rearrange("p (t e) -> p t e", t=TT)
            reduce_angle(rsn[:, :, :], kk, rc[:, :, :])
            dve.nop().then_inc(angle_ready, 1)
            dve.wait_ge(sine_ready, 2)

            with dve.Fori(0, DEPTH) as l:
                dve.wait_ge(arrive, 2)
                dve.sem_clear(arrive)
                for s in layer_sems:
                    dve.sem_clear(s)
                steps[0] = 0
                dve.nop().then_inc(release_pe, 1)
                dve.nop().then_inc(release_act, 1)

                p0 = dve.value_load(passes[0:1, 0:1], min_val=0, max_val=MAX_PASSES * DEPTH)

                dve.wait_ge(rows_ready, (l + 1) * (16 * N_ROWS))
                after(dve.tensor_copy(raw[0:16, :].rearrange("j (h n) -> j h n", h=2),
                                      ldt[:, :].unsqueeze(2).to_broadcast([16, 2, NS])))
                dve.nop().then_inc(raw_dt, 1)

                def normed(n):
                    dve.wait_ge(ss_ready, n)
                    tsc(small[:, 2:4], small[:, 0:2], 1.0 / D, 1e-6, MUL, ADD)
                    dve.nop().then_inc(var_ready, 1)
                    return small[:, 2:4]

                def scaled(m):
                    dve.wait_ge(root_ready, m)
                    after(dve.reciprocal(small[:, 4:6], small[:, 2:4]))
                    for t in range(TT):
                        tsc(stage[:, t, :], x[:, t, :], small[:, 4 + t:5 + t], None, MUL)
                    dve.nop().then_inc(xn_ready, 1)

                normed(1)
                scaled(1)

                dve.wait_ge(col_copied, 1)
                e = small[:, 20:40]
                tsc(small[:, 20:36], col[:, R_DT:R_DT + JT], 1 / 32, None, MUL)
                tsc(small[:, 40:44], col[:, R_LAM:R_LAM + KW], -1.0, None, MUL)
                tt(small[:, 36:40], small[:, 40:44], col[:, R_LAM:R_LAM + KW], MIN)
                tsc(small[:, 36:40], small[:, 36:40], 1 / 32, None, MUL)
                dve.nop().then_inc(fn_asked, 1)
                dve.wait_ge(fn_served, 1)
                den = small[:, 100:120]
                tsc(den, e, -1.0, 1.0, MUL, ADD)
                tsc(e, e, 1.0, None, ADD)
                after(dve.reciprocal(den, den))
                tt(e, e, den, MUL)
                for _ in range(4):
                    tt(e, e, e, MUL)
                dt = small[:, 20:36]
                lr, li = col[:, R_RE:R_RE + JT], col[:, R_IM:R_IM + JT]
                Q, MAG, SN, CS, AR, AI, CR, CI, T0, T1, T2 = (s5[:, n, :] for n in (0, 1, 3, 4, 5, 6, 7, 8, 9, 10, 11))
                stt(Q, lr, -0.5, dt, MUL, MUL)
                dve.nop().then_inc(fn_asked, 1)
                tt(SN, li, dt, MUL)
                reduce_angle(SN, T0, CS)
                dve.nop().then_inc(fn_asked, 1)
                y4, z4, zz, po = small[:, 36:40], small[:, 120:124], small[:, 124:128], small[:, 128:132]
                tsc(zz, y4, 2.0, None, ADD)
                after(dve.reciprocal(zz, zz))
                tt(z4, y4, zz, MUL)
                tt(zz, z4, z4, MUL)
                tsc(po, zz, 1 / 19, 1 / 17, MUL, ADD)
                for n in (15, 13, 11, 9, 7, 5, 3, 1):
                    tt(po, po, zz, MUL)
                    tsc(po, po, 1 / n, None, ADD)
                stt(po, z4, 2.0, po, MUL, MUL)
                stt(po, small[:, 40:44], 0.0, po, MAX, ADD)
                tsc(small[:, 44:48], po, 4.0, None, MUL)
                dve.nop().then_inc(sp_ready, 1)
                tt(small[:, 84:85], col[:, R_SUB:R_SUB + 1], cst[:, ds(l + C_ONEM, 1)], MUL)
                dve.wait_ge(fn_served, 2)
                tsc(T0, Q, 1.0, None, ADD)
                after(dve.reciprocal(T0, T0))
                tsc(MAG, Q, -1.0, 1.0, MUL, ADD)
                tt(MAG, MAG, T0, MUL)
                dve.wait_ge(fn_served, 3)
                tt(AR, MAG, CS, MUL)
                tt(AI, MAG, SN, MUL)
                tt(T0, lr, lr, MUL)
                tt(T1, li, li, MUL)
                tt(T0, T0, T1, ADD)
                after(dve.reciprocal(T0, T0))
                tsc(T2, AR, -1.0, None, ADD)
                tt(CR, T2, lr, MUL)
                tt(T1, AI, li, MUL)
                tt(CR, CR, T1, ADD)
                tt(CR, CR, T0, MUL)
                tt(CI, AI, lr, MUL)
                tt(T1, T2, li, MUL)
                tt(CI, CI, T1, SUB)
                tt(CI, CI, T0, MUL)
                dve.wait_ge(params_ready, (l + 1) * (16 * N_PARAMS))
                for n in range(2):
                    tt(lamv[:, 2 * n, :], lamv[:, 2 * n, :], lamv[:, 2 * n + 1, :], MUL)
                    after(dve.tensor_reduce(small[:, 86 + n:87 + n], lamv[:, 2 * n, :], AX, ADD))
                dve.nop().then_inc(fn_asked, 1)
                dve.wait_ge(c_copied, 1)
                cre = work[:, 0, 0:512].rearrange("p (j c) -> p j c", j=JT)
                cim = work[:, 0, 512:1024].rearrange("p (j c) -> p j c", j=JT)
                crb, cib = (v.unsqueeze(2).to_broadcast([P, JT, 32]) for v in (CR, CI))
                c0, c1, c2 = (ccoef[:, n, :, :] for n in range(3))
                tt(c0, cre, crb, MUL)
                tt(c1, cim, cib, MUL)
                tt(c0, c0, c1, SUB)
                tt(c2, cre, cib, MUL)
                tt(c1, cim, crb, MUL)
                stt(c2, c2, -1.0, c1, MUL, SUB)
                tsc(c1, c0, -1.0, None, MUL)
                dve.wait_ge(turn_copied, 1)
                for k in range(KW):
                    xc = work[:, 0, k * SEQ:(k + 1) * SEQ]
                    tsc(xc, xrT[:, k, 3:3 + SEQ], col[:, R_CW + k:R_CW + k + 1], col[:, R_CB + k:R_CB + k + 1], MUL, ADD)
                    for j in range(1, 4):
                        c = R_CW + 4 * j + k
                        stt(xc, xrT[:, k, 3 - j:3 - j + SEQ], col[:, c:c + 1], xc, MUL, ADD)
                dve.nop().then_inc(conv_ready, 1)

                after(dve.tensor_copy(pre[:, :, 0, 0], CS))
                after(dve.tensor_copy(pre[:, :, 0, 1], SN))
                for n in range(7):
                    re, im = pre[:, :, n, 0], pre[:, :, n, 1]
                    tt(T0, re, re, MUL)
                    tt(T1, im, im, MUL)
                    tt(pre[:, :, n + 1, 0], T0, T1, SUB)
                    stt(pre[:, :, n + 1, 1], re, 2.0, im, MUL, MUL)

                def double(tc, tsn, n, power, t0, t1, j0, nj):
                    er = pre[:, j0:j0 + nj, power, 0].unsqueeze(2).to_broadcast([P, nj, n])
                    ei = pre[:, j0:j0 + nj, power, 1].unsqueeze(2).to_broadcast([P, nj, n])
                    c, s = tc[:, :, 0:n], tsn[:, :, 0:n]
                    tt(t0, c, er, MUL)
                    tt(t1, s, ei, MUL)
                    tt(tc[:, :, n:2 * n], t0, t1, SUB)
                    tt(t0, c, ei, MUL)
                    tt(t1, s, er, MUL)
                    tt(tsn[:, :, n:2 * n], t0, t1, ADD)

                after(dve.memset(bcos[:, :, 0:1], 1.0))
                after(dve.memset(bsin[:, :, 0:1], 0.0))
                flat = [w.rearrange("p a b -> p (a b)") for w in (tcos[:, :, :], tsin[:, :, :])]
                for n in range(5):
                    t0, t1 = (w[:, 0:JT << n].rearrange("p (j n) -> p j n", j=JT) for w in flat)
                    double(bcos[:, :, :], bsin[:, :, :], 1 << n, n, t0, t1, 0, JT)

                def tables(k, tmp):
                    after(dve.tensor_copy(tcos[:, :, 0:32], bcos[:, 4 * k:4 * k + 4, :]))
                    after(dve.tensor_copy(tsin[:, :, 0:32], bsin[:, 4 * k:4 * k + 4, :]))
                    for n in (5, 6, 7):
                        t0, t1 = (tmp[:, r * 512:r * 512 + (4 << n)].rearrange("p (j n) -> p j n", j=4) for r in range(2))
                        double(tcos[:, :, :], tsin[:, :, :], 1 << n, n, t0, t1, 4 * k, 4)

                def turn_in(m):
                    q = 2 * (m % 2)
                    dve.wait_ge(bu_done, m + 1)
                    pr, pi = ps[:, 4:6, 0:SEQ], ps[:, 4:6, SEQ:2 * SEQ]
                    c, s = tcos[:, q:q + 2, :], tsin[:, q:q + 2, :]
                    w = [work[:, n, q * SEQ:(q + 2) * SEQ].rearrange("p (j s) -> p j s", j=2) for n in range(4)]
                    tt(w[0], pr, c, MUL)
                    tt(w[1], pi, s, MUL)
                    tt(w[2], pi, c, MUL)
                    tt(w[3], pr, s, MUL)
                    dve.nop().then_inc(bu_read, 1)

                def scans(k, n):
                    for q in range(4):
                        r = slice(q * SEQ, (q + 1) * SEQ)
                        m = MAG[:, 4 * k + q:4 * k + q + 1].to_broadcast([P, SEQ])
                        after(dve.tensor_tensor_scan(work[:, n + 1, r], m, work[:, n, r], 0.0, MUL, ADD))

                def recur_re(k):
                    tt(work[:, 0, :], work[:, 0, :], work[:, 1, :], ADD)
                    tt(work[:, 2, :], work[:, 2, :], work[:, 3, :], SUB)
                    scans(k, 0)

                def recur_im(k):
                    scans(k, 2)
                    c, s = (v[:, :, :].rearrange("p j s -> p (j s)") for v in (tcos, tsin))
                    tt(work[:, 0, :], work[:, 1, :], c, MUL)
                    tt(work[:, 2, :], work[:, 1, :], s, MUL)
                    tt(work[:, 1, :], work[:, 3, :], s, MUL)
                    tt(work[:, 3, :], work[:, 3, :], c, MUL)
                    dve.nop().then_inc(s_ready, 1)

                def y_out(k):
                    dve.wait_ge(y_done, k + 1)
                    stt(zT[:, k, :], uT[:, k, :], col[:, R_D + k:R_D + k + 1], ps[:, 4, 0:SEQ], MUL, ADD)
                    dve.nop().then_inc(y_read, 1)

                tables(0, zT[:, :, :].rearrange("p k s -> p (k s)"))

                dve.wait_ge(rg_root, 1)
                z = zT[:, :, :].rearrange("p k s -> p (k s)")
                def kws(v):
                    return v.rearrange("p (k s) -> p k s", k=KW)
                nrb = notreset[:, :].unsqueeze(1).to_broadcast([P, KW, SEQ])
                rsb = isreset[:, :].unsqueeze(1).to_broadcast([P, KW, SEQ])
                tsc(z, work[:, 1, :], 1.0, None, ADD)
                after(dve.reciprocal(z, z))
                stt(work[:, 1, :], work[:, 1, :], -1.0, z, ADD, MUL)
                tt(kws(work[:, 1, :]), kws(work[:, 1, :]), nrb, MUL)
                stt(work[:, 3, :], work[:, 3, :], -2.0, z, MUL, MUL)
                tt(kws(work[:, 3, :]), kws(work[:, 3, :]), nrb, MUL)
                tt(kws(work[:, 3, :]), kws(work[:, 3, :]), rsb, ADD)
                tt(work[:, 2, :], work[:, 2, :], work[:, 0, :], MUL)
                tt(work[:, 3, :], work[:, 3, :], work[:, 2, :], MUL)
                for k in range(KW):
                    r = slice(k * SEQ, (k + 1) * SEQ)
                    after(dve.tensor_tensor_scan(xrT[:, k, 3:], work[:, 1, r], work[:, 3, r], 0.0, MUL, ADD))

                mask = cst[:, C_MASK:C_MASK + P]

                def masked(n):
                    t = n % TT
                    dve.wait_ge(score_done, n + 1)
                    sc, e, r = ps[:, 6:8, 0:SEQ], attn_e[:, n % 2], A_SMALL[n % 2]
                    if t == 1:
                        after(dve.tensor_copy(e[:, :, 0:P], sc[:, :, 0:P]))
                    tt(e[:, :, t * P:(t + 1) * P], sc[:, :, t * P:(t + 1) * P],
                       mask.unsqueeze(1).to_broadcast([P, 2, P]), ADD)
                    after(dve.tensor_reduce(small[:, r:r + 2], e[:, :, 0:(t + 1) * P], AX, MAX))
                    tsc(small[:, r:r + 2], small[:, r:r + 2], -HD ** -0.5, None, MUL)
                    dve.nop().then_inc(prob_in, 1)

                def weights(n):
                    t = n % TT
                    e, r = attn_e[:, n % 2], A_SMALL[n % 2]
                    dve.wait_ge(prob_ready, n + 1)
                    after(dve.reciprocal(small[:, r + 4:r + 6], small[:, r + 2:r + 4]))
                    tt(small[:, r + 5:r + 6], small[:, r + 5:r + 6], small[:, 88:89], MUL)
                    if n >= 1:
                        dve.wait_ge(wT_done, n)
                    w = attn_w[:, 0:(t + 1) * P]
                    tsc(w, e[:, 0, 0:(t + 1) * P], small[:, r + 4:r + 5], None, MUL)
                    stt(w, e[:, 1, 0:(t + 1) * P], small[:, r + 5:r + 6], w, MUL, ADD)
                    dve.nop().then_inc(w_ready, 1)

                turn_in(0)
                turn_in(1)
                recur_re(0)
                recur_im(0)
                dve.wait_ge(chunk_out, 5)
                dve.wait_ge(turned, 3)
                flat = stage[:, 0, :], stage[:, 1, :]
                for t in range(TT):
                    xx = qkv[:, t, 0:2 * W].rearrange("p (h c e) -> p h c e", c=2, e=HALF)
                    t0, t1 = (w.rearrange("p (h c e) -> p h c e", c=2, e=HALF) for w in flat)
                    cb, sbc = (v[:, t, :].unsqueeze(1).unsqueeze(1).to_broadcast([P, 4 * HEADS, 2, HALF]) for v in (rc, rsn))
                    tt(t0, xx, cb, MUL)
                    tt(t1, xx, sbc, MUL)
                    tt(xx[:, :, 0, :], t0[:, :, 0, :], t1[:, :, 1, :], SUB)
                    tt(xx[:, :, 1, :], t0[:, :, 1, :], t1[:, :, 0, :], ADD)
                dve.nop().then_inc(rope_ready, 1)

                dve.wait_ge(gelu_g, 1)
                tt(grT[:, :, :], grT[:, :, :], xrT[:, :, 3:], MUL)
                dve.nop().then_inc(yrnn_ready, 1)
                tmp = stage[:, 0, :]
                tables(1, tmp)
                y_out(0)
                turn_in(2)
                turn_in(3)
                recur_re(1)
                recur_im(1)
                dve.wait_ge(fn_served, 4)
                tt(small[:, 88:89], small[:, 87:88], small[:, 86:87], SUB)
                tt(small[:, 88:89], small[:, 88:89], cst[:, ds(l + C_LINIT, 1)], SUB)

                s5_steps = (
                    lambda: (tables(2, tmp), y_out(1)), lambda: turn_in(4), lambda: (turn_in(5), recur_re(2)), lambda: recur_im(2),
                    lambda: (tables(3, tmp), y_out(2)), lambda: turn_in(6), lambda: (turn_in(7), recur_re(3)), lambda: recur_im(3))
                masked(0)
                for n in range(2 * HEADS):
                    if n + 1 < 2 * HEADS:
                        masked(n + 1)
                    s5_steps[n]()
                    weights(n)
                y_out(3)
                dve.nop().then_inc(z_in, 1)

                dve.wait_ge(o_out, 2 * HEADS)
                o8 = attn_o[:, :, :].rearrange("p t (h v) -> p (t h) v", v=P)
                sq = work[:, 1, :].rearrange("p (g v) -> p g v", v=P)
                tt(sq, o8, o8, MUL)
                after(dve.tensor_reduce(small[:, 64:72], sq, AX, ADD))
                tsc(small[:, 64:72], small[:, 64:72], 1.0 / P, 1e-5, MUL, ADD)
                dve.nop().then_inc(var_ready, 1)
                dve.wait_ge(root_ready, 2)
                after(dve.reciprocal(small[:, 72:80], small[:, 64:72]))
                tt(o8, o8, small[:, 72:80].unsqueeze(2).to_broadcast([P, TT * HEADS, P]), MUL)
                dve.nop().then_inc(o_normed, 1)

                def gated(n):
                    b, h = divmod(n, 2)
                    used_in_mixer(dve, PROJ_UNIT[b] + h, l, p0)
                    bank = 2 * (n % 2)
                    gt = gates[:, :, b * D + h * W:b * D + (h + 1) * W]
                    mg = stage[:, :, h * W:(h + 1) * W]
                    tt(mg if b == 0 else gt, ps[:, bank:bank + 2, :], gt, MUL)
                    if b:
                        tt(mg, mg, gt, ADD)
                    dve.nop().then_inc(proj_read, 1)

                gated(0)
                gated(1)
                dve.wait_ge(glu_out, 1)
                tt(uT[:, :, :], zT[:, :, :], kws(work[:, 0, :]), MUL)
                dve.nop().then_inc(yssm_ready, 1)
                for n in range(2, 6):
                    gated(n)
                dve.nop().then_inc(arena_free, 1)
                for h in range(2):
                    used_in_mixer(dve, OUT_UNIT + 1 + 2 * h, l, p0)
                    tt(x[:, :, h * W:(h + 1) * W], ps[:, 2 * h:2 * h + 2, :], x[:, :, h * W:(h + 1) * W], ADD)
                dve.nop().then_inc(res_read, 1)


                normed(2)
                scaled(3)
                after(dve.memset(ye, 0.0))
                after(dve.memset(pgT, 0.0))
                dve.nop().then_inc(blank_pair, 1)
                dve.wait_ge(logit_done, 1)
                tt(lg[:, :, :], ps[:, 6, 0:2 * 64].rearrange("p (t n) -> p t n", t=TT)[:, :, 0:36],
                   rbias[:, :].unsqueeze(1).to_broadcast([P, TT, 36]), ADD)
                coarse, fine = lg[:, :, 0:4], lg[:, :, 4:36]
                m2, m3 = small[:, 90:92], small[:, 92:94]

                def first_of_max(oh, v, n, io):
                    after(dve.tensor_reduce(m2, v, AX, MAX))
                    tt(oh, v, m2.unsqueeze(2).to_broadcast([P, TT, n]), EQ)
                    stt(oh, oh, -64.0, io, MUL, ADD)
                    after(dve.tensor_reduce(m3, oh, AX, MIN))
                    tsc(m3, m3, 64.0, None, ADD)
                    tt(oh, io, m3.unsqueeze(2).to_broadcast([P, TT, n]), EQ)

                io32 = cst[:, C_I32:C_I32 + NEXP].unsqueeze(1).to_broadcast([P, TT, NEXP])
                io4 = cst[:, C_I32:C_I32 + 4].unsqueeze(1).to_broadcast([P, TT, 4])
                goh = ro[:, 2, :, 0:4]
                first_of_max(goh, coarse, 4, io4)
                tt(ro[:, 1, :, 0:4], coarse, m2.unsqueeze(2).to_broadcast([P, TT, 4]), SUB)
                dve.nop().then_inc(fn_asked, 1)
                pen = ro[:, 3, :, 0:4]
                tsc(pen, goh, 1e30, -1e30, MUL, ADD)
                fm = ro[:, 4, :, :]
                fm4, fine4 = (v.rearrange("p t (g e) -> p t g e", g=4) for v in (fm, fine))
                for t in range(TT):
                    tt(fm4[:, t], fine4[:, t], goh[:, t].unsqueeze(2).to_broadcast([P, 4, 8]), MUL)
                    tt(fm4[:, t], fm4[:, t], pen[:, t].unsqueeze(2).to_broadcast([P, 4, 8]), ADD)
                dve.wait_ge(fn_served, 5)
                psel = small[:, 94:96]
                after(dve.tensor_reduce(psel, ro[:, 1, :, 0:4], AX, ADD))
                after(dve.reciprocal(psel, psel))
                oh1, oh2 = ro[:, 5, :, :], ro[:, 1, :, :]
                first_of_max(oh1, fm, NEXP, io32)
                after(dve.tensor_copy(small[:, 82:84], m2))
                stt(fm, oh1, -2e30, fm, MUL, ADD)
                first_of_max(oh2, fm, NEXP, io32)
                sel = ro[:, 0, :, :]
                tt(sel, oh1, oh2, ADD)
                dve.nop().then_inc(sel_ready, 1)
                e2 = small[:, 80:82]
                tt(e2, m2, small[:, 82:84], SUB)
                dve.nop().then_inc(fn_asked, 1)
                dve.wait_ge(fn_served, 6)
                w1s, w2s = small[:, 96:98], small[:, 98:100]
                tsc(w1s, e2, 1.0, None, ADD)
                after(dve.reciprocal(w1s, w1s))
                tt(w1s, w1s, psel, MUL)
                tt(w2s, w1s, e2, MUL)
                gt = gate[:, :, 0:NEXP]
                tt(gt, oh1, w1s.unsqueeze(2).to_broadcast([P, TT, NEXP]), MUL)
                tt(oh2, oh2, w2s.unsqueeze(2).to_broadcast([P, TT, NEXP]), MUL)
                tt(gt, gt, oh2, ADD)
                after(dve.tensor_copy(gate[:, :, NEXP:], gate[:, :, 0:2]))
                dve.wait_ge(cum_done, 1)
                rk = rank[:, :, 0:NEXP]
                stt(rk, ps[:, 7, 0:64].rearrange("p (t n) -> p t n", t=TT), 1.0, sel, ADD, MUL)
                tsc(rk, rk, -1.0, None, ADD)
                tsc(rank[:, :, NEXP:], rank[:, :, 0:2], -float(SLOTS), None, ADD)
                top = small[:, 132:133]
                after(dve.tensor_reduce(top, ps[:, 7, 64:96], AX, MAX))
                for n in range(1, MAX_PASSES):
                    tsc(small[:, 133:134], top, float(n * SLOTS), None, ALU.is_gt)
                    tt(passes_f[:, :], passes_f[:, :], small[:, 133:134], ADD)
                tsc(passes_f[:, :], passes_f[:, :], 1.0, None, ADD)
                after(dve.tensor_copy(passes[:, :], passes_f[:, :]))
                for s in (passes_pe, passes_act, passes_sp):
                    dve.nop().then_inc(s, 1)
                p1 = dve.value_load(passes[0:1, 0:1], min_val=0, max_val=MAX_PASSES * DEPTH)

                io64 = cst[:, C_I64:C_I64 + SLOTS]

                def one_hots(e0):
                    for e in range(2):
                        for t in range(TT):
                            ins = dve.tensor_scalar(onehot[:, t, e * SLOTS:(e + 1) * SLOTS], io64,
                                                    rank[:, t, ds(e0 + e, 1)], None, EQ)
                    return ins

                def weigh(e0):
                    for e in range(2):
                        for t in range(TT):
                            ins = dve.tensor_scalar(weighted[:, t, e * SLOTS:(e + 1) * SLOTS], io64,
                                                    rank[:, t, ds(e0 + e, 1)], gate[:, t, ds(e0 + e, 1)], EQ, MUL)
                    return ins

                one_hots(0).then_inc(onehot_ready, 1)
                weigh(0).then_inc(weighted_ready, 1)
                with dve.Fori(p0, p1) as p:
                    with dve.Fori(0, PAIRS) as i:
                        g = p * PAIRS + i
                        dve.wait_ge(gather_done, g + (l + 1))
                        one_hots(i * 2 + 2).then_inc(onehot_ready, 1)
                        dve.wait_ge(silu_out, g + 1)
                        used_in_pair(dve, 7, l, g)
                        dve.tensor_tensor(hid, ps[:, 1, :], sil, MUL).then_inc(hid_ready, 1)
                        for n in range(2 * TT):
                            h, t = divmod(n, TT)
                            dve.wait_ge(scat_done, (g + l) * (2 * TT) + n + 1)
                            xh = x[:, t, h * W:(h + 1) * W]
                            dve.tensor_tensor(xh, ps[:, 7 - n % 2, :], xh, ADD).then_inc(scat_read, 1)
                        dve.wait_ge(pgT_done, g + 1)
                        weigh(i * 2 + 2).then_inc(weighted_ready, 1)
                        dve.wait_ge(weighted_ready, g + (l + 2))
                        dve.wait_ge(onehot_ready, g + (l + 2))
                        rn = rank[:, :, ds(i * 2 + 2, 2)]
                        dve.tensor_scalar(rn, rn, -float(SLOTS), None, ADD).then_inc(rank_moved, 1)
                        dve.wait_ge(rank_moved, g + 1)
                for n in range(2 * TT):
                    h, t = divmod(n, TT)
                    dve.wait_ge(scat_done, (p1 * PAIRS + l) * (2 * TT) + n + 1)
                    xh = x[:, t, h * W:(h + 1) * W]
                    dve.tensor_tensor(xh, ps[:, 7 - n % 2, :], xh, ADD).then_inc(scat_read, 1)
                dve.wait_ge(scat_read, (p1 * PAIRS + l + 1) * (2 * TT) + 2)
                dve.nop().then_inc(layer_out, 1)

            done = steps[0]
            after(dve.tensor_copy(small[:, 90:91], ones[:, 0:1]))
            dve.nop().then_inc(final_in, 1)
            dve.wait_ge(final_out, 2)
            tsc(small[:, 2:4], small[:, 0:2], 1.0 / D, 1e-6, MUL, ADD)
            dve.nop().then_inc(final_in, 1)
            dve.wait_ge(final_out, 3)
            after(dve.reciprocal(small[:, 4:6], small[:, 2:4]))
            dve.wait_ge(final_g_ready, 16)
            for t in range(TT):
                stt(stage[:, t, :], x[:, t, :], small[:, 4 + t:5 + t], gates[:, 0, 0:D], MUL, MUL)
            dve.nop().then_inc(out_ready, 1)


def constants():
    import math

    import numpy as np
    c = np.zeros((P, C_COLS), np.float32)
    r = np.arange(P)
    c[:, C_ID:C_ID + P] = np.eye(P)
    c[:, C_TRI:C_TRI + P] = r[:, None] < r[None, :]
    c[:, C_MASK:C_MASK + P] = np.where(r[None, :] <= r[:, None], 0.0, -1e30 * HD ** 0.5)
    c[:, C_I64:C_I64 + SLOTS] = np.arange(SLOTS)
    c[:, C_I32:C_I32 + NEXP] = np.arange(NEXP)
    c[:, C_FREQ:C_FREQ + HALF] = np.float32(10000.0) ** (-np.arange(0, HD, 2, dtype=np.float32) / np.float32(HD))
    for n in range(DEPTH):
        init = 0.8 - 0.6 * math.exp(-0.3 * n)
        c[:, C_LINIT + n] = init
        c[:, C_ONEM + n] = 1.0 - init
    return c


def kernel(**inputs):
    import numpy as _np
    import concourse.bacc as _bacc
    from concourse import mybir as _mybir
    from concourse.bass_utils import run_bass_kernel_spmd as _run

    nc = _bacc.Bacc("TRN2", target_bir_lowering=False, num_devices=1)
    arrays, aps = {}, {}
    for name, v in inputs.items():
        v = _np.ascontiguousarray(v)
        if v.ndim == 1:
            v = v.reshape(1, -1)
        arrays["in_" + name] = v
        aps[name] = nc.dram_tensor("in_" + name, v.shape, _mybir.dt.from_np(v.dtype), kind="ExternalInput").ap()
    arrays["consts"] = constants()
    consts = nc.dram_tensor("consts", (P, C_COLS), F32, kind="ExternalInput").ap()
    out = nc.dram_tensor("result", (1, SEQ, D), F32, kind="ExternalOutput").ap()
    hybrid_kernel(nc, aps, consts, out)
    return _run(nc, [arrays], core_ids=[0]).results[0]["result"]
```

```python
from contextlib import ExitStack

import concourse.bass as bass
from concourse import mybir

F32 = mybir.dt.float32
I32 = mybir.dt.int32
ALU = mybir.AluOpType
ACT = mybir.ActivationFunctionType
AX = mybir.AxisListType.X
ds = bass.ds

P = 128
DEPTH = 2
D = 1024
KD = D // P
SEQ = 256
TT = SEQ // P
W = 512
KW = W // P
GATE0 = 6 * W
HEADS = 4
HD = 64
HALF = HD // 2
JT = 16
NS = 64
GI = 16
NEXP = 32
PAIRS = NEXP // 2
SLOTS = 64
FF = 512
MAX_PASSES = SEQ // SLOTS

UNITS = 6
PAIR_UNITS = 12
UNIT = 2048
MIX_UNITS = 36
A_QKV = 3 * KD * SEQ
MIX_FILLS = MIX_UNITS // UNITS

C_ID, C_TRI, C_MASK, C_I64, C_I32, C_FREQ, C_LINIT, C_ONEM, C_I32M = 0, 128, 256, 384, 448, 480, 512, 514, 516
C_COLS = 548

R_DT, R_RE, R_IM, R_MIXG, R_FFNG, R_CW, R_CB, R_BA, R_BX, R_LAM, R_D, R_GLUB, R_SUB = (
    0, 16, 32, 48, 56, 64, 80, 84, 88, 92, 96, 100, 104)
R_ROWS = 105
LATE = 7
EARLY = 4 * (12 - LATE) - 15
PROJ_UNIT, GLU_UNIT, OUT_UNIT = (24, 28, 30), 26, 32

PARAM_ROWS = (
    (R_MIXG, "mix_norm_g", 8), (R_RE, "ssm_lambda_re", 16), (R_IM, "ssm_lambda_im", 16), (R_FFNG, "ffn_norm_g", 8),
    (R_CW, "conv_w", 16), (R_CB, "conv_b", 4), (R_BA, "rg_ba", 4), (R_BX, "rg_bx", 4), (R_LAM, "rg_lambda", 4),
    (R_D, "ssm_d", 4), (R_GLUB, "ssm_glu_b", 4), (R_SUB, "subln_g", 1))
N_ROWS = 1 + len(PARAM_ROWS)
N_PARAMS = 32

A_SMALL = 52, 136

BU_BANK = (4, 6, 4, 6, 4, 4, 4, 4)

MAGIC = 12582912.0
INV_2PI = 0.15915494309189535
PI = 3.141592502593994
PI_2A, PI_2B, PI_2C = 6.28125, 0.0019350051879882812, 3.0199159819567e-07


def mixer_units():
    units = []
    for c in (0, 5, 2, 3, 1, 4):
        units += [("in", c * W, kh) for kh in range(2)]
    for c in range(6):
        units += [("in", GATE0 + c * W, kh) for kh in range(2)]
    units += [("proj", 0, h) for h in range(2)]
    units += [("glu", 0, 0), ("glu", 1, 0)]
    units += [("proj", b, h) for b in (1, 2) for h in range(2)]
    units += [("out", h, kh) for h in range(2) for kh in range(2)]
    assert len(units) == MIX_UNITS
    return units


def hybrid_kernel(nc, a, consts, out):
    ctx = ExitStack()
    with ctx:
        def sb(name, shape, dt=F32):
            return ctx.enter_context(nc.sbuf_tensor(name, shape, dt))

        def sem(name):
            return ctx.enter_context(nc.semaphore(name))

        ring = sb("ring", [P, UNITS, UNIT])
        cst = sb("cst", [P, C_COLS])
        x = sb("x", [P, TT, D])
        xT = sb("xT", [P, KD, SEQ])
        stage = sb("stage", [P, TT, D])
        arena = sb("arena", [P, PAIR_UNITS - UNITS, UNIT])
        flat_arena = arena[:, :, :].rearrange("p u n -> p (u n)")
        gatesT = flat_arena[:, 0:A_QKV].rearrange("p (k s) -> p k s", s=SEQ)
        qkv = flat_arena[:, A_QKV:A_QKV + 3 * W * TT].rearrange("p (t n) -> p t n", t=TT)
        xrT = sb("xrT", [P, KW, SEQ + 3])
        grT, uT, zT = (flat_arena[:, c:c + KW * SEQ].rearrange("p (k s) -> p k s", k=KW)
                       for c in range(A_QKV + 3 * W * TT, (PAIR_UNITS - UNITS) * UNIT, KW * SEQ))
        qT = sb("qT", [P, HEADS, SEQ])
        kT = sb("kT", [P, HEADS, SEQ])
        work = sb("work", [P, 4, 4 * SEQ])
        tcos = sb("tcos", [P, 4, SEQ])
        tsin = sb("tsin", [P, 4, SEQ])
        bcos = sb("bcos", [P, JT, 32])
        bsin = sb("bsin", [P, JT, 32])
        attn_e = sb("attn_e", [P, 2, 2, SEQ])
        attn_w = sb("attn_w", [P, SEQ])
        attn_wT = sb("attn_wT", [P, 2, P])
        attn_o = sb("attn_o", [P, TT, W])
        raw = sb("raw", [P, P])
        ldt = sb("ldt", [16, 2])
        col = sb("col", [P, P])
        lamv = sb("lamv", [P, 4, HD])
        rbias = sb("rbias", [P, 36])
        rw = sb("rw", [P, KD, 36])
        wa = sb("wa", [P, KW, P])
        wx = sb("wx", [P, KW, P])
        bnat = sb("bnat", [P, 2, JT, 2 * GI])
        bmat = sb("bmat", [P, 2, KW, P])
        cdup = sb("cdup", [P, 2, KW, P])
        ccoef = sb("ccoef", [P, 3, JT, 2 * GI])
        s5 = sb("s5", [P, 12, JT])
        pre = sb("pre", [P, JT, 8, 2])
        rc = sb("rc", [P, TT, HALF])
        rsn = sb("rsn", [P, TT, HALF])
        angles = sb("angles", [P, 2, TT, HALF])
        notreset = sb("notreset", [P, SEQ])
        small = sb("small", [P, 160])
        lg = sb("lg", [P, TT, 36])
        ro = sb("ro", [P, 6, TT, NEXP])
        rank = sb("rank", [P, TT, NEXP + 2])
        gate = sb("gate", [P, TT, NEXP + 2])
        passes = sb("passes", [P, 1], I32)
        passes_f = sb("passes_f", [P, 1])
        ones = sb("ones", [P, P])
        pos_i = sb("pos_i", [P, TT], I32)
        isreset = sb("isreset", [P, SEQ])
        ps = ctx.enter_context(nc.psum_tensor("ps", [P, 8, 512], F32))

        final_g = flat_arena[:, 0:D]
        mT = stage[:, :, :].rearrange("p t (k s) -> p (t k) s", s=SEQ)
        rotor_tmp = zT[:, 2:4, :]
        rms_row = sb("rms_row", [P, SEQ])
        ident = cst[:, C_ID:C_ID + P]
        xe = work[:, 0, :].rearrange("p (k s) -> p k s", k=KD)
        ye = work[:, 1, :]
        hid = work[:, 2, 0:FF]
        sil = work[:, 2, FF:2 * FF]
        hT = work[:, 3, 0:FF].rearrange("p (f s) -> p f s", f=4)
        pgT = work[:, 3, FF:FF + SEQ]
        onehot = attn_o[:, :, 0:P]
        weighted = attn_o[:, :, P:2 * P]

        ring_ready = [sem(f"ring_ready{i}") for i in range(PAIR_UNITS)]
        unit_used = [sem(f"unit_used{i}") for i in range(PAIR_UNITS)]
        rows_ready, params_ready = sem("rows_ready"), sem("params_ready")
        arena_free = sem("arena_free")
        rotor_base, rotor_ready, rotor_used = sem("rotor_base"), sem("rotor_ready"), sem("rotor_used")
        pool_step = sem("pool_step")
        paced = sem("paced")
        pos_ready = sem("pos_ready")
        zeroed = sem("zeroed")
        out_ready = sem("out_ready")
        stored = sem("stored")
        layer_sems = []

        def lsem(name):
            s = sem(name)
            layer_sems.append(s)
            return s

        router_over, cleared = sem("router_over"), sem("cleared")
        x_loaded = sem("x_loaded")
        blocks_zeroed = sem("blocks_zeroed")
        dve_step, act_step = lsem("dve_step"), lsem("act_step")
        param_cols, col_copied = lsem("param_cols"), lsem("col_copied")
        raw_dt = lsem("raw_dt")
        b_turned, b_copied = lsem("b_turned"), lsem("b_copied")
        c_turned, c_copied = lsem("c_turned"), lsem("c_copied")
        ss_ready, var_ready, root_ready = lsem("ss_ready"), lsem("var_ready"), lsem("root_ready")
        x_turned, xT_ready, xn_ready = lsem("x_turned"), lsem("xT_ready"), lsem("xn_ready")
        chunk_out = lsem("chunk_out")
        late_done, late_out = lsem("late_done"), lsem("late_out")
        diag_ready, row_done = lsem("diag_ready"), lsem("row_done")
        turned, turn_copied = lsem("turned"), lsem("turn_copied")
        fn_asked, fn_served = lsem("fn_asked"), lsem("fn_served")
        sp_ready = lsem("sp_ready")
        conv_ready, rgate_done, rgate_out = lsem("conv_ready"), lsem("rgate_done"), lsem("rgate_out")
        rg_root, yrnn_ready = lsem("rg_root"), lsem("yrnn_ready")
        rope_ready = lsem("rope_ready")
        score_done, w_ready = lsem("score_done"), lsem("w_ready")
        prob_in, prob_ready = lsem("prob_in"), lsem("prob_ready")
        wT_done, wT_out, o_done, o_out = lsem("wT_done"), lsem("wT_out"), lsem("o_done"), lsem("o_out")
        o_normed, oT_done, oT_out = lsem("o_normed"), lsem("oT_done"), lsem("oT_out")
        bu_done, bu_read = lsem("bu_done"), lsem("bu_read")
        s_ready, y_done, y_read = lsem("s_ready"), lsem("y_done"), lsem("y_read")
        z_in, z_out, glu_out, yssm_ready = lsem("z_in"), lsem("z_out"), lsem("glu_out"), lsem("yssm_ready")
        proj_read = lsem("proj_read")
        res_read = lsem("res_read")
        logit_done, sel_ready, cum_done = lsem("logit_done"), lsem("sel_ready"), lsem("cum_done")
        blank_pair = lsem("blank_pair")
        passes_pe, passes_act, passes_sp = sem("passes_pe"), sem("passes_act"), sem("passes_sp")
        silu_out, hid_ready = sem("silu_out"), sem("hid_ready")
        hT_done, hT_out = sem("hT_done"), sem("hT_out")
        pgT_done, pgT_out = sem("pgT_done"), sem("pgT_out")
        gather_done, xe_out, onehot_ready, weighted_ready = (
            sem("gather_done"), sem("xe_out"), sem("onehot_ready"), sem("weighted_ready"))
        ye_out = sem("ye_out")
        scat_done, scat_read = sem("scat_done"), sem("scat_read")
        rank_moved, layer_out, final_g_ready = sem("rank_moved"), sem("layer_out"), sem("final_g_ready")
        angle_ready, sine_ready = sem("angle_ready"), lsem("sine_ready")
        final_in, final_out = sem("final_in"), sem("final_out")

        units = mixer_units()

        def unit(u):
            v = ring[:, u, :] if u < UNITS else arena[:, u - UNITS, :]
            return v.rearrange("p (k n) -> p k n", n=W)

        def mixer_fill(i, l, p0):
            return l * MIX_FILLS + p0 * PAIRS + i // UNITS

        def pair_fill(u, l, g):
            return (l + 1) * MIX_FILLS + g if u < UNITS else g

        def used_in_mixer(eng, i, l, p0):
            eng.wait_ge(unit_used[i % UNITS], mixer_fill(i, l, p0) + 2)

        def used_in_pair(eng, u, l, g):
            eng.wait_ge(unit_used[u], pair_fill(u, l, g) + 2)

        def doubling(eng, tc, tsn, n, power, t0, t1, j0, nj):
            er = pre[:, j0:j0 + nj, power, 0].unsqueeze(2).to_broadcast([P, nj, n])
            ei = pre[:, j0:j0 + nj, power, 1].unsqueeze(2).to_broadcast([P, nj, n])
            c, s = tc[:, :, 0:n], tsn[:, :, 0:n]
            yield eng.tensor_tensor(t0, c, er, ALU.mult)
            yield eng.tensor_tensor(t1, s, ei, ALU.mult)
            yield eng.tensor_tensor(tc[:, :, n:2 * n], t0, t1, ALU.subtract)
            yield eng.tensor_tensor(t0, c, ei, ALU.mult)
            yield eng.tensor_tensor(t1, s, er, ALU.mult)
            yield eng.tensor_tensor(tsn[:, :, n:2 * n], t0, t1, ALU.add)

        rotors = ((tcos[:, :, :], tsin[:, :, :]), tuple(stage[:, t, :].rearrange("p (j s) -> p j s", s=SEQ) for t in range(2)))

        block = ctx.enter_context(nc.Block())

        @block.gpsimd
        def _(pool):
            for v in (bnat, cdup, wa, wx):
                ins = pool.memset(v[:], 0.0)
            ins.then_inc(blocks_zeroed, 1)
            with pool.Fori(0, DEPTH) as l:
                steps = [0]

                def after(ins):
                    steps[0] += 1
                    ins.then_inc(pool_step, 1)
                    pool.wait_ge(pool_step, steps[0])

                pool.wait_ge(rotor_base, l + 1)
                for k in range(1, 4):
                    if k >= 2:
                        pool.wait_ge(rotor_used, l * 2 + k - 1)
                    pool.sem_inc(paced, 1)
                    tc, tsn = rotors[k % 2]
                    after(pool.tensor_copy(tc[:, :, 0:32], bcos[:, 4 * k:4 * k + 4, :]))
                    after(pool.tensor_copy(tsn[:, :, 0:32], bsin[:, 4 * k:4 * k + 4, :]))
                    for n in (5, 6, 7):
                        nj = min(4, SEQ >> n)
                        for j in range(0, 4, nj):
                            t0, t1 = (rotor_tmp[:, r, 0:nj << n].rearrange("p (j n) -> p j n", j=nj) for r in range(2))
                            for ins in doubling(pool, tc[:, j:j + nj], tsn[:, j:j + nj], 1 << n, n, t0, t1, 4 * k + j, nj):
                                after(ins)
                    pool.sem_inc(rotor_ready, 1)
                pool.sem_clear(pool_step)
                pool.wait_ge(router_over, 3)
                pool.sem_clear(router_over)
                for s in layer_sems:
                    pool.sem_clear(s)
                pool.sem_inc(cleared, 1)

        @block.sync
        def _(sp):
            w_in = a["w_in"].rearrange("l (kh k p) n -> l kh p k n", kh=2, p=P)
            w_out = a["w_out"].rearrange("l (kh k p) n -> l kh p k n", kh=2, p=P)
            proj = [a[n].rearrange("l (k p) n -> l p k n", p=P) for n in ("proj_rnn", "proj_attn", "proj_ssm")]
            glu = a["ssm_glu_w"].rearrange("l (h k p) n -> l h p k n", h=2, p=P)
            w1 = a["expert_w1"].rearrange("l g e (kh k p) f -> (l g e) kh p k f", kh=2, p=P)
            w3 = a["expert_w3"].rearrange("l g e (kh k p) f -> (l g e) kh p k f", kh=2, p=P)
            w2 = a["expert_w2"].rearrange("l g e (k p) n -> (l g e) p k n", p=P)

            def one(ap, l):
                v = ap[ds(l, 1)]
                names = " ".join("bcdef"[:len(v.shape) - 1])
                return v.rearrange(f"a {names} -> (a {names.split()[0]}) {' '.join(names.split()[1:])}")

            sp.dma_start(cst[:, :], consts).then_inc(x_loaded, 16)
            sp.dma_start(x[:, :, :], a["x"].rearrange("b (t p) d -> (b p) t d", p=P)).then_inc(x_loaded, 16)
            with nc.allow_non_contiguous_dma(reason="one position per partition"):
                sp.dma_start(pos_i[:, :], a["positions"].rearrange("b (t p) -> (b p) t", p=P)).then_inc(pos_ready, 16)
            sp.dma_start(notreset[:, :].bitcast(I32), a["positions"].to_broadcast([P, SEQ])).then_inc(pos_ready, 16)
            sp.wait_ge(zeroed, 1)

            with sp.Fori(0, DEPTH) as l:
                p0 = sp.value_load(passes[0:1, 0:1], min_val=0, max_val=MAX_PASSES * DEPTH)

                loads = [0]

                def load(dst, src):
                    loads[0] += 1
                    sp.dma_start(dst, src).then_inc(params_ready, 16)

                def rows(r, name, n):
                    v = a[name][ds(l, 1)]
                    names = "b c d"[:2 * len(v.shape) - 3]
                    sp.dma_start(raw[r:r + n, :], v.rearrange(f"a {names} -> (a {names})").rearrange("(n p) -> n p", p=P))\
                      .then_inc(rows_ready, 16)

                def fill(u, before, src, hold=False):
                    sp.wait_ge(unit_used[u], before + 1)
                    if hold:
                        sp.sem_inc(paced, 1)
                    src = src.rearrange("a p k n -> (a p) k n")
                    sp.dma_start(unit(u)[:, 0:src.shape[1], :], src).then_inc(ring_ready[u], 16)

                def mixer_units_from(first, end):
                    for i in range(first, end):
                        name, b, c = units[i]
                        if name == "in":
                            src = w_in[ds(l, 1), c, :, :, b:b + W]
                        elif name == "proj":
                            src = proj[b][ds(l, 1), :, :, c * W:(c + 1) * W]
                        elif name == "glu":
                            src = glu[ds(l, 1), b]
                        else:
                            src = w_out[ds(l, 1), c, :, :, b * W:(b + 1) * W]
                        fill(i % UNITS, mixer_fill(i, l, p0), src, hold=(i == 0))

                with nc.allow_non_contiguous_dma(reason="small parameters"):
                    sp.dma_start(ldt[:, :], a["ssm_log_dt"][ds(l, 1)].rearrange("a (j h) -> (a j) h", h=2))\
                      .then_inc(rows_ready, 16)
                    for row in PARAM_ROWS:
                        rows(*row)
                mixer_units_from(0, UNITS)
                sp.wait_ge(blocks_zeroed, 1)
                with nc.allow_non_contiguous_dma(reason="small parameters"):
                    for n, name in enumerate(("ssm_b_re", "ssm_b_im")):
                        b = a[name][ds(l, 1)].rearrange("a (j h) n i -> (a h) n j i", h=2)
                        for h in range(2):
                            load(bnat[NS * h:NS * h + NS, n, :, GI * h:GI * h + GI], b[h])
                    for n, name in enumerate(("ssm_c_re", "ssm_c_im")):
                        c = a[name][ds(l, 1)].rearrange("a (k j h) i n -> (a j) h i k n", k=KW, h=2)
                        for j in range(4):
                            for h in range(2):
                                r = 32 * j + GI * h
                                load(cdup[r:r + GI, n, :, NS * h:NS * h + NS], c[j, h])
                    for t, name in ((wa, "rg_wa"), (wx, "rg_wx")):
                        g = a[name][ds(l, 1)].rearrange("a (k h) i j -> (a h) i k j", h=2)
                        for h in range(2):
                            load(t[64 * h:64 * h + 64, :, 64 * h:64 * h + 64], g[h])
                    for n, name in enumerate(("lam_q1", "lam_k1", "lam_q2", "lam_k2")):
                        load(lamv[:, n, :], a[name][ds(l, 1)].to_broadcast([P, HD]))
                    load(rbias[:, 0:4], a["router_coarse_b"][ds(l, 1)].to_broadcast([P, 4]))
                    load(rbias[:, 4:36], a["router_fine_b"][ds(l, 1)].to_broadcast([P, NEXP]))
                    load(rw[:, :, 0:4], a["router_coarse_w"][ds(l, 1)].rearrange("a (k p) n -> (a p) k n", p=P))
                    load(rw[:, :, 4:36], a["router_fine_w"][ds(l, 1)].rearrange("a (k p) n -> (a p) k n", p=P))
                assert loads[0] == N_PARAMS, loads[0]

                mixer_units_from(UNITS, MIX_UNITS)

                def fill_pair(p, i):
                    g = p * PAIRS + i
                    u = 0
                    for w in (w1, w3):
                        for kh in range(2):
                            for e in range(2):
                                if u == UNITS:
                                    sp.wait_ge(arena_free, l + 1)
                                    sp.sem_inc(paced, 1)
                                fill(u, pair_fill(u, l, g), w[ds(l * NEXP + i * 2 + e, 1), kh])
                                u += 1
                    for h in range(2):
                        for e in range(2):
                            fill(u, pair_fill(u, l, g), w2[ds(l * NEXP + i * 2 + e, 1), :, :, h * W:(h + 1) * W])
                            u += 1

                with sp.Fori(0, PAIRS) as i:
                    fill_pair(p0, i)
                sp.wait_ge(passes_sp, 1)
                sp.sem_clear(passes_sp)
                p1 = sp.value_load(passes[0:1, 0:1], min_val=0, max_val=MAX_PASSES * DEPTH)
                with sp.If(p0 + 1 < p1):
                    with sp.Fori(p0 + 1, p1) as p:
                        with sp.Fori(0, PAIRS) as i:
                            fill_pair(p, i)

            sp.wait_ge(layer_out, 2 * DEPTH + 2)
            sp.dma_start(final_g, a["final_norm_g"].to_broadcast([P, D])).then_inc(final_g_ready, 16)
            sp.wait_ge(out_ready, 1)
            sp.dma_start(out.rearrange("b (t p) d -> (b p) t d", p=P), stage[:, :, :]).then_inc(stored, 16)
            sp.wait_ge(stored, 16)

        @block.tensor
        def _(pe):
            for u in range(PAIR_UNITS):
                pe.nop().then_inc(unit_used[u], 1)
            pe.wait_ge(x_loaded, 32)
            pe.wait_ge(zeroed, 1)

            with pe.Fori(0, DEPTH) as l:
                p0 = pe.value_load(passes[0:1, 0:1], min_val=0, max_val=MAX_PASSES * DEPTH)
                pe.wait_ge(cleared, l + 1)

                def turn_x(k0, k1):
                    for k in range(k0, k1):
                        for t in range(TT):
                            mm = pe.transpose(ps[:, k // 2, (k % 2) * SEQ + t * P:(k % 2) * SEQ + (t + 1) * P],
                                              x[:, t, k * P:(k + 1) * P], ident)
                    return mm

                def spread_rms(n):
                    pe.wait_ge(diag_ready, n)
                    pe.wait_ge(xe_out, (l + 1) + p0 * PAIRS)
                    pe.matmul(ps[:, 4, 0:SEQ], ones[:, :], attn_w[:, :], start=True, stop=True).then_inc(row_done, 1)

                for h in range(2):
                    pe.wait_ge(layer_out, l * 2 + (h + 1))
                    mm = turn_x(h * KD // 2, (h + 1) * KD // 2)
                mm.then_inc(x_turned, 1)
                pe.wait_ge(raw_dt, 1)
                pe.transpose(ps[:, 6, 0:R_ROWS], raw[0:R_ROWS, :], ident[0:R_ROWS, 0:R_ROWS]).then_inc(param_cols, 1)
                spread_rms(1)

                def turn_bc():
                    pe.wait_ge(params_ready, (l + 1) * (16 * N_PARAMS))
                    for n in range(2):
                        for k in range(KW):
                            v = bnat[:, n, 4 * k:4 * k + 4, :].rearrange("p j c -> p (j c)")
                            mm = pe.transpose(ps[:, 4 + n, k * P:(k + 1) * P], v, ident)
                    mm.then_inc(b_turned, 1)
                    pe.wait_ge(col_copied, 1)
                    for n in range(2):
                        for k in range(KW):
                            mm = pe.transpose(ps[:, 6 + n, k * P:(k + 1) * P], cdup[:, n, k, :], ident)
                    mm.then_inc(c_turned, 1)

                def unit_ready(i):
                    pe.wait_ge(ring_ready[i % UNITS], (mixer_fill(i, l, p0) + 1) * 16)

                def in_part(c, kh, t):
                    i = 2 * c + kh
                    if t == 0:
                        if kh == 0 and c >= 2:
                            pe.wait_ge(chunk_out, c - 1)
                        unit_ready(i)
                    for k in range(4):
                        kk = 4 * kh + k
                        mm = pe.matmul(ps[:, 2 * (c % 2) + t, :], xT[:, kk, t * P:(t + 1) * P], unit(i % UNITS)[:, k, :],
                                       start=(kk == 0), stop=(kk == KD - 1))
                    if t == TT - 1:
                        mm.then_inc(unit_used[i % UNITS], 1)

                def in_half(c, kh):
                    for t in range(TT):
                        in_part(c, kh, t)

                def weights_first(bank, wt, m, k, yT, kk, last):
                    return pe.matmul(ps[:, bank + m // 2, (m % 2) * SEQ:(m % 2 + 1) * SEQ], wt[:, k, m * P:(m + 1) * P],
                                     yT[:, kk, :], start=(kk == 0), stop=(kk == last))

                def tile_T(c, m, bank):
                    for k in range(KD):
                        if c == 0 and m == 0 and k % 4 == 0:
                            pe.wait_ge(xT_ready, 1 + k // 4)
                        i = 2 * c + k // 4
                        mm = weights_first(bank, unit(i % UNITS), m, k % 4, xT, k, KD - 1)
                        if m == KW - 1 and k % 4 == 3:
                            mm.then_inc(unit_used[i % UNITS], 1)
                    return mm

                def in_half_T(c, h):
                    if h == 0:
                        if c >= 2:
                            pe.wait_ge(chunk_out, c - 1)
                        unit_ready(2 * c)
                        unit_ready(2 * c + 1)
                    for m in (2 * h, 2 * h + 1):
                        tile_T(c, m, 2 * (c % 2))

                def late_part(q):
                    c, m = LATE + q // KW, q % KW
                    j = q // 2
                    if m % 2 == 0:
                        if j < 2:
                            pe.wait_ge(chunk_out, LATE - 1 + LATE % 2)
                        else:
                            pe.wait_ge(late_out, j - 1)
                    if m == 0:
                        unit_ready(2 * c)
                        unit_ready(2 * c + 1)
                    mm = tile_T(c, m, 0)
                    if m == 1:
                        mm.then_inc(late_done, 1)

                def turn_chunk(n):
                    if n == 0:
                        pe.wait_ge(rope_ready, 1)
                        pe.wait_ge(bu_read, 2)
                    else:
                        pe.wait_ge(turn_copied, n)
                    for k in range(KW):
                        for t in range(TT):
                            mm = pe.transpose(ps[:, 6 + k // 2, (k % 2) * SEQ + t * P:(k % 2) * SEQ + (t + 1) * P],
                                              qkv[:, t, n * W + k * P:n * W + (k + 1) * P], ident)
                    mm.then_inc(turned, 1)

                def rgate(n, wt):
                    if n == 0:
                        pe.wait_ge(conv_ready, 1)
                        pe.wait_ge(b_copied, 1)
                    else:
                        pe.wait_ge(c_copied, 1)
                    for k in range(KW):
                        mm = pe.matmul(ps[:, 4 + 2 * n + k // 2, (k % 2) * SEQ:(k % 2 + 1) * SEQ], wt[:, k, :],
                                       work[:, 0, k * SEQ:(k + 1) * SEQ], start=True, stop=True)
                    mm.then_inc(rgate_done, 1)

                def scores(n):
                    h, t = divmod(n, TT)
                    if n == 0:
                        pe.wait_ge(turn_copied, 2)
                        pe.wait_ge(bu_read, 4)
                    else:
                        pe.wait_ge(prob_in, n)
                    for c in range(2):
                        mm = pe.matmul(ps[:, 6 + c, 0:(t + 1) * P], qT[64 * c:64 * c + 64, h, t * P:(t + 1) * P],
                                       kT[64 * c:64 * c + 64, h, 0:(t + 1) * P], start=True, stop=True)
                    mm.then_inc(score_done, 1)

                def turn_w(n):
                    h, t = divmod(n, TT)
                    if n == 0:
                        pe.wait_ge(chunk_out, LATE)
                    pe.wait_ge(w_ready, n + 1)
                    for k in range(t + 1):
                        mm = pe.transpose(ps[:, 2, k * P:(k + 1) * P], attn_w[:, k * P:(k + 1) * P], ident)
                    mm.then_inc(wT_done, 1)

                def attend(n):
                    h, t = divmod(n, TT)
                    pe.wait_ge(wT_out, n + 1)
                    if n >= 1:
                        pe.wait_ge(o_out, n)
                    for k in range(t + 1):
                        mm = pe.matmul(ps[:, 3, 0:P], attn_wT[:, k, :], qkv[:, k, 2 * W + h * P:2 * W + (h + 1) * P],
                                       start=(k == 0), stop=(k == t))
                    mm.then_inc(o_done, 1)

                def bu(m):
                    bank = BU_BANK[m]
                    if m == 0:
                        pe.wait_ge(rgate_out, 1)
                        pe.wait_ge(chunk_out, 2)
                    elif m == 1:
                        pe.wait_ge(rgate_out, 2)
                    elif m == 3:
                        pe.wait_ge(turn_copied, 2)
                    else:
                        pe.wait_ge(bu_read, m if m > 4 else m - 1)
                        pe.wait_ge(y_read, m // 2)
                    for n in range(2):
                        for j in (2 * m, 2 * m + 1):
                            k, q = divmod(j, 4)
                            mm = pe.matmul(ps[:, bank + j % 2, n * SEQ:(n + 1) * SEQ], bmat[32 * q:32 * q + 32, n, k, :],
                                           uT[32 * q:32 * q + 32, k, :], start=True, stop=True)
                    mm.then_inc(bu_done, 1)

                def cy(k):
                    pe.wait_ge(s_ready, k + 1)
                    for q in range(4):
                        j = 4 * k + q
                        for n, (cm, w) in enumerate(((0, 0), (1, 1), (2, 2), (2, 3))):
                            mm = pe.matmul(ps[32 * q:32 * q + 32, 4, 0:SEQ], ccoef[:, cm, j, :],
                                           work[:, w, q * SEQ:(q + 1) * SEQ], start=(n == 0), stop=(n == 3))
                    mm.then_inc(y_done, 1)

                def project(b, yT, halves):
                    for h in halves:
                        i = PROJ_UNIT[b] + h
                        n = 2 * b + h
                        if n == 0:
                            pe.wait_ge(late_out, 2 * (12 - LATE))
                        if n == 1:
                            pe.wait_ge(o_out, 2 * HEADS)
                        if n >= 2:
                            pe.wait_ge(proj_read, n - 1)
                        unit_ready(i)
                        for m in range(KW):
                            for k in range(KW):
                                mm = weights_first(2 * (n % 2), unit(i % UNITS), m, k, yT, k, KW - 1)
                        mm.then_inc(unit_used[i % UNITS], 1)

                in_half_T(0, 0)
                in_half_T(0, 1)
                turn_bc()
                in_half_T(1, 0)
                in_half_T(1, 1)
                rgate(0, wa)
                rgate(1, wx)
                in_half(2, 0)
                bu(0)
                in_half(2, 1)
                bu(1)
                in_half(3, 0)
                in_half(3, 1)
                in_half_T(4, 0)
                in_half_T(4, 1)
                in_half(5, 0)
                in_half(5, 1)
                turn_chunk(0)
                in_half_T(6, 0)
                turn_chunk(1)
                cy(0)
                bu(2)
                in_half_T(6, 1)
                bu(3)
                late_part(0)
                late_part(1)
                scores(0)
                late_part(2)
                late_part(3)
                cy(1)
                scores(1)
                late_part(4)
                for n in range(2 * HEADS):
                    late_part(EARLY + 2 * n)
                    turn_w(n)
                    if n + 2 < 2 * HEADS:
                        scores(n + 2)
                    if n % 4 < 2:
                        bu(4 + n // 4 * 2 + n % 4)
                    elif n == 3:
                        cy(2)
                    if n + 1 < 2 * HEADS:
                        late_part(EARLY + 2 * n + 1)
                    attend(n)
                cy(3)
                pe.wait_ge(yrnn_ready, 1)
                project(0, grT, (0, 1))
                pe.wait_ge(o_normed, 1)
                for h in range(HEADS):
                    for t in range(TT):
                        mm = pe.transpose(ps[:, 6 + h // 2, (h % 2) * SEQ + t * P:(h % 2) * SEQ + (t + 1) * P],
                                          attn_o[:, t, h * P:(h + 1) * P], ident)
                mm.then_inc(oT_done, 1)
                pe.wait_ge(z_out, 1)
                unit_ready(GLU_UNIT)
                unit_ready(GLU_UNIT + 1)
                for m in range(KW):
                    for k in range(KW):
                        u = (GLU_UNIT + k // 2) % UNITS
                        mm = pe.matmul(ps[:, 4 + m // 2, (m % 2) * SEQ:(m % 2 + 1) * SEQ],
                                       unit(u)[:, k % 2, m * P:(m + 1) * P], zT[:, k, :], start=(k == 0), stop=(k == KW - 1))
                        if m == KW - 1 and k % 2 == 1:
                            mm.then_inc(unit_used[u], 1)
                pe.wait_ge(oT_out, 1)
                project(1, qT, (0, 1))
                pe.wait_ge(yssm_ready, 1)
                project(2, uT, (0, 1))
                def out_half(h, kh):
                    i = OUT_UNIT + 2 * h + kh
                    pe.wait_ge(proj_read, 5 + kh)
                    unit_ready(i)
                    wt = unit(i % UNITS)
                    for t in range(TT):
                        for k in range(4):
                            kk = 4 * kh + k
                            mm = pe.matmul(ps[:, 2 * h + t, :], xT[:, kk, t * P:(t + 1) * P], wt[:, k, :],
                                           start=(kk == 0), stop=(kk == KD - 1))
                    mm.then_inc(unit_used[i % UNITS], 1)

                def logits(h):
                    pe.wait_ge(xT_ready, 3 + h)
                    for t in range(TT):
                        for k in range(4 * h, 4 * h + 4):
                            mm = pe.matmul(ps[:, 6 + t, 0:36], xT[:, k, t * P:(t + 1) * P], rw[:, k, :],
                                           start=(k == 0), stop=(k == KD - 1))
                    return mm

                out_half(0, 0)
                out_half(0, 1)
                out_half(1, 0)
                pe.wait_ge(res_read, 1)
                turn_x(0, KD // 2).then_inc(x_turned, 1)
                out_half(1, 1)
                logits(0)
                pe.wait_ge(res_read, 2)
                turn_x(KD // 2, KD).then_inc(x_turned, 1)
                logits(1).then_inc(logit_done, 1)

                pe.wait_ge(sel_ready, 1)
                sel = ro[:, 0, :, :]
                tri = cst[:, C_TRI:C_TRI + P]
                pe.matmul(ps[:, 7, 0:32], tri, sel[:, 0, :], start=True, stop=True)
                pe.matmul(ps[:, 7, 32:64], ones[:, :], sel[:, 0, :], start=True, stop=False)
                pe.matmul(ps[:, 7, 32:64], tri, sel[:, 1, :], start=False, stop=True)
                pe.matmul(ps[:, 7, 64:96], ones[:, :], sel[:, 0, :], start=True, stop=False)
                pe.matmul(ps[:, 7, 64:96], ones[:, :], sel[:, 1, :], start=False, stop=True).then_inc(cum_done, 1)

                def gather(ready):
                    pe.wait_ge(onehot_ready, ready)
                    pe.wait_ge(xe_out, ready)
                    for k in range(KD):
                        for t in range(TT):
                            mm = pe.matmul(ps[:, 4 + k // 4, (k % 4) * P:(k % 4 + 1) * P], stage[:, t, k * P:(k + 1) * P],
                                           onehot[:, t, :], start=(t == 0), stop=(t == TT - 1))
                    mm.then_inc(gather_done, 1)

                def scatter(g):
                    for n in range(2 * TT):
                        h, t = divmod(n, TT)
                        pe.wait_ge(scat_read, g * (2 * TT) + n + 1)
                        pe.matmul(ps[:, 7 - n % 2, :], pgT[:, t * P:(t + 1) * P], ye[:, h * W:(h + 1) * W],
                                  start=True, stop=True).then_inc(scat_done, 1)

                pe.wait_ge(xn_ready, 1)
                gather((l + 1) + p0 * PAIRS)
                pe.wait_ge(blank_pair, 1)
                pe.wait_ge(passes_pe, 1)
                pe.sem_clear(passes_pe)
                pe.nop().then_inc(router_over, 1)
                p1 = pe.value_load(passes[0:1, 0:1], min_val=0, max_val=MAX_PASSES * DEPTH)
                with pe.Fori(p0, p1) as p:
                    with pe.Fori(0, PAIRS) as i:
                        g = p * PAIRS + i
                        pe.wait_ge(xe_out, g + (l + 2))
                        u = 0
                        for n in range(2):
                            for kh in range(2):
                                for e in range(2):
                                    pe.wait_ge(ring_ready[u + e], (pair_fill(u + e, l, g) + 1) * 16)
                                for k in range(4):
                                    kk = 4 * kh + k
                                    for e in range(2):
                                        wt = unit(u + e)
                                        mm = pe.matmul(ps[64 * e:64 * e + 64, n, :], xe[:, kk, 64 * e:64 * e + 64], wt[:, k, :],
                                                       start=(kk == 0), stop=(kk == KD - 1))
                                        if k == 3:
                                            mm.then_inc(unit_used[u + e], 1)
                                u += 2
                        pe.wait_ge(ye_out, g + 1)
                        pe.wait_ge(pgT_out, g + 1)
                        scatter(g + l)
                        pe.wait_ge(hid_ready, g + 1)
                        pe.wait_ge(scat_read, (g + l + 1) * (2 * TT) + 2)
                        for f in range(4):
                            mm = pe.transpose(ps[:, 6, f * P:(f + 1) * P], hid[:, f * P:(f + 1) * P], ident)
                        mm.then_inc(hT_done, 1)
                        pe.wait_ge(weighted_ready, g + (l + 1))
                        for t in range(TT):
                            mm = pe.transpose(ps[:, 7, t * P:(t + 1) * P], weighted[:, t, :], ident)
                        mm.then_inc(pgT_done, 1)
                        gather(g + (l + 2))
                        pe.wait_ge(hT_out, g + 1)
                        for h in range(2):
                            for e in range(2):
                                pe.wait_ge(ring_ready[u + e], (pair_fill(u + e, l, g) + 1) * 16)
                            for k in range(4):
                                for e in range(2):
                                    wt = unit(u + e)
                                    mm = pe.matmul(ps[64 * e:64 * e + 64, 2 + h, :], hT[:, k, 64 * e:64 * e + 64], wt[:, k, :],
                                                   start=(k == 0), stop=(k == 3))
                                    if k == 3:
                                        mm.then_inc(unit_used[u + e], 1)
                            u += 2
                pe.wait_ge(ye_out, p1 * PAIRS + 1)
                pe.wait_ge(pgT_out, p1 * PAIRS + 1)
                scatter(p1 * PAIRS + l)

        @block.scalar
        def _(act):
            act.wait_ge(x_loaded, 32)
            act.wait_ge(zeroed, 1)

            act.nop().then_inc(xe_out, 1)
            act.nop().then_inc(ye_out, 1)
            act.nop().then_inc(pgT_out, 1)

            with act.Fori(0, DEPTH) as l:
                p0 = act.value_load(passes[0:1, 0:1], min_val=0, max_val=MAX_PASSES * DEPTH)
                act.wait_ge(cleared, l + 1)
                steps = [0]

                def after(ins):
                    steps[0] += 1
                    ins.then_inc(act_step, 1)
                    act.wait_ge(act_step, steps[0])

                def squares(c0, c1, s):
                    for t in range(TT):
                        after(act.activation(work[:, 3, c0:c1], x[:, t, c0:c1], ACT.Square,
                                             accum_out=small[:, s + t:s + t + 1]))

                def root(v, m):
                    act.wait_ge(var_ready, m)
                    act.activation(v, v, ACT.Sqrt).then_inc(root_ready, 1)

                for h in range(2):
                    act.wait_ge(layer_out, l * 2 + (h + 1))
                    squares(h * W, (h + 1) * W, 6 * h)
                act.nop().then_inc(ss_ready, 1)
                root(small[:, 2:4], 1)
                act.wait_ge(param_cols, 1)
                after(act.activation(col[:, 0:R_ROWS], ps[:, 6, 0:R_ROWS], ACT.Copy))
                act.nop().then_inc(col_copied, 1)

                def serve(m, v, f):
                    act.wait_ge(fn_asked, m + 1)
                    act.activation(v, v, f).then_inc(fn_served, 1)

                serve(0, small[:, 20:40], ACT.Tanh)
                serve(1, s5[:, 0, :], ACT.Tanh)
                serve(2, s5[:, 3:5, :], ACT.Sin)
                act.wait_ge(angle_ready, 1)
                act.activation(rsn[:, :, :], angles[:, 0, :, :], ACT.Sin).then_inc(sine_ready, 1)
                act.activation(rc[:, :, :], angles[:, 1, :, :], ACT.Sin).then_inc(sine_ready, 1)

                def chunk(c):
                    used_in_mixer(act, 2 * c + 1, l, p0)
                    src, f = ps[:, 2 * (c % 2):2 * (c % 2) + 2, :], ACT.Copy
                    if c in (2, 3, 5):
                        n = (2, 3, 5).index(c)
                        dst = qkv[:, :, n * W:(n + 1) * W]
                    else:
                        src = src.rearrange("p b (k s) -> p (b k) s", s=SEQ)
                        if c == 4:
                            dst, f = grT[:, :, :], ACT.Gelu_apprx_tanh
                        elif c < 2:
                            dst = (xrT[:, :, 3:], uT[:, :, :])[c]
                        else:
                            dst, f = gatesT[:, (c - 6) * KW:(c - 5) * KW, :], ACT.Sigmoid
                    act.activation(dst, src, f).then_inc(chunk_out, 1)

                def turn_copy(n, dst):
                    act.wait_ge(turned, n + 1)
                    act.activation(dst, ps[:, 6:8, :].rearrange("p b (k s) -> p (b k) s", s=SEQ), ACT.Copy)\
                       .then_inc(turn_copied, 1)

                chunk(0)
                act.wait_ge(b_turned, 1)
                for n in range(2):
                    after(act.activation(bmat[:, n, :, :].rearrange("p k c -> p (k c)"), ps[:, 4 + n, :], ACT.Copy))
                act.nop().then_inc(b_copied, 1)
                act.wait_ge(c_turned, 1)
                after(act.activation(work[:, 0, :], ps[:, 6:8, :].rearrange("p b n -> p (b n)"), ACT.Copy))
                act.nop().then_inc(c_copied, 1)
                chunk(1)
                for n in range(2):
                    act.wait_ge(rgate_done, n + 1)
                    for k in range(KW):
                        b = (R_BA, R_BX)[n] + k
                        after(act.activation(work[:, 1 + n, k * SEQ:(k + 1) * SEQ],
                                             ps[:, 4 + 2 * n + k // 2, (k % 2) * SEQ:(k % 2 + 1) * SEQ], ACT.Sigmoid,
                                             bias=col[:, b:b + 1]))
                    act.nop().then_inc(rgate_out, 1)
                act.wait_ge(sp_ready, 1)
                for k in range(KW):
                    after(act.activation(work[:, 1, k * SEQ:(k + 1) * SEQ], work[:, 1, k * SEQ:(k + 1) * SEQ], ACT.Tanh,
                                         scale=small[:, 44 + k:45 + k]))
                after(act.activation(work[:, 3, :], work[:, 1, :], ACT.Sqrt))
                act.nop().then_inc(rg_root, 1)
                chunk(2)
                serve(3, small[:, 86:88], ACT.Exp)
                chunk(3)
                chunk(4)
                turn_copy(0, qT[:, :, :])
                chunk(5)
                turn_copy(1, kT[:, :, :])
                chunk(6)

                def exponentials(n):
                    t = n % TT
                    act.wait_ge(prob_in, n + 1)
                    e, r = attn_e[:, n % 2], A_SMALL[n % 2]
                    for c in range(2):
                        ins = act.activation(e[:, c, 0:(t + 1) * P], e[:, c, 0:(t + 1) * P], ACT.Exp,
                                             bias=small[:, r + c:r + c + 1], scale=HD ** -0.5,
                                             accum_out=small[:, r + 2 + c:r + 3 + c])
                        after(ins)
                    act.nop().then_inc(prob_ready, 1)

                def late_chunk(j):
                    c, mh = LATE + j // 2, j % 2
                    if mh == 0:
                        act.wait_ge(late_done, j // 2 + 1)
                    else:
                        used_in_mixer(act, 2 * c + 1, l, p0)
                    k = (c - 6) * KW + 2 * mh
                    act.activation(gatesT[:, k:k + 2, :], ps[:, j % 2, :].rearrange("p (k s) -> p k s", s=SEQ),
                                   ACT.Sigmoid).then_inc(late_out, 1)

                for j in range(EARLY // 2):
                    late_chunk(j)
                exponentials(0)
                for n in range(2 * HEADS):
                    h, t = divmod(n, TT)
                    if n + 1 < 2 * HEADS:
                        exponentials(n + 1)
                    act.wait_ge(wT_done, n + 1)
                    act.activation(attn_wT[:, 0:t + 1, :], ps[:, 2, 0:(t + 1) * P].rearrange("p (k s) -> p k s", s=P),
                                   ACT.Copy).then_inc(wT_out, 1)
                    late_chunk(EARLY // 2 + n)
                    act.wait_ge(o_done, n + 1)
                    act.activation(attn_o[:, t, h * P:(h + 1) * P], ps[:, 3, 0:P], ACT.Copy).then_inc(o_out, 1)
                act.wait_ge(z_in, 1)
                act.activation(zT[:, :, :], zT[:, :, :], ACT.Gelu_apprx_tanh).then_inc(z_out, 1)
                root(small[:, 64:72], 2)
                act.wait_ge(oT_done, 1)
                act.activation(qT[:, :, :], ps[:, 6:8, :].rearrange("p b (k s) -> p (b k) s", s=SEQ), ACT.Copy,
                               scale=small[:, 84:85]).then_inc(oT_out, 1)
                used_in_mixer(act, GLU_UNIT + 1, l, p0)
                for m in range(KW):
                    after(act.activation(work[:, 0, m * SEQ:(m + 1) * SEQ], ps[:, 4 + m // 2, (m % 2) * SEQ:(m % 2 + 1) * SEQ],
                                         ACT.Sigmoid, bias=col[:, R_GLUB + m:R_GLUB + m + 1]))
                act.nop().then_inc(glu_out, 1)

                act.wait_ge(res_read, 1)
                squares(0, W, 0)
                act.wait_ge(x_turned, 2)
                for k in range(KD // 2):
                    after(act.activation(xT[:, k, :], ps[:, k // 2, (k % 2) * SEQ:(k % 2 + 1) * SEQ], ACT.Copy,
                                         scale=col[:, R_FFNG + k:R_FFNG + k + 1]))
                act.nop().then_inc(xT_ready, 1)
                act.wait_ge(res_read, 2)
                squares(W, D, 6)
                act.nop().then_inc(ss_ready, 1)
                root(small[:, 2:4], 3)
                act.wait_ge(fn_asked, 5)
                act.activation(ro[:, 3, :, 8:12], ro[:, 3, :, 8:12], ACT.Exp).then_inc(fn_served, 1)
                act.wait_ge(fn_asked, 6)
                act.activation(small[:, 80:82], small[:, 80:82], ACT.Exp).then_inc(fn_served, 1)

                act.wait_ge(passes_act, 1)
                act.sem_clear(passes_act)
                act.nop().then_inc(router_over, 1)
                p1 = act.value_load(passes[0:1, 0:1], min_val=0, max_val=MAX_PASSES * DEPTH)

                def gathered(n):
                    act.wait_ge(gather_done, n)
                    for k in range(KD):
                        ins = act.activation(xe[:, k, :], ps[:, 4 + k // 4, (k % 4) * P:(k % 4 + 1) * P], ACT.Copy,
                                             scale=col[:, R_FFNG + k:R_FFNG + k + 1])
                    ins.then_inc(xe_out, 1)

                gathered((l + 1) + p0 * PAIRS)
                with act.Fori(p0, p1) as p:
                    with act.Fori(0, PAIRS) as i:
                        g = p * PAIRS + i
                        used_in_pair(act, 3, l, g)
                        act.activation(sil, ps[:, 0, :], ACT.Silu).then_inc(silu_out, 1)
                        act.wait_ge(hT_done, g + 1)
                        act.activation(hT[:, :, :], ps[:, 6, :].rearrange("p (f s) -> p f s", f=4), ACT.Copy).then_inc(hT_out, 1)
                        act.wait_ge(pgT_done, g + 1)
                        act.activation(pgT, ps[:, 7, 0:SEQ], ACT.Copy).then_inc(pgT_out, 1)
                        gathered(g + (l + 2))
                        used_in_pair(act, 11, l, g)
                        act.activation(ye.rearrange("p (h n) -> p h n", h=2), ps[:, 2:4, :], ACT.Copy).then_inc(ye_out, 1)
            act.wait_ge(final_in, 1)
            for t in range(TT):
                act.activation(work[:, 3, :], x[:, t, :], ACT.Square, accum_out=small[:, t:t + 1]).then_inc(final_out, 1)
                act.wait_ge(final_out, t + 1)
            act.wait_ge(final_in, 2)
            act.activation(small[:, 2:4], small[:, 2:4], ACT.Sqrt).then_inc(final_out, 1)

        @block.vector
        def _(dve):
            steps = [0]

            def after(ins):
                steps[0] += 1
                ins.then_inc(dve_step, 1)
                dve.wait_ge(dve_step, steps[0])

            def tt(o, i0, i1, op):
                after(dve.tensor_tensor(o, i0, i1, op))

            def tsc(o, i0, s1, s2, op0, op1=None):
                after(dve.tensor_scalar(o, i0, s1, s2, op0, op1) if op1 is not None
                      else dve.tensor_scalar(o, i0, s1, None, op0))

            def stt(o, i0, s, i1, op0, op1):
                after(dve.scalar_tensor_tensor(o, i0, s, i1, op0, op1))

            MUL, ADD, SUB, MAX, MIN, EQ = ALU.mult, ALU.add, ALU.subtract, ALU.max, ALU.min, ALU.is_equal

            def reduce_angle(th, kk, c):
                tsc(kk, th, INV_2PI, MAGIC, MUL, ADD)
                tsc(kk, kk, MAGIC, None, SUB)
                for part in (PI_2A, PI_2B, PI_2C):
                    stt(th, kk, -part, th, MUL, ADD)
                tsc(th, th, -PI, PI, MAX, MIN)
                stt(c, th, -1.0, th, MUL, MAX)
                tsc(c, c, -1.0, PI / 2, MUL, ADD)

            after(dve.memset(xrT[:, :, 0:3], 0.0))
            after(dve.memset(ones[:, :], 1.0))
            after(dve.memset(passes_f[:, :], 0.0))
            after(dve.tensor_copy(passes[:, :], passes_f[:, :]))
            dve.nop().then_inc(zeroed, 1)
            dve.nop().then_inc(scat_read, 1)
            dve.nop().then_inc(scat_read, 1)
            dve.nop().then_inc(cleared, 1)
            dve.nop().then_inc(layer_out, 2)
            dve.wait_ge(x_loaded, 32)
            dve.wait_ge(pos_ready, 32)
            after(dve.tensor_copy(isreset[:, :], notreset[:, :].bitcast(I32)))
            tsc(isreset[:, :], isreset[:, :], 0.0, None, EQ)
            tsc(notreset[:, :], isreset[:, :], -1.0, None, ADD)
            after(dve.tensor_copy(small[:, 8:8 + TT], pos_i[:, :]))
            for t in range(TT):
                tsc(angles[:, 0, t, :], cst[:, C_FREQ:C_FREQ + HALF], small[:, 8 + t:9 + t], None, MUL)
            kk = attn_w[:, 0:TT * HALF].rearrange("p (t e) -> p t e", t=TT)
            reduce_angle(angles[:, 0, :, :], kk, angles[:, 1, :, :])
            dve.nop().then_inc(angle_ready, 1)
            dve.sem_clear(dve_step)

            with dve.Fori(0, DEPTH) as l:
                p0 = dve.value_load(passes[0:1, 0:1], min_val=0, max_val=MAX_PASSES * DEPTH)
                dve.wait_ge(cleared, l + 1)
                steps[0] = 0

                dve.wait_ge(rows_ready, (l + 1) * (16 * N_ROWS))
                after(dve.tensor_copy(raw[0:16, :].rearrange("j (h n) -> j h n", h=2),
                                      ldt[:, :].unsqueeze(2).to_broadcast([16, 2, NS])))
                dve.nop().then_inc(raw_dt, 1)

                def inverse_rms(n, m):
                    dve.wait_ge(ss_ready, n)
                    tt(small[:, 2:4], small[:, 0:2], small[:, 6:8], ADD)
                    tsc(small[:, 2:4], small[:, 2:4], 1.0 / D, 1e-6, MUL, ADD)
                    dve.nop().then_inc(var_ready, 1)
                    dve.wait_ge(root_ready, m)
                    after(dve.reciprocal(small[:, 4:6], small[:, 2:4]))

                def normed(n, m, g0):
                    inverse_rms(n, m)
                    for t in range(TT):
                        tsc(attn_w[:, t * P:(t + 1) * P], ident, small[:, 4 + t:5 + t], None, MUL)
                    dve.nop().then_inc(diag_ready, 1)
                    dve.wait_ge(row_done, n)
                    after(dve.tensor_copy(rms_row[:, :], ps[:, 4, 0:SEQ]))
                    dve.wait_ge(x_turned, n)
                    dve.wait_ge(col_copied, 1)
                    for k in range(KD):
                        stt(xT[:, k, :], ps[:, k // 2, (k % 2) * SEQ:(k % 2 + 1) * SEQ], col[:, g0 + k:g0 + k + 1],
                            rms_row[:, :], MUL, MUL)
                        if k % 4 == 3:
                            dve.nop().then_inc(xT_ready, 1)

                normed(1, 1, R_MIXG)

                e = small[:, 20:40]
                tsc(small[:, 20:36], col[:, R_DT:R_DT + JT], 1 / 32, None, MUL)
                tsc(small[:, 40:44], col[:, R_LAM:R_LAM + KW], -1.0, None, MUL)
                tt(small[:, 36:40], small[:, 40:44], col[:, R_LAM:R_LAM + KW], MIN)
                tsc(small[:, 36:40], small[:, 36:40], 1 / 32, None, MUL)
                dve.nop().then_inc(fn_asked, 1)
                dve.wait_ge(fn_served, 1)
                den = small[:, 100:120]
                tsc(den, e, -1.0, 1.0, MUL, ADD)
                tsc(e, e, 1.0, None, ADD)
                after(dve.reciprocal(den, den))
                tt(e, e, den, MUL)
                for _ in range(4):
                    tt(e, e, e, MUL)
                dt = small[:, 20:36]
                lr, li = col[:, R_RE:R_RE + JT], col[:, R_IM:R_IM + JT]
                Q, MAG, SN, CS, AR, AI, CR, CI, T0, T1, T2 = (s5[:, n, :] for n in (0, 1, 3, 4, 5, 6, 7, 8, 9, 10, 11))
                stt(Q, lr, -0.5, dt, MUL, MUL)
                dve.nop().then_inc(fn_asked, 1)
                tt(SN, li, dt, MUL)
                reduce_angle(SN, T0, CS)
                dve.nop().then_inc(fn_asked, 1)
                y4, z4, zz, po = small[:, 36:40], small[:, 120:124], small[:, 124:128], small[:, 128:132]
                tsc(zz, y4, 2.0, None, ADD)
                after(dve.reciprocal(zz, zz))
                tt(z4, y4, zz, MUL)
                tt(zz, z4, z4, MUL)
                tsc(po, zz, 1 / 19, 1 / 17, MUL, ADD)
                for n in (15, 13, 11, 9, 7, 5, 3, 1):
                    tt(po, po, zz, MUL)
                    tsc(po, po, 1 / n, None, ADD)
                stt(po, z4, 2.0, po, MUL, MUL)
                stt(po, small[:, 40:44], 0.0, po, MAX, ADD)
                tsc(small[:, 44:48], po, 4.0, None, MUL)
                dve.nop().then_inc(sp_ready, 1)
                tt(small[:, 84:85], col[:, R_SUB:R_SUB + 1], cst[:, ds(l + C_ONEM, 1)], MUL)
                dve.wait_ge(fn_served, 2)
                tsc(T0, Q, 1.0, None, ADD)
                after(dve.reciprocal(T0, T0))
                tsc(MAG, Q, -1.0, 1.0, MUL, ADD)
                tt(MAG, MAG, T0, MUL)
                dve.wait_ge(fn_served, 3)
                tt(AR, MAG, CS, MUL)
                tt(AI, MAG, SN, MUL)
                tt(T0, lr, lr, MUL)
                tt(T1, li, li, MUL)
                tt(T0, T0, T1, ADD)
                after(dve.reciprocal(T0, T0))
                tsc(T2, AR, -1.0, None, ADD)
                tt(CR, T2, lr, MUL)
                tt(T1, AI, li, MUL)
                tt(CR, CR, T1, ADD)
                tt(CR, CR, T0, MUL)
                tt(CI, AI, lr, MUL)
                tt(T1, T2, li, MUL)
                tt(CI, CI, T1, SUB)
                tt(CI, CI, T0, MUL)
                dve.wait_ge(params_ready, (l + 1) * (16 * N_PARAMS))
                for n in range(2):
                    tt(lamv[:, 2 * n, :], lamv[:, 2 * n, :], lamv[:, 2 * n + 1, :], MUL)
                    after(dve.tensor_reduce(small[:, 86 + n:87 + n], lamv[:, 2 * n, :], AX, ADD))
                dve.nop().then_inc(fn_asked, 1)
                dve.wait_ge(c_copied, 1)
                cre = work[:, 0, 0:512].rearrange("p (j c) -> p j c", j=JT)
                cim = work[:, 0, 512:1024].rearrange("p (j c) -> p j c", j=JT)
                crb, cib = (v.unsqueeze(2).to_broadcast([P, JT, 32]) for v in (CR, CI))
                c0, c1, c2 = (ccoef[:, n, :, :] for n in range(3))
                tt(c0, cre, crb, MUL)
                tt(c1, cim, cib, MUL)
                tt(c0, c0, c1, SUB)
                tt(c2, cre, cib, MUL)
                tt(c1, cim, crb, MUL)
                stt(c2, c2, -1.0, c1, MUL, SUB)
                tsc(c1, c0, -1.0, None, MUL)
                dve.wait_ge(chunk_out, 1)
                for k in range(KW):
                    xc = work[:, 0, k * SEQ:(k + 1) * SEQ]
                    tsc(xc, xrT[:, k, 3:3 + SEQ], col[:, R_CW + k:R_CW + k + 1], col[:, R_CB + k:R_CB + k + 1], MUL, ADD)
                    for j in range(1, 4):
                        c = R_CW + 4 * j + k
                        stt(xc, xrT[:, k, 3 - j:3 - j + SEQ], col[:, c:c + 1], xc, MUL, ADD)
                dve.nop().then_inc(conv_ready, 1)

                after(dve.tensor_copy(pre[:, :, 0, 0], CS))
                after(dve.tensor_copy(pre[:, :, 0, 1], SN))
                for n in range(7):
                    re, im = pre[:, :, n, 0], pre[:, :, n, 1]
                    tt(T0, re, re, MUL)
                    tt(T1, im, im, MUL)
                    tt(pre[:, :, n + 1, 0], T0, T1, SUB)
                    stt(pre[:, :, n + 1, 1], re, 2.0, im, MUL, MUL)

                def double(tc, tsn, n, power, t0, t1, j0, nj):
                    for ins in doubling(dve, tc, tsn, n, power, t0, t1, j0, nj):
                        after(ins)

                after(dve.memset(bcos[:, :, 0:1], 1.0))
                after(dve.memset(bsin[:, :, 0:1], 0.0))
                flat = [w.rearrange("p a b -> p (a b)") for w in (tcos[:, :, :], tsin[:, :, :])]
                for n in range(5):
                    t0, t1 = (w[:, 0:JT << n].rearrange("p (j n) -> p j n", j=JT) for w in flat)
                    double(bcos[:, :, :], bsin[:, :, :], 1 << n, n, t0, t1, 0, JT)

                def tables(k, tmp):
                    tc, tsn = rotors[k % 2]
                    after(dve.tensor_copy(tc[:, :, 0:32], bcos[:, 4 * k:4 * k + 4, :]))
                    after(dve.tensor_copy(tsn[:, :, 0:32], bsin[:, 4 * k:4 * k + 4, :]))
                    for n in (5, 6, 7):
                        t0, t1 = (tmp[:, r * 512:r * 512 + (4 << n)].rearrange("p (j n) -> p j n", j=4) for r in range(2))
                        double(tc, tsn, 1 << n, n, t0, t1, 4 * k, 4)

                def turn_in(m):
                    q = 2 * (m % 2)
                    dve.wait_ge(bu_done, m + 1)
                    bank = BU_BANK[m]
                    pr, pi = ps[:, bank:bank + 2, 0:SEQ], ps[:, bank:bank + 2, SEQ:2 * SEQ]
                    c, s = (v[:, q:q + 2, :] for v in rotors[m // 2 % 2])
                    w = [work[:, n, q * SEQ:(q + 2) * SEQ].rearrange("p (j s) -> p j s", j=2) for n in range(4)]
                    tt(w[0], pr, c, MUL)
                    tt(w[1], pi, s, MUL)
                    tt(w[2], pi, c, MUL)
                    tt(w[3], pr, s, MUL)
                    dve.nop().then_inc(bu_read, 1)

                def scans(k, n):
                    for q in range(4):
                        r = slice(q * SEQ, (q + 1) * SEQ)
                        m = MAG[:, 4 * k + q:4 * k + q + 1].to_broadcast([P, SEQ])
                        after(dve.tensor_tensor_scan(work[:, n + 1, r], m, work[:, n, r], 0.0, MUL, ADD))

                def recur_re(k):
                    tt(work[:, 0, :], work[:, 0, :], work[:, 1, :], ADD)
                    tt(work[:, 2, :], work[:, 2, :], work[:, 3, :], SUB)
                    scans(k, 0)

                def recur_im(k):
                    scans(k, 2)
                    c, s = (v.rearrange("p j s -> p (j s)") for v in rotors[k % 2])
                    tt(work[:, 0, :], work[:, 1, :], c, MUL)
                    tt(work[:, 2, :], work[:, 1, :], s, MUL)
                    tt(work[:, 1, :], work[:, 3, :], s, MUL)
                    tt(work[:, 3, :], work[:, 3, :], c, MUL)
                    dve.nop().then_inc(s_ready, 1)
                    if k < 2:
                        dve.nop().then_inc(rotor_used, 1)

                def y_out(k):
                    dve.wait_ge(y_done, k + 1)
                    stt(zT[:, k, :], uT[:, k, :], col[:, R_D + k:R_D + k + 1], ps[:, 4, 0:SEQ], MUL, ADD)
                    dve.nop().then_inc(y_read, 1)

                dve.nop().then_inc(rotor_base, 1)
                tables(0, qT[:, :, :].rearrange("p k s -> p (k s)"))

                dve.wait_ge(rg_root, 1)
                z = kT[:, :, :].rearrange("p k s -> p (k s)")
                def kws(v):
                    return v.rearrange("p (k s) -> p k s", k=KW)
                nrb = notreset[:, :].unsqueeze(1).to_broadcast([P, KW, SEQ])
                rsb = isreset[:, :].unsqueeze(1).to_broadcast([P, KW, SEQ])
                tsc(z, work[:, 1, :], 1.0, None, ADD)
                after(dve.reciprocal(z, z))
                stt(work[:, 1, :], work[:, 1, :], -1.0, z, ADD, MUL)
                tt(kws(work[:, 1, :]), kws(work[:, 1, :]), nrb, MUL)
                stt(work[:, 3, :], work[:, 3, :], -2.0, z, MUL, MUL)
                tt(kws(work[:, 3, :]), kws(work[:, 3, :]), nrb, MUL)
                tt(kws(work[:, 3, :]), kws(work[:, 3, :]), rsb, ADD)
                tt(work[:, 2, :], work[:, 2, :], work[:, 0, :], MUL)
                tt(work[:, 3, :], work[:, 3, :], work[:, 2, :], MUL)
                for k in range(KW):
                    r = slice(k * SEQ, (k + 1) * SEQ)
                    after(dve.tensor_tensor_scan(xrT[:, k, 3:], work[:, 1, r], work[:, 3, r], 0.0, MUL, ADD))

                mask = cst[:, C_MASK:C_MASK + P]

                def masked(n):
                    t = n % TT
                    dve.wait_ge(score_done, n + 1)
                    sc, e, r = ps[:, 6:8, 0:SEQ], attn_e[:, n % 2], A_SMALL[n % 2]
                    if t == 1:
                        after(dve.tensor_copy(e[:, :, 0:P], sc[:, :, 0:P]))
                    tt(e[:, :, t * P:(t + 1) * P], sc[:, :, t * P:(t + 1) * P],
                       mask.unsqueeze(1).to_broadcast([P, 2, P]), ADD)
                    after(dve.tensor_reduce(small[:, r:r + 2], e[:, :, 0:(t + 1) * P], AX, MAX))
                    tsc(small[:, r:r + 2], small[:, r:r + 2], -HD ** -0.5, None, MUL)
                    dve.nop().then_inc(prob_in, 1)

                def weights(n):
                    t = n % TT
                    e, r = attn_e[:, n % 2], A_SMALL[n % 2]
                    dve.wait_ge(prob_ready, n + 1)
                    after(dve.reciprocal(small[:, r + 4:r + 6], small[:, r + 2:r + 4]))
                    tt(small[:, r + 5:r + 6], small[:, r + 5:r + 6], small[:, 88:89], MUL)
                    if n >= 1:
                        dve.wait_ge(wT_done, n)
                    w = attn_w[:, 0:(t + 1) * P]
                    tsc(w, e[:, 0, 0:(t + 1) * P], small[:, r + 4:r + 5], None, MUL)
                    stt(w, e[:, 1, 0:(t + 1) * P], small[:, r + 5:r + 6], w, MUL, ADD)
                    dve.nop().then_inc(w_ready, 1)

                dve.wait_ge(sine_ready, 2)
                dve.wait_ge(chunk_out, 4)
                flat = work[:, 0, :], work[:, 1, :]
                for t in range(TT):
                    xx = qkv[:, t, 0:2 * W].rearrange("p (h c e) -> p h c e", c=2, e=HALF)
                    t0, t1 = (w.rearrange("p (h c e) -> p h c e", c=2, e=HALF) for w in flat)
                    cb, sbc = (v[:, t, :].unsqueeze(1).unsqueeze(1).to_broadcast([P, 4 * HEADS, 2, HALF]) for v in (rc, rsn))
                    tt(t0, xx, cb, MUL)
                    tt(t1, xx, sbc, MUL)
                    tt(xx[:, :, 0, :], t0[:, :, 0, :], t1[:, :, 1, :], SUB)
                    tt(xx[:, :, 1, :], t0[:, :, 1, :], t1[:, :, 0, :], ADD)
                dve.nop().then_inc(rope_ready, 1)

                turn_in(0)
                turn_in(1)
                recur_re(0)
                recur_im(0)
                dve.wait_ge(chunk_out, 5)
                tt(grT[:, :, :], grT[:, :, :], xrT[:, :, 3:], MUL)
                dve.nop().then_inc(yrnn_ready, 1)
                y_out(0)
                dve.wait_ge(rotor_ready, l * 3 + 1)
                turn_in(2)
                turn_in(3)
                recur_re(1)
                recur_im(1)
                dve.wait_ge(fn_served, 4)
                tt(small[:, 88:89], small[:, 87:88], small[:, 86:87], SUB)
                tt(small[:, 88:89], small[:, 88:89], cst[:, ds(l + C_LINIT, 1)], SUB)

                def s5_step(n):
                    k = 2 + n // 4
                    if n % 4 == 0:
                        dve.wait_ge(rotor_ready, l * 3 + k)
                        y_out(k - 1)
                    elif n % 4 == 1:
                        turn_in(2 * k)
                    elif n % 4 == 2:
                        turn_in(2 * k + 1)
                        recur_re(k)
                    else:
                        recur_im(k)

                masked(0)
                for n in range(2 * HEADS):
                    if n + 1 < 2 * HEADS:
                        masked(n + 1)
                    s5_step(n)
                    weights(n)
                y_out(3)
                dve.nop().then_inc(z_in, 1)

                dve.wait_ge(o_out, 2 * HEADS)
                o8 = attn_o[:, :, :].rearrange("p t (h v) -> p (t h) v", v=P)
                sq = work[:, 1, :].rearrange("p (g v) -> p g v", v=P)
                tt(sq, o8, o8, MUL)
                after(dve.tensor_reduce(small[:, 64:72], sq, AX, ADD))
                tsc(small[:, 64:72], small[:, 64:72], 1.0 / P, 1e-5, MUL, ADD)
                dve.nop().then_inc(var_ready, 1)
                dve.wait_ge(root_ready, 2)
                after(dve.reciprocal(small[:, 72:80], small[:, 64:72]))
                tt(o8, o8, small[:, 72:80].unsqueeze(2).to_broadcast([P, TT * HEADS, P]), MUL)
                dve.nop().then_inc(o_normed, 1)

                def gated(n):
                    b, h = divmod(n, 2)
                    used_in_mixer(dve, PROJ_UNIT[b] + h, l, p0)
                    bank = 2 * (n % 2)
                    gt = gatesT[:, b * KD + h * KW:b * KD + (h + 1) * KW, :]
                    mg = mT[:, h * KW:(h + 1) * KW, :]
                    prod = ps[:, bank:bank + 2, :].rearrange("p b (k s) -> p (b k) s", s=SEQ)
                    tt(mg if b == 0 else gt, prod, gt, MUL)
                    if b:
                        tt(mg if b == 1 else xT[:, h * KW:(h + 1) * KW, :], mg, gt, ADD)
                    dve.nop().then_inc(proj_read, 1)

                gated(0)
                gated(1)
                dve.wait_ge(glu_out, 1)
                tt(uT[:, :, :], zT[:, :, :], kws(work[:, 0, :]), MUL)
                dve.nop().then_inc(yssm_ready, 1)
                for n in range(2, 6):
                    gated(n)
                dve.nop().then_inc(arena_free, 1)
                for h in range(2):
                    used_in_mixer(dve, OUT_UNIT + 1 + 2 * h, l, p0)
                    tt(x[:, :, h * W:(h + 1) * W], ps[:, 2 * h:2 * h + 2, :], x[:, :, h * W:(h + 1) * W], ADD)
                    dve.nop().then_inc(res_read, 1)


                dve.wait_ge(x_turned, 3)
                for k in range(KD // 2, KD):
                    tsc(xT[:, k, :], ps[:, k // 2, (k % 2) * SEQ:(k % 2 + 1) * SEQ], col[:, R_FFNG + k:R_FFNG + k + 1],
                        None, MUL)
                dve.nop().then_inc(xT_ready, 1)
                inverse_rms(2, 3)
                dve.wait_ge(logit_done, 1)
                for t in range(TT):
                    stt(lg[:, t, :], ps[:, 6 + t, 0:36], small[:, 4 + t:5 + t], rbias[:, :], MUL, ADD)
                coarse, fine = lg[:, :, 0:4], lg[:, :, 4:36]
                m2, m3 = small[:, 90:92], small[:, 92:94]

                def first_of_max(oh, v, n):
                    io, io_less = (cst[:, c:c + n].unsqueeze(1).to_broadcast([P, TT, n]) for c in (C_I32, C_I32M))
                    after(dve.tensor_reduce(m2, v, AX, MAX))
                    tt(oh, v, m2.unsqueeze(2).to_broadcast([P, TT, n]), EQ)
                    stt(oh, oh, -64.0, io, MUL, ADD)
                    after(dve.tensor_reduce(m3, oh, AX, MIN))
                    tt(oh, io_less, m3.unsqueeze(2).to_broadcast([P, TT, n]), EQ)

                goh = ro[:, 2, :, 0:4]
                first_of_max(goh, coarse, 4)
                shares = ro[:, 3, :, 8:12]
                tt(shares, coarse, m2.unsqueeze(2).to_broadcast([P, TT, 4]), SUB)
                dve.nop().then_inc(fn_asked, 1)
                pen = ro[:, 3, :, 0:4]
                tsc(pen, goh, 1e30, -1e30, MUL, ADD)
                fm = ro[:, 4, :, :]
                fm4, fine4 = (v.rearrange("p t (g e) -> p t g e", g=4) for v in (fm, fine))
                tt(fm4, fine4, pen.unsqueeze(3).to_broadcast([P, TT, 4, 8]), ADD)
                oh1, oh2 = ro[:, 5, :, :], ro[:, 1, :, :]
                first_of_max(oh1, fm, NEXP)
                after(dve.tensor_copy(small[:, 82:84], m2))
                stt(fm, oh1, -2e30, fm, MUL, ADD)
                first_of_max(oh2, fm, NEXP)
                sel = ro[:, 0, :, :]
                tt(sel, oh1, oh2, ADD)
                dve.nop().then_inc(sel_ready, 1)
                for t in range(TT):
                    tsc(stage[:, t, :], x[:, t, :], small[:, 4 + t:5 + t], None, MUL)
                dve.nop().then_inc(xn_ready, 1)
                e2 = small[:, 80:82]
                tt(e2, m2, small[:, 82:84], SUB)
                dve.nop().then_inc(fn_asked, 1)
                dve.wait_ge(cum_done, 1)
                rk = rank[:, :, 0:NEXP]
                stt(rk, ps[:, 7, 0:64].rearrange("p (t n) -> p t n", t=TT), 1.0, sel, ADD, MUL)
                tsc(rk, rk, -1.0, None, ADD)
                tsc(rank[:, :, NEXP:], rank[:, :, 0:2], -float(SLOTS), None, ADD)
                io64 = cst[:, C_I64:C_I64 + SLOTS]

                def one_hots(e0):
                    for e in range(2):
                        for t in range(TT):
                            ins = dve.tensor_scalar(onehot[:, t, e * SLOTS:(e + 1) * SLOTS], io64,
                                                    rank[:, t, ds(e0 + e, 1)], None, EQ)
                    return ins

                def weigh(e0):
                    for e in range(2):
                        for t in range(TT):
                            ins = dve.tensor_scalar(weighted[:, t, e * SLOTS:(e + 1) * SLOTS], io64,
                                                    rank[:, t, ds(e0 + e, 1)], gate[:, t, ds(e0 + e, 1)], EQ, MUL)
                    return ins

                one_hots(0).then_inc(onehot_ready, 1)
                top = small[:, 132:133]
                after(dve.tensor_reduce(top, ps[:, 7, 64:96], AX, MAX))
                for n in range(1, MAX_PASSES):
                    tsc(small[:, 133:134], top, float(n * SLOTS), None, ALU.is_gt)
                    tt(passes_f[:, :], passes_f[:, :], small[:, 133:134], ADD)
                tsc(passes_f[:, :], passes_f[:, :], 1.0, None, ADD)
                after(dve.tensor_copy(passes[:, :], passes_f[:, :]))
                for s in (passes_pe, passes_act, passes_sp):
                    dve.nop().then_inc(s, 1)
                p1 = dve.value_load(passes[0:1, 0:1], min_val=0, max_val=MAX_PASSES * DEPTH)
                dve.wait_ge(fn_served, 6)
                psel = small[:, 94:96]
                after(dve.tensor_reduce(psel, shares, AX, ADD))
                after(dve.reciprocal(psel, psel))
                w1s, w2s = small[:, 96:98], small[:, 98:100]
                tsc(w1s, e2, 1.0, None, ADD)
                after(dve.reciprocal(w1s, w1s))
                tt(w1s, w1s, psel, MUL)
                tt(w2s, w1s, e2, MUL)
                gt = gate[:, :, 0:NEXP]
                tt(gt, oh1, w1s.unsqueeze(2).to_broadcast([P, TT, NEXP]), MUL)
                tt(oh2, oh2, w2s.unsqueeze(2).to_broadcast([P, TT, NEXP]), MUL)
                tt(gt, gt, oh2, ADD)
                after(dve.tensor_copy(gate[:, :, NEXP:], gate[:, :, 0:2]))
                after(dve.memset(ye, 0.0))
                after(dve.memset(pgT, 0.0))
                dve.nop().then_inc(blank_pair, 1)
                dve.nop().then_inc(router_over, 1)
                weigh(0).then_inc(weighted_ready, 1)
                with dve.Fori(p0, p1) as p:
                    with dve.Fori(0, PAIRS) as i:
                        g = p * PAIRS + i
                        dve.wait_ge(gather_done, g + (l + 1))
                        one_hots(i * 2 + 2).then_inc(onehot_ready, 1)
                        dve.wait_ge(silu_out, g + 1)
                        used_in_pair(dve, 7, l, g)
                        dve.tensor_tensor(hid, ps[:, 1, :], sil, MUL).then_inc(hid_ready, 1)
                        for n in range(2 * TT):
                            h, t = divmod(n, TT)
                            dve.wait_ge(scat_done, (g + l) * (2 * TT) + n + 1)
                            xh = x[:, t, h * W:(h + 1) * W]
                            dve.tensor_tensor(xh, ps[:, 7 - n % 2, :], xh, ADD).then_inc(scat_read, 1)
                        dve.wait_ge(pgT_done, g + 1)
                        weigh(i * 2 + 2).then_inc(weighted_ready, 1)
                        dve.wait_ge(weighted_ready, g + (l + 2))
                        dve.wait_ge(onehot_ready, g + (l + 2))
                        rn = rank[:, :, ds(i * 2 + 2, 2)]
                        dve.tensor_scalar(rn, rn, -float(SLOTS), None, ADD).then_inc(rank_moved, 1)
                        dve.wait_ge(rank_moved, g + 1)
                for n in range(2 * TT):
                    h, t = divmod(n, TT)
                    dve.wait_ge(scat_done, (p1 * PAIRS + l) * (2 * TT) + n + 1)
                    xh = x[:, t, h * W:(h + 1) * W]
                    dve.tensor_tensor(xh, ps[:, 7 - n % 2, :], xh, ADD).then_inc(scat_read, 1)
                    if t == TT - 1:
                        dve.wait_ge(scat_read, (p1 * PAIRS + l) * (2 * TT) + n + 3)
                        dve.nop().then_inc(layer_out, 1)

            dve.wait_ge(cleared, DEPTH + 1)
            steps[0] = 0
            dve.nop().then_inc(final_in, 1)
            dve.wait_ge(final_out, 2)
            tsc(small[:, 2:4], small[:, 0:2], 1.0 / D, 1e-6, MUL, ADD)
            dve.nop().then_inc(final_in, 1)
            dve.wait_ge(final_out, 3)
            after(dve.reciprocal(small[:, 4:6], small[:, 2:4]))
            dve.wait_ge(final_g_ready, 16)
            for t in range(TT):
                stt(stage[:, t, :], x[:, t, :], small[:, 4 + t:5 + t], final_g, MUL, MUL)
            dve.nop().then_inc(out_ready, 1)


def constants():
    import math

    import numpy as np
    c = np.zeros((P, C_COLS), np.float32)
    r = np.arange(P)
    c[:, C_ID:C_ID + P] = np.eye(P)
    c[:, C_TRI:C_TRI + P] = r[:, None] < r[None, :]
    c[:, C_MASK:C_MASK + P] = np.where(r[None, :] <= r[:, None], 0.0, -1e30 * HD ** 0.5)
    c[:, C_I64:C_I64 + SLOTS] = np.arange(SLOTS)
    c[:, C_I32:C_I32 + NEXP] = np.arange(NEXP)
    c[:, C_I32M:C_I32M + NEXP] = np.arange(NEXP) - 64
    c[:, C_FREQ:C_FREQ + HALF] = np.float32(10000.0) ** (-np.arange(0, HD, 2, dtype=np.float32) / np.float32(HD))
    for n in range(DEPTH):
        init = 0.8 - 0.6 * math.exp(-0.3 * n)
        c[:, C_LINIT + n] = init
        c[:, C_ONEM + n] = 1.0 - init
    return c


def kernel(**inputs):
    import numpy as _np
    import concourse.bacc as _bacc
    from concourse import mybir as _mybir
    from concourse.bass_utils import run_bass_kernel_spmd as _run

    nc = _bacc.Bacc("TRN2", target_bir_lowering=False, num_devices=1)
    arrays, aps = {}, {}
    for name, v in inputs.items():
        v = _np.ascontiguousarray(v)
        if v.ndim == 1:
            v = v.reshape(1, -1)
        arrays["in_" + name] = v
        aps[name] = nc.dram_tensor("in_" + name, v.shape, _mybir.dt.from_np(v.dtype), kind="ExternalInput").ap()
    arrays["consts"] = constants()
    consts = nc.dram_tensor("consts", (P, C_COLS), F32, kind="ExternalInput").ap()
    out = nc.dram_tensor("result", (1, SEQ, D), F32, kind="ExternalOutput").ap()
    hybrid_kernel(nc, aps, consts, out)
    return _run(nc, [arrays], core_ids=[0]).results[0]["result"]
```
